# Optimizing a Trainium2 kernel written in Bass

```python
import math
import jax, jax.numpy as jnp
from jax import lax
import numpy as np

D_MODEL = 1024
BATCH = 1
SEQ = 512
DEPTH = 2

N_MIXERS = 2
DIFF_HEAD_DIM = 64
DIFF_HEADS = D_MODEL // (2 * DIFF_HEAD_DIM)
SB_HEAD_DIM = 64
SB_HEADS = D_MODEL // SB_HEAD_DIM
PROJ_WIDTH = 3 * D_MODEL
ROPE_THETA = 500000.0
ROPE_DIMS = DIFF_HEAD_DIM // 4
Q_BLOCK = 128
N_EXPERTS = 32
N_GROUPS = 4
EXPERTS_PER_GROUP = N_EXPERTS // N_GROUPS
TOP_K = 2
D_EXPERT = D_MODEL // 2
EXPERT_BLOCK = 256
NORM_EPS = 1e-6
N_DIFF_LAYERS = (DEPTH + 1) // 2

kernel_name = "hybrid_diffattn_stickbreak_grouped_moe"

def rms_norm(x, g):
    x32 = x.astype(jnp.float32)
    y = x32 * lax.rsqrt(jnp.mean(x32 * x32, axis=-1, keepdims=True) + NORM_EPS)
    return (y * g.astype(jnp.float32)).astype(x.dtype)

def partial_rope(x, positions):
    half = ROPE_DIMS // 2
    inv_freq = jnp.power(jnp.float32(ROPE_THETA), -jnp.arange(half, dtype=jnp.float32) * (2.0 / ROPE_DIMS))
    ang = positions.astype(jnp.float32)[..., None] * inv_freq
    ang = ang.reshape(ang.shape[:2] + (1,) * (x.ndim - 3) + (half,))
    cos, sin = jnp.cos(ang), jnp.sin(ang)
    xr = x[..., :ROPE_DIMS].astype(jnp.float32)
    x1, x2 = xr[..., :half], xr[..., half:]
    rot = jnp.concatenate([x1 * cos - x2 * sin, x2 * cos + x1 * sin], axis=-1)
    return jnp.concatenate([rot.astype(x.dtype), x[..., ROPE_DIMS:]], axis=-1)

def diff_attention(h, positions, w_in, w_out, lam, subln_g, layer_idx):
    B, S, _ = h.shape
    H, DH = DIFF_HEADS, DIFF_HEAD_DIM
    proj = h @ w_in
    q = proj[..., :D_MODEL].reshape(B, S, H, 2, DH)
    k = proj[..., D_MODEL:2 * D_MODEL].reshape(B, S, H, 2, DH)
    v = proj[..., 2 * D_MODEL:].reshape(B, S, H, 2 * DH).astype(jnp.float32)
    q = partial_rope(q, positions).astype(jnp.float32) * (DH ** -0.5)
    k = partial_rope(k, positions).astype(jnp.float32)
    lam_init = 0.8 - 0.6 * math.exp(-0.3 * layer_idx)
    lam32 = lam.astype(jnp.float32)
    lam_full = jnp.exp(jnp.sum(lam32[0] * lam32[1])) - jnp.exp(jnp.sum(lam32[2] * lam32[3])) + lam_init
    nb = S // Q_BLOCK
    qb = q.reshape(B, nb, Q_BLOCK, H, 2, DH).swapaxes(0, 1)
    key_pos = jnp.arange(S)

    def block(args):
        q_blk, i = args
        t = i * Q_BLOCK + jnp.arange(Q_BLOCK)
        causal = key_pos[None, :] <= t[:, None]
        s = jnp.einsum('bqhcd,bkhcd->bhcqk', q_blk, k)
        p = jax.nn.softmax(jnp.where(causal, s, -jnp.inf), axis=-1)
        a = p[:, :, 0] - lam_full * p[:, :, 1]
        return jnp.einsum('bhqk,bkhe->bqhe', a, v)

    o = lax.map(block, (qb, jnp.arange(nb)))
    o = o.swapaxes(0, 1).reshape(B, S, H, 2 * DH)
    o = rms_norm(o, subln_g) * (1.0 - lam_init)
    return o.reshape(B, S, D_MODEL).astype(h.dtype) @ w_out

def stick_breaking_attention(h, w_in, w_out):
    B, S, _ = h.shape
    H, DH = SB_HEADS, SB_HEAD_DIM
    proj = h @ w_in
    q = proj[..., :D_MODEL].reshape(B, S, H, DH).astype(jnp.float32) * (DH ** -0.5)
    k = proj[..., D_MODEL:2 * D_MODEL].reshape(B, S, H, DH).astype(jnp.float32)
    v = proj[..., 2 * D_MODEL:].reshape(B, S, H, DH).astype(jnp.float32)
    nb = S // Q_BLOCK
    qb = q.reshape(B, nb, Q_BLOCK, H, DH).swapaxes(0, 1)
    key_pos = jnp.arange(S)

    def block(args):
        q_blk, i = args
        t = i * Q_BLOCK + jnp.arange(Q_BLOCK)
        strict = key_pos[None, :] < t[:, None]
        z = jnp.einsum('bqhd,bkhd->bhqk', q_blk, k)
        log_beta = jax.nn.log_sigmoid(z)
        log_rest = jnp.where(strict, log_beta - z, 0.0)
        after = lax.cumsum(log_rest, axis=3, reverse=True) - log_rest
        a = jnp.where(strict, jnp.exp(log_beta + after), 0.0)
        return jnp.einsum('bhqk,bkhd->bqhd', a, v)

    o = lax.map(block, (qb, jnp.arange(nb)))
    o = o.swapaxes(0, 1).reshape(B, S, D_MODEL)
    return o.astype(h.dtype) @ w_out

def grouped_moe(h, w_router, b_router, w_gate, w_up, w_down):
    B, S, D = h.shape
    N = B * S
    E, K, EB = N_EXPERTS, TOP_K, EXPERT_BLOCK
    xf = h.reshape(N, D)
    scores = jax.nn.softmax((xf @ w_router).astype(jnp.float32), axis=-1)
    sel = scores + b_router.astype(jnp.float32)
    sel_g = sel.reshape(N, N_GROUPS, EXPERTS_PER_GROUP)
    group_score = lax.top_k(sel_g, K)[0].sum(-1)
    g_best = jnp.argmax(group_score, axis=-1)
    sel_in = jnp.take_along_axis(sel_g, g_best[:, None, None], axis=1)[:, 0]
    _, local = lax.top_k(sel_in, K)
    expert_idx = (g_best[:, None] * EXPERTS_PER_GROUP + local).astype(jnp.int32)
    gate = jnp.take_along_axis(scores, expert_idx, axis=1)
    gate = gate / jnp.sum(gate, axis=-1, keepdims=True)

    flat_e = expert_idx.reshape(-1)
    flat_w = gate.reshape(-1)
    flat_tok = jnp.arange(N * K, dtype=jnp.int32) // K
    order = jnp.argsort(flat_e)
    sorted_e = flat_e[order]
    counts = jnp.zeros((E,), jnp.int32).at[flat_e].add(1)
    padded = ((counts + EB - 1) // EB) * EB
    offs = jnp.cumsum(counts) - counts
    poffs_end = jnp.cumsum(padded)
    poffs = poffs_end - padded
    dest = poffs[sorted_e] + (jnp.arange(N * K, dtype=jnp.int32) - offs[sorted_e])
    P = N * K + E * EB
    n_blk = P // EB
    row_tok = jnp.full((P,), N, jnp.int32).at[dest].set(flat_tok[order])
    row_w = jnp.zeros((P,), jnp.float32).at[dest].set(flat_w[order])
    x_pad = jnp.concatenate([xf, jnp.zeros((1, D), xf.dtype)], axis=0)
    x_rows = x_pad[row_tok].reshape(n_blk, EB, D)
    blk_e = jnp.minimum(jnp.searchsorted(poffs_end, jnp.arange(n_blk) * EB, side='right'), E - 1)

    def expert_block(args):
        xb, e = args
        hid = jax.nn.silu(xb @ w_gate[e]) * (xb @ w_up[e])
        return hid @ w_down[e]

    y_rows = lax.map(expert_block, (x_rows, blk_e)).reshape(P, D)
    y = jax.ops.segment_sum(y_rows.astype(jnp.float32) * row_w[:, None], row_tok, num_segments=N + 1)[:N]
    return y.reshape(B, S, D).astype(h.dtype)

def setup_inputs(seed: int = 0) -> dict:
    key = jax.random.key(seed)
    ks = jax.random.split(key, 17)
    D, E, F = D_MODEL, N_EXPERTS, D_EXPERT
    nrm = jax.random.normal
    x = nrm(ks[0], (BATCH, SEQ, D), jnp.float32)
    c = nrm(ks[1], (BATCH, D), jnp.float32)
    offsets = jax.random.randint(ks[2], (BATCH, 1), 0, 4096, dtype=jnp.int32)
    positions = offsets + jnp.arange(SEQ, dtype=jnp.int32)[None, :]
    w_ada = nrm(ks[3], (DEPTH, D, 6 * D), jnp.float32) * (0.5 * D ** -0.5)
    b_ada = nrm(ks[4], (DEPTH, 6 * D), jnp.float32) * 0.02
    norm_g = 1.0 + 0.02 * nrm(ks[5], (DEPTH, 2, D), jnp.float32)
    w_in = nrm(ks[6], (DEPTH, D, PROJ_WIDTH), jnp.float32) * D ** -0.5
    w_out = nrm(ks[7], (DEPTH, D, D), jnp.float32) * D ** -0.5
    diff_lambda = nrm(ks[8], (N_DIFF_LAYERS, 4, DIFF_HEAD_DIM), jnp.float32) * 0.1
    diff_subln_g = 1.0 + 0.02 * nrm(ks[9], (N_DIFF_LAYERS, 2 * DIFF_HEAD_DIM), jnp.float32)
    w_router = nrm(ks[10], (D, E), jnp.float32) * D ** -0.5
    b_router = nrm(ks[11], (E,), jnp.float32) * 0.01
    w_gate = nrm(ks[12], (DEPTH, E, D, F), jnp.float32) * D ** -0.5
    w_up = nrm(ks[13], (DEPTH, E, D, F), jnp.float32) * D ** -0.5
    w_down = nrm(ks[14], (DEPTH, E, F, D), jnp.float32) * F ** -0.5
    final_norm_g = 1.0 + 0.02 * nrm(ks[15], (D,), jnp.float32)
    return {"x": x, "c": c, "positions": positions, "w_ada": w_ada, "b_ada": b_ada,
            "norm_g": norm_g, "w_in": w_in, "w_out": w_out, "diff_lambda": diff_lambda,
            "diff_subln_g": diff_subln_g, "w_router": w_router, "b_router": b_router,
            "w_gate": w_gate, "w_up": w_up, "w_down": w_down, "final_norm_g": final_norm_g}

def reference(x, c, positions, w_ada, b_ada, norm_g, w_in, w_out, diff_lambda, diff_subln_g,
              w_router, b_router, w_gate, w_up, w_down, final_norm_g):
    c_act = jax.nn.silu(c)
    for i in range(DEPTH):
        mod = c_act @ w_ada[i] + b_ada[i]
        sh_a, sc_a, g_a, sh_m, sc_m, g_m = jnp.split(mod, 6, axis=-1)
        h = rms_norm(x, norm_g[i, 0]) * (1.0 + sc_a[:, None]) + sh_a[:, None]
        if i % N_MIXERS == 0:
            mix = diff_attention(h, positions, w_in[i], w_out[i], diff_lambda[i // N_MIXERS],
                                 diff_subln_g[i // N_MIXERS], i)
        else:
            mix = stick_breaking_attention(h, w_in[i], w_out[i])
        x = x + g_a[:, None] * mix
        h = rms_norm(x, norm_g[i, 1]) * (1.0 + sc_m[:, None]) + sh_m[:, None]
        x = x + g_m[:, None] * grouped_moe(h, w_router, b_router, w_gate[i], w_up[i], w_down[i])
    return rms_norm(x, final_norm_g)


_drawn_inputs = setup_inputs


def setup_inputs(seed=0):
    import zlib

    import numpy as np

    out = dict(_drawn_inputs(seed))
    spreads = {}
    factors = {'diff_subln_g': 3.024, 'final_norm_g': 2.867}
    for name, (base, spread) in spreads.items():
        noise = np.random.default_rng([zlib.crc32(name.encode()), seed]).standard_normal(out[name].shape)
        drawn = base * np.exp(spread * noise) if base else spread * noise
        out[name] = __import__('jax').numpy.asarray(drawn.astype(out[name].dtype))
    for name, factor in factors.items():
        out[name] = (out[name] * factor).astype(out[name].dtype)
    return out
```

```python
from contextlib import ExitStack

import concourse.bass as bass
from concourse import mybir

ALU = mybir.AluOpType
ACT = mybir.ActivationFunctionType
AX = mybir.AxisListType
F32 = mybir.dt.float32
BF16 = mybir.dt.bfloat16
I32 = mybir.dt.int32
U32 = mybir.dt.uint32

P = 128
D = 1024
S = 512
DEPTH = 2
KC = D // P
TT = S // P
H64 = P // 2
E = 32
NG = 4
EG = E // NG
F = D // 2
FC = F // P
NV = 6
QV = D // 4
EPS = 1e-6
BIG = 1e30
STEPS = KC + 1
NOV = 7
NB = 3
YROWS = 40 * P
WA = 4
SH_A, SC_A, G_A, SH_M, SC_M, G_M = range(NV)

C_ID, C_ONE, C_SEL, C_IOTA, C_FOLD, C_MC, C_MS, C_TRI = 0, 128, 256, 768, 896, 928, 1056, 1184
C_E, C_REV, C_GRV, C_COL = 1312, 1344, 1376, 1380
C_EPS, C_INVF, C_SGN, C_ROT, C_PASS = range(C_COL, C_COL + 5)
C_OVE, C_OVB, C_OVJ, C_128B = 1385, 1481, 1577, 1584
C_N = 1680


class Chain:

    def __init__(self, eng, sem):
        self.eng, self.sem, self.base, self.n = eng, sem, 0, 0

    def link(self, ins):
        self.n += 1
        ins.then_inc(self.sem, 1)
        self.eng.wait_ge(self.sem, self.base + self.n)

    def enter(self, it, per):
        self.before = self.base + self.n
        self.base, self.n, self.per = self.before + it * per, 0, per

    def leave(self, turns):
        assert self.n == self.per, (self.n, self.per)
        self.base, self.n = self.before, turns * self.per


def build_trunk(nc, x_in, c_in, positions, w_ada, b_ada, norm_g, w_in, w_out, diff_lambda, diff_subln_g,
                w_router, b_router, w_gate, w_up, w_down, final_g, consts, out):
    with ExitStack() as ctx:
        def sb(name, shape, dt=F32):
            return ctx.enter_context(nc.sbuf_tensor(name, shape, dt))

        held = []

        def sem(name):
            held.append(nc.alloc_semaphore(name=name))
            return held[-1]

        def clear_semaphores():
            nc.clear_and_free_semaphores(held)
            held.clear()
            nc.all_engine_barrier()

        vec, act_e, pool_e, pe_e = nc.vector, nc.scalar, nc.gpsimd, nc.tensor

        x = sb("x_res", [P, TT, D])
        hT = sb("hT", [P, KC, S])
        cst = sb("cst", [P, C_N])
        cbf = sb("cbf", [P, 5 * P], BF16)
        modrow = sb("modrow", [P, DEPTH * NV, QV])
        modcol = sb("modcol", [P, DEPTH * NV, KC])
        gbc = sb("gbc", [P, D])
        veccol = sb("veccol", [P, 41])
        cact = sb("cact", [P, KC, 32])
        wrt = sb("wrt", [P, KC, E])
        brt = sb("brt", [P, E])
        small = sb("small", [P, 64])
        arena = sb("arena", [P, 2 * 12288])
        region = sb("region", [P, 12288])
        posm = sb("posm", [P, TT, E])
        slots = sb("slots", [P, 2, TT], U32)
        gates = sb("gates", [P, 2, TT])
        counts = sb("counts", [1, E], I32)
        overs = sb("overs", [1, 2, 8], I32)
        ybuf = nc.dram_tensor("ybuf", [YROWS, D], F32).ap()

        ident = cst[:, C_ID:C_ID + P]
        ones = cst[:, C_ONE:C_ONE + P]
        identb, onesb, maskc, masks, trib = (cbf[:, i * P:(i + 1) * P] for i in range(5))
        eps = cst[:, C_EPS:C_EPS + 1]
        neglam = small[:, 0:1]
        subg = small[:, 1:2]
        ss, rstd = small[:, 4:8], small[:, 8:12]
        nmx = small[:, 12:16].rearrange("p (a b) -> p a b", a=2)
        lsum = small[:, 16:20].rearrange("p (a b) -> p a b", a=2)
        lrec = small[:, 20:24].rearrange("p (a b) -> p a b", a=2)

        def modvec(L, v):
            return modcol[:, L * NV + v, :]

        def bank(name, shape, stack):
            return stack.enter_context(nc.psum_tensor(name, shape, F32))

        w_ada_rows = w_ada.rearrange("l (k p) n -> l k p n", p=P)

        def ada_products(pe, banks, wa, s_wa, s_used):
            for n, ps in enumerate(banks):
                for k in range(KC):
                    m = n * KC + k
                    pe.wait_ge(s_wa[m % WA], 16 * (m // WA + 1))
                    for j in range(4):
                        last = pe_e.matmul(ps[32 * j:32 * j + 32, 0:QV], cact[:, k, :],
                                           wa[m % WA][:, j * QV:(j + 1) * QV], start=(k == 0), stop=(k == KC - 1))
                    last.then_inc(s_used, 1)

        with ExitStack() as ph:
            psT = bank("su_psT", [P, 512], ph)
            psA = [bank(f"su_psA{i}", [P, 512], ph) for i in range(2)]
            s_cst, s_vec, s_x, s_bias, s_misc = sem("su_cst"), sem("su_vec"), sem("su_x"), sem("su_bias"), sem("su_misc")
            s_wa = [sem(f"su_wa{i}") for i in range(WA)]
            s_t, s_col, s_cact, s_row, s_use, s_ch, s_ach = (sem("su_" + n) for n in (
                "vecT", "veccol", "cact", "modrow", "waused", "dve", "act"))
            s_lam, s_lexp, s_z = sem("su_lam"), sem("su_lamexp"), sem("su_zero")
            vrows = region[0:41, 0:P]
            lamb = region[:, 128:384]
            lamt = region[:, 384:448]
            wa = [arena[:, 4096 + i * 1024:4096 + (i + 1) * 1024] for i in range(WA)]

            with nc.Block() as block:
                @block.sync
                def _(sp):
                    sp.dma_start(vrows[0:32, :], norm_g.rearrange("l i (k p) -> (l i k) p", p=P)).then_inc(s_vec, 16)
                    sp.dma_start(vrows[32:40, :], c_in.rearrange("a (k p) -> (a k) p", p=P)).then_inc(s_vec, 16)
                    sp.dma_start(vrows[40:41, :], diff_subln_g).then_inc(s_vec, 16)
                    sp.dma_start(cst[:, :], consts).then_inc(s_cst, 16)
                    for m in range(2 * KC):
                        v, k = m // KC, m % KC
                        if m >= WA:
                            sp.wait_ge(s_use, m - WA + 1)
                        sp.dma_start(wa[m % WA], w_ada_rows[0, k, :, v * D:(v + 1) * D]).then_inc(s_wa[m % WA], 16)
                    sp.wait_ge(s_x, 16)
                    sp.wait_ge(s_misc, 48)

                @block.gpsimd
                def _(pool):
                    pool.dma_start(x[:, :, :], x_in[0].rearrange("(t p) d -> p t d", p=P)).then_inc(s_x, 16)
                    for j in range(4):
                        src = b_ada.rearrange("l (v j n) -> j (l v) n", v=NV, j=4)[j]
                        pool.dma_start(modrow[32 * j:32 * j + 32, :, :], src.partition_broadcast(32)).then_inc(s_bias, 16)
                    pool.dma_start(lamb, diff_lambda.rearrange("a b c -> a (b c)")[0].partition_broadcast(P)).then_inc(s_lam, 16)
                    pool.dma_start(wrt[:, :, :], w_router.rearrange("(k p) e -> p k e", p=P)).then_inc(s_misc, 16)
                    pool.dma_start(brt[:, :], b_router.partition_broadcast(P)).then_inc(s_misc, 16)
                    pool.dma_start(region[:, 512:1024].bitcast(I32), positions[0].partition_broadcast(P)).then_inc(s_misc, 16)

                @block.tensor
                def _(pe):
                    pe.wait_ge(s_vec, 48)
                    pe.wait_ge(s_cst, 16)
                    pe_e.transpose(psT[:, 0:41], vrows, cst[0:41, C_ID:C_ID + 41]).then_inc(s_t, 1)
                    pe.wait_ge(s_cact, 1)
                    ada_products(pe, psA, wa, s_wa, s_use)

                @block.scalar
                def _(act):
                    ch = Chain(act, s_ach)
                    act.wait_ge(s_col, 1)
                    act_e.activation(cact[:, :, :], veccol[:, 32:40].unsqueeze(2).to_broadcast([P, KC, 32]),
                                     ACT.Silu).then_inc(s_cact, 1)
                    act.wait_ge(s_cst, 16)
                    for i, col in enumerate((C_ID, C_ONE, C_MC, C_MS, C_TRI)):
                        last = act_e.activation(cbf[:, i * P:(i + 1) * P], cst[:, col:col + P], ACT.Copy)
                    ch.link(last)
                    act.wait_ge(s_lexp, 1)
                    act_e.activation(small[:, 2:4], small[:, 2:4], ACT.Exp).then_inc(s_lexp, 1)

                @block.vector
                def _(dve):
                    ch = Chain(dve, s_ch)
                    dve.wait_ge(s_t, 1)
                    vec.tensor_copy(veccol[:, :], psT[:, 0:41]).then_inc(s_col, 1)
                    dve.wait_ge(s_lam, 16)
                    for i in range(2):
                        ch.link(vec.tensor_tensor(lamt, lamb[:, i * 128:i * 128 + 64],
                                                  lamb[:, i * 128 + 64:i * 128 + 128], ALU.mult))
                        ch.link(vec.tensor_reduce(small[:, 2 + i:3 + i], lamt, AX.X, ALU.add))
                    vec.memset(small[:, 4:64], 0.0).then_inc(s_lexp, 1)
                    dve.wait_ge(s_lexp, 2)
                    ch.link(vec.tensor_tensor(neglam, small[:, 3:4], small[:, 2:3], ALU.subtract))
                    lam_init = 0.8 - 0.6 * 1.0
                    ch.link(vec.tensor_scalar(neglam, neglam, -lam_init, None, ALU.add))
                    dve.wait_ge(s_col, 1)
                    ch.link(vec.tensor_scalar(subg, veccol[:, 40:41], 1.0 - lam_init, None, ALU.mult))
                    dve.wait_ge(s_bias, 64)
                    for v in range(2):
                        dve.wait_ge(s_use, (v + 1) * KC)
                        vec.tensor_tensor(modrow[:, v, :], psA[v][:, 0:QV], modrow[:, v, :], ALU.add).then_inc(s_row, 1)
                    dve.wait_ge(s_row, 2)


        def vectors_to_columns(tag, L, which):
            with ExitStack() as ph:
                ps = bank(tag + "_ps", [P, len(which), 2, P], ph)
                s_p, s_c, s_ch = sem(tag + "_T"), sem(tag + "_done"), sem(tag + "_dve")
                with nc.Block() as block:
                    @block.tensor
                    def _(pe):
                        for n, v in enumerate(which):
                            for i in range(2):
                                last = pe_e.transpose(ps[:, n, i, :], modrow[:, L * NV + v, i * P:(i + 1) * P], ident)
                        last.then_inc(s_p, 1)

                    @block.vector
                    def _(dve):
                        ch = Chain(dve, s_ch)
                        dve.wait_ge(s_p, 1)
                        for n, v in enumerate(which):
                            dst = modvec(L, v).rearrange("p (j i) -> p i j", i=2)
                            ch.link(vec.tensor_copy(dst, ps[:, n, :, 0:P:32]))
                            if v in (SC_A, SC_M):
                                g = veccol[:, (2 * L + (v == SC_M)) * KC:(2 * L + (v == SC_M)) * KC + KC]
                                ch.link(vec.scalar_tensor_tensor(modvec(L, v), modvec(L, v), 1.0, g, ALU.add, ALU.mult))

        def vector_broadcast(tag, L, v):
            with ExitStack() as ph:
                ps = bank(tag + "_ps", [P, 4, QV], ph)
                s_p, s_c = sem(tag + "_mm"), sem(tag + "_done")
                with nc.Block() as block:
                    @block.tensor
                    def _(pe):
                        for j in range(4):
                            sel = cst[:, C_SEL + j * P:C_SEL + (j + 1) * P]
                            last = pe_e.matmul(ps[:, j, :], sel, modrow[:, L * NV + v, :], start=True, stop=True)
                        last.then_inc(s_p, 1)

                    @block.vector
                    def _(dve):
                        dve.wait_ge(s_p, 1)
                        vec.tensor_copy(gbc[:, :].rearrange("p (j n) -> p j n", j=4), ps[:, :, :]).then_inc(s_c, 1)
                        dve.wait_ge(s_c, 1)


        def norm_parts():
            return region[:, 0:6144].bitcast(BF16).rearrange("p (n t d) -> p n t d", n=3, t=TT)

        def norm_transpose(tag, L, sc, sh, parts=None):
            with ExitStack() as ph:
                ps = [bank(f"{tag}_ps{i}", [P, KC, P], ph) for i in range(2)]
                s_ss, s_rs, s_ach, s_dch, s_xn, s_tr, s_ea, s_ed, s_pt = (sem(f"{tag}_{n}") for n in (
                    "sumsq", "rstd", "act", "dve", "xn", "transposed", "evac_act", "evac_dve", "parts"))
                xn = [region[:, 6144 + i * D:6144 + (i + 1) * D] for i in range(2)]
                res = region[:, 6144 + 2 * D:6144 + 3 * D]
                junk = region[:, 6144 + 3 * D:6144 + 4 * D]
                with nc.Block() as block:
                    @block.scalar
                    def _(act):
                        ch = Chain(act, s_ach)
                        for t in range(TT):
                            ch.link(act_e.activation(junk, x[:, t, :], ACT.Square, accum_out=ss[:, t:t + 1]))
                        ch.link(act_e.activation(rstd, ss, ACT.Ln, scale=1.0 / D, bias=eps))
                        act_e.activation(rstd, rstd, ACT.Exp, scale=-0.5).then_inc(s_rs, 1)
                        for t in range(TT):
                            act.wait_ge(s_tr, t + 1)
                            for k in range(KC // 2):
                                last = act_e.activation(hT[:, k, t * P:(t + 1) * P], ps[t % 2][:, k, :], ACT.Identity,
                                                        scale=modvec(L, sc)[:, k:k + 1], bias=modvec(L, sh)[:, k:k + 1])
                            last.then_inc(s_ea, 1)

                    @block.vector
                    def _(dve):
                        ch = Chain(dve, s_dch)
                        dve.wait_ge(s_rs, 1)

                        def normalise(t):
                            if t >= 2:
                                dve.wait_ge(s_tr, t - 1)
                            vec.tensor_scalar(xn[t % 2], x[:, t, :], rstd[:, t:t + 1], None, ALU.mult).then_inc(s_xn, 1)

                        normalise(0)
                        for t in range(TT):
                            if t + 1 < TT:
                                normalise(t + 1)
                            if parts is not None:
                                dve.wait_ge(s_xn, t + 1)
                                hi, mid, lo = (parts[:, n, t, :] for n in range(3))
                                ch.link(vec.tensor_copy(hi, xn[t % 2]))
                                ch.link(vec.tensor_tensor(res, xn[t % 2], hi, ALU.subtract))
                                ch.link(vec.tensor_copy(mid, res))
                                vec.tensor_tensor(lo, res, mid, ALU.subtract).then_inc(s_pt, 1)
                                dve.wait_ge(s_pt, t + 1)
                            dve.wait_ge(s_tr, t + 1)
                            for k in range(KC // 2, KC):
                                last = vec.tensor_scalar(hT[:, k, t * P:(t + 1) * P], ps[t % 2][:, k, :],
                                                         modvec(L, sc)[:, k:k + 1], modvec(L, sh)[:, k:k + 1],
                                                         ALU.mult, ALU.add)
                            last.then_inc(s_ed, 1)

                    @block.tensor
                    def _(pe):
                        for t in range(TT):
                            pe.wait_ge(s_xn, t + 1)
                            if t >= 2:
                                pe.wait_ge(s_ea, t - 1)
                                pe.wait_ge(s_ed, t - 1)
                            for k in range(KC):
                                last = pe_e.transpose(ps[t % 2][:, k, :], xn[t % 2][:, k * P:(k + 1) * P], ident)
                            last.then_inc(s_tr, 1)

        def attention(tag, L, diff):
            A = arena
            win = [A[:, i * 3072:(i + 1) * 3072].rearrange("p (k g n) -> p k g n", k=KC, g=3) for i in range(2)]
            wa = [A[:, 6144 + i * 1024:6144 + (i + 1) * 1024] for i in range(WA)]
            qz = [A[:, 10240 + i * 1024:10240 + (i + 1) * 1024].rearrange("p (h n) -> p h n", h=2) for i in range(2)]
            kT = [A[:, 12288 + i * 512:12288 + (i + 1) * 512] for i in range(2)]
            vn = [A[:, 13312 + i * 512:13312 + (i + 1) * 512].rearrange("p (t n) -> p t n", t=TT) for i in range(2)]
            vT = A[:, 14336:14848]
            aT = [A[:, 14848 + i * 2048:14848 + (i + 1) * 2048].rearrange("p (k q) -> p k q", k=TT) for i in range(2)]
            tA = [A[:, 18944 + i * 1024:18944 + (i + 1) * 1024].rearrange("p (h n) -> p h n", h=2) for i in range(2)]
            tB = [A[:, 20992 + i * 1024:20992 + (i + 1) * 1024].rearrange("p (h n) -> p h n", h=2) for i in range(2)]
            raw = A[:, 23040:23552]
            shf = A[:, 23552:24064]
            cosT, sinT, osb, osq = (A[:, 16896 + i * 512:16896 + (i + 1) * 512] for i in range(4))
            oT = region[:, 0:4096].rearrange("p (k n) -> p k n", k=KC)
            wo = region[:, 4096:12288].rearrange("p (k n) -> p k n", k=KC)
            NH = 1 if diff else 2
            with ExitStack() as ph:
                Z = [bank(f"{tag}_Z{i}", [P, 2, S], ph) for i in range(2)]
                PB = [bank(f"{tag}_P{i}", [P, S], ph) for i in range(2)]
                TR = bank(tag + "_TR", [P, S], ph)
                O = bank(tag + "_O", [P, S], ph)
                names = ("proj q_evac k_evac v_evac q_ready k_ready z_done nm_done p_done a_done t_done tr_evac vt_done "
                         "v_ready pv_done o_evac sp_done d_done used row ss_done rs_done rstd angles tables o_done dve act zero fill wo").split()
                s_ = {n: sem(f"{tag}_{n}") for n in names}
                s_win = [sem(f"{tag}_win{i}") for i in range(2)]
                s_wa = [sem(f"{tag}_wa{i}") for i in range(WA)]
                if not diff:
                    s_["q_ready"], s_["k_ready"] = s_["q_evac"], s_["k_evac"]
                z_free = s_["p_done"] if diff else s_["d_done"]
                ada = {0: [G_A], 1: [SH_M], STEPS - 1: [SC_M, G_M]} if diff else {}

                def steps(body, eng_obj, chains=(), per=()):
                    body(0, 0, 0)
                    body(1, 1, 0)
                    turns = (STEPS - 3) // 2
                    with eng_obj.Fori(0, turns) as i:
                        for c, n in zip(chains, per):
                            c.enter(i, n)
                        body(i * 2 + 2, 0, i + 1)
                        body(i * 2 + 3, 1, i + 1)
                    for c in chains:
                        c.leave(turns)
                    body(STEPS - 1, 0, turns + 1)
                    body(STEPS, 1, turns + 1)

                def rope_angles(dve, ch):
                    two_pi = (6.28125, 0.0019353071795864769)
                    magic = 12582912.0
                    ch.link(vec.tensor_copy(raw, region[:, 512:1024].bitcast(I32)))
                    ch.link(vec.tensor_scalar(raw, raw, cst[:, C_INVF:C_INVF + 1], None, ALU.mult))
                    ch.link(vec.tensor_scalar(shf, raw, 0.15915494309189535, magic, ALU.mult, ALU.add))
                    ch.link(vec.tensor_scalar(shf, shf, -magic, None, ALU.add))
                    for part in two_pi:
                        ch.link(vec.scalar_tensor_tensor(raw, shf, -part, raw, ALU.mult, ALU.add))
                    ch.link(vec.tensor_scalar(cosT, raw, 1.5707963267948966, None, ALU.add))
                    ch.link(vec.tensor_scalar(shf, cosT, 3.141592653589793, -6.283185307179586, ALU.is_gt, ALU.mult))
                    ch.link(vec.tensor_tensor(cosT, cosT, shf, ALU.add))
                    for dst, src in ((cosT, cosT), (sinT, raw)):
                        last = vec.tensor_scalar(dst, src, 3.1415925, -3.1415925, ALU.min, ALU.max)
                    last.then_inc(s_["angles"], 1)

                def doing(s):
                    if not isinstance(s, int):
                        return True, True, True
                    return s < KC, 1 <= s <= KC, s >= 2

                with nc.Block() as block:
                    @block.sync
                    def _(sp):
                        wv = w_in[L].rearrange("(k p) (g c n) -> p k g c n", p=P, g=3, c=KC)

                        def body(s, b, use):
                            if not doing(s)[0]:
                                return
                            if not isinstance(s, int) or s >= 2:
                                sp.wait_ge(s_["proj"], (s - 1) * 3)
                            for g in range(3):
                                src = wv[:, :, g, bass.ds(s, 1), :].rearrange("p k c n -> p k (c n)")
                                sp.dma_start(win[b][:, :, g, :], src).then_inc(s_win[b], 16)
                            if diff:
                                if isinstance(s, int) and s == 0:
                                    sp.wait_ge(s_["zero"], 3)
                                for n in range(YROWS // P // KC):
                                    rows = bass.ds(s * (YROWS // KC) + n * P, P)
                                    sp.dma_start(ybuf[rows, :], gbc[:, :]).then_inc(s_["fill"], 16)

                        steps(body, sp)
                        if diff:
                            sp.wait_ge(s_["fill"], 16 * YROWS // P)
                        sp.dma_start(wo, w_out[L].rearrange("(k p) n -> p k n", p=P)).then_inc(s_["wo"], 16)
                        sp.wait_ge(s_["wo"], 16)

                    @block.gpsimd
                    def _(pool):
                        for i in range(2):
                            pool_e.memset(qz[i][:, :, :], 0.0).then_inc(s_["zero"], 1)
                        if not diff:
                            return
                        pool_e.memset(gbc[:, :], 0.0).then_inc(s_["zero"], 1)
                        pool.sem_inc(s_["o_done"], 1)

                        def tile(vector, m0, k, row, col):
                            m = m0 + k
                            if not isinstance(m, int) or m >= WA:
                                pool.wait_ge(s_["used"], m - (WA - 1))
                            src = w_ada.rearrange("l r n -> (l r) n")[bass.ds(row, P), bass.ds(col, D)]
                            pool.dma_start(wa[k % WA], src).then_inc(s_wa[k % WA], 16)

                        def body(s, b, use):
                            static = isinstance(s, int)
                            vs = ada.get(s, []) if static else [None]
                            for n, v in enumerate(vs):
                                for k in range(KC):
                                    if static:
                                        tile(v, (s + n) * KC, k, k * P, v * D)
                                    else:
                                        tile(v, s * KC, k, D + k * P, (s - 2) * D)

                        steps(body, pool)

                    @block.tensor
                    def _(pe):
                        def project(s, b, use, g):
                            if g == 0:
                                pe.wait_ge(s_win[b], use * 48 + 48)
                                if not isinstance(s, int) or s >= 1:
                                    pe.wait_ge(s_["v_evac"], s)
                            elif g == 1:
                                if not isinstance(s, int) or s >= 1:
                                    pe.wait_ge(s_["k_evac"], s)
                                    if diff:
                                        pe.wait_ge(s_["row"], s)
                            else:
                                pe.wait_ge(s_["q_evac"], s + 1)
                            for k in range(KC):
                                last = pe_e.matmul(PB[g % 2][:, :], win[b][:, k, g, :], hT[:, k, :],
                                                   start=(k == 0), stop=(k == KC - 1))
                            last.then_inc(s_["proj"], 1)

                        def ada_half(s, b, half, extra=0):
                            if half == 0:
                                if isinstance(s, int) and s == STEPS - 1:
                                    pe.wait_ge(s_["row"], s + extra)
                                else:
                                    pe.wait_ge(s_["k_evac"], s + 1)
                            for k in range(4 * half, 4 * half + 4):
                                m = (s + extra) * KC + k
                                pe.wait_ge(s_wa[k % WA], ((s + extra) * 2 + half + 1) * 16)
                                for j in range(4):
                                    last = pe_e.matmul(PB[1][32 * j:32 * j + 32, 0:QV], cact[:, k, :],
                                                       wa[k % WA][:, j * QV:(j + 1) * QV],
                                                       start=(k == 0), stop=(k == KC - 1))
                                last.then_inc(s_["used"], 1)

                        def scores(s, cb, qb):
                            n = (s - 1) * 4 + qb
                            if qb == 0:
                                pe.wait_ge(s_["q_ready"], s)
                                pe.wait_ge(s_["k_ready"], s)
                            if not isinstance(n, int) or n >= 2:
                                pe.wait_ge(z_free, n - 1)
                            N = (qb + 1) * P
                            for h in range(2):
                                pe_e.matmul(Z[qb % 2][:, h, 0:N], qz[cb][:, h, qb * P:N], kT[cb][:, 0:N],
                                            start=True, stop=False)
                                last = pe_e.matmul(Z[qb % 2][:, h, qb * P:N], identb, maskc if diff else masks,
                                                   start=False, stop=True)
                            last.then_inc(s_["z_done"], 1)

                        def transposes(s, qb):
                            n = (s - 1) * 4 + qb
                            pe.wait_ge(s_["a_done"], n + 1)
                            if not isinstance(n, int) or n >= 1:
                                pe.wait_ge(s_["tr_evac"], n * NH)
                            if qb == 0:
                                pe.wait_ge(s_["v_ready"], s)
                                if NH == 2 and (not isinstance(s, int) or s >= 2):
                                    pe.wait_ge(s_["o_evac"], s - 1)
                            for h in range(NH):
                                src = tB[qb % 2] if diff else tA[qb % 2]
                                for kc in range(qb + 1):
                                    last = pe_e.transpose((TR, O)[h][:, kc * P:(kc + 1) * P],
                                                          src[:, h, kc * P:(kc + 1) * P], ident)
                                last.then_inc(s_["t_done"], 1)

                        def values(s, cb):
                            pe.wait_ge(s_["v_ready"], s - 1)
                            pe.wait_ge(s_["tr_evac"], (s - 1) * (4 * NH))
                            if diff:
                                pe.wait_ge(s_["o_done"], s - 1)
                            for kc in range(TT):
                                for h in range(NH):
                                    rows = slice(0, P) if diff else slice(h * H64, (h + 1) * H64)
                                    last = pe_e.matmul(O[rows, kc * P:S], vn[cb][:, kc, rows], aT[h][:, kc, kc * P:S],
                                                       start=(kc == 0), stop=(kc == TT - 1))
                            last.then_inc(s_["pv_done"], 1)

                        def square_sum(s):
                            pe.wait_ge(s_["o_evac"], s - 1)
                            pe_e.matmul(O[:, :], ones, osq, start=True, stop=True).then_inc(s_["ss_done"], 1)

                        def v_transpose(s):
                            pe.wait_ge(s_["v_evac"], s)
                            if not isinstance(s, int) or s >= 2:
                                pe.wait_ge(s_["tr_evac"], (s - 1) * (4 * NH))
                            for t in range(TT):
                                last = pe_e.transpose(TR[:, t * P:(t + 1) * P], vT[:, t * P:(t + 1) * P], ident)
                            last.then_inc(s_["vt_done"], 1)

                        def body(s, b, use):
                            proj, attend, weigh = doing(s)
                            cb = 1 - b
                            if attend:
                                scores(s, cb, 0)
                                scores(s, cb, 1)
                            if weigh:
                                values(s, b)
                            if attend:
                                v_transpose(s)
                            if proj:
                                project(s, b, use, 0)
                            if weigh and diff:
                                square_sum(s)
                            if attend:
                                transposes(s, 0)
                                scores(s, cb, 2)
                                transposes(s, 1)
                                scores(s, cb, 3)
                            if proj:
                                project(s, b, use, 1)
                            elif diff and attend:
                                ada_half(s, b, 0, 0)
                                ada_half(s, b, 1, 0)
                            if attend:
                                transposes(s, 2)
                            if diff and proj:
                                ada_half(s, b, 0)
                                ada_half(s, b, 1)
                            if proj:
                                project(s, b, use, 2)
                            elif diff and attend:
                                ada_half(s, b, 0, 1)
                                ada_half(s, b, 1, 1)
                            if attend:
                                transposes(s, 3)

                        pe.wait_ge(s_["zero"], 2)
                        steps(body, pe)

                    @block.scalar
                    def _(act):
                        ch = Chain(act, s_["act"])

                        def exps(s, qb):
                            n, N, b = (s - 1) * 4 + qb, (qb + 1) * P, qb % 2
                            act.wait_ge(s_["nm_done"], n + 1)
                            if not isinstance(n, int) or n >= 2:
                                act.wait_ge(s_["a_done"], n - 1)
                            for h in range(2):
                                last = act_e.activation(tA[b][:, h, 0:N], Z[b][:, h, 0:N], ACT.Exp,
                                                        bias=nmx[:, b, h:h + 1], accum_out=lsum[:, b, h:h + 1])
                            last.then_inc(s_["p_done"], 1)

                        def softplus_terms(s, qb):
                            n, N, b = (s - 1) * 4 + qb, (qb + 1) * P, qb % 2
                            act.wait_ge(s_["z_done"], n + 1)
                            if not isinstance(n, int) or n >= 2:
                                act.wait_ge(s_["t_done"], (n - 1) * 2)
                            ch.link(act_e.activation(tA[b][:, :, 0:N], Z[b][:, :, 0:N], ACT.Abs))
                            ch.link(act_e.activation(tA[b][:, :, 0:N], tA[b][:, :, 0:N], ACT.Exp, scale=-1.0))
                            act_e.activation(tA[b][:, :, 0:N], tA[b][:, :, 0:N], ACT.Ln, bias=1.0).then_inc(s_["sp_done"], 1)

                        def weights(s, qb):
                            n, N, b = (s - 1) * 4 + qb, (qb + 1) * P, qb % 2
                            act.wait_ge(s_["d_done"], n + 1)
                            act_e.activation(tA[b][:, :, 0:N], tB[b][:, :, 0:N], ACT.Exp).then_inc(s_["a_done"], 1)

                        def q_out(s, b):
                            act.wait_ge(s_["proj"], s * 3 + 1)
                            if diff:
                                if not isinstance(s, int) or s >= 1:
                                    act.wait_ge(s_["k_ready"], s)
                                act_e.activation(raw, PB[0][:, :], ACT.Copy, scale=0.125).then_inc(s_["q_evac"], 1)
                                return
                            if not isinstance(s, int) or s >= 2:
                                act.wait_ge(s_["z_done"], (s - 1) * 4)
                            for h in range(2):
                                rows = slice(h * H64, (h + 1) * H64)
                                last = act_e.activation(qz[b][rows, h, :], PB[0][rows, :], ACT.Copy, scale=0.125)
                            last.then_inc(s_["q_evac"], 1)

                        def k_out(s, b):
                            act.wait_ge(s_["proj"], s * 3 + 2)
                            if diff:
                                act.wait_ge(s_["q_ready"], s + 1)
                                act_e.activation(raw, PB[1][:, :], ACT.Copy).then_inc(s_["k_evac"], 1)
                                return
                            if not isinstance(s, int) or s >= 2:
                                act.wait_ge(s_["z_done"], (s - 1) * 4)
                            act_e.activation(kT[b], PB[1][:, :], ACT.Copy).then_inc(s_["k_evac"], 1)

                        def v_out(s, b):
                            act.wait_ge(s_["proj"], s * 3 + 3)
                            if not isinstance(s, int) or s >= 1:
                                act.wait_ge(s_["vt_done"], s)
                            act_e.activation(vT, PB[0][:, :], ACT.Copy).then_inc(s_["v_evac"], 1)

                        def v_natural(s, b):
                            act.wait_ge(s_["vt_done"], s)
                            if not isinstance(s, int) or s >= 2:
                                act.wait_ge(s_["pv_done"], s - 1)
                            act_e.activation(vn[b][:, :, :], TR[:, :].rearrange("p (t n) -> p t n", t=TT),
                                             ACT.Copy).then_inc(s_["v_ready"], 1)

                        def a_transposed(s, qb):
                            n = (s - 1) * 4 + qb
                            act.wait_ge(s_["t_done"], n + 1)
                            if qb == 0 and (not isinstance(s, int) or s >= 2):
                                act.wait_ge(s_["pv_done"], s - 1)
                            act_e.activation(aT[0][:, 0:qb + 1, qb * P:(qb + 1) * P],
                                             TR[:, 0:(qb + 1) * P].rearrange("p (k q) -> p k q", q=P),
                                             ACT.Copy).then_inc(s_["tr_evac"], 1)

                        def o_out(s):
                            act.wait_ge(s_["pv_done"], s - 1)
                            if diff:
                                act.wait_ge(s_["o_done"], s - 1)
                                act_e.activation(osb, O[:, :], ACT.Copy)
                                act_e.activation(osq, O[:, :], ACT.Square).then_inc(s_["o_evac"], 1)
                                return
                            act_e.activation(oT[:, bass.ds(s - 2, 1), :].rearrange("p c n -> p (c n)"), O[:, :],
                                             ACT.Copy).then_inc(s_["o_evac"], 1)

                        def o_rstd(s):
                            act.wait_ge(s_["ss_done"], s - 1)
                            act_e.activation(tR, O[:, :], ACT.Ln, scale=1.0 / P, bias=eps).then_inc(s_["rs_done"], 1)
                            act.wait_ge(s_["rs_done"], s - 1)
                            act_e.activation(tR, tR, ACT.Exp, scale=-0.5).then_inc(s_["rstd"], 1)

                        tR = A[:, 24064:24576]

                        def body(s, b, use):
                            proj, attend, weigh = doing(s)
                            first = exps if diff else softplus_terms
                            if attend:
                                first(s, 0)
                                first(s, 1)
                            if weigh:
                                o_out(s)
                            if attend:
                                v_natural(s, 1 - b)
                                if not diff:
                                    weights(s, 0)
                                    weights(s, 1)
                            if proj:
                                q_out(s, b)
                            if weigh and diff:
                                o_rstd(s)
                            if attend and diff:
                                a_transposed(s, 0)
                                first(s, 2)
                                a_transposed(s, 1)
                                first(s, 3)
                            if attend and not diff:
                                first(s, 2)
                                first(s, 3)
                                weights(s, 2)
                            if proj:
                                k_out(s, b)
                            if attend:
                                if diff:
                                    a_transposed(s, 2)
                                else:
                                    weights(s, 3)
                            if proj:
                                v_out(s, b)
                            if attend and diff:
                                a_transposed(s, 3)

                        if diff:
                            act.wait_ge(s_["zero"], 2)
                            act.wait_ge(s_["angles"], 1)
                            act_e.activation(sinT, sinT, ACT.Sin)
                            act_e.activation(cosT, cosT, ACT.Sin).then_inc(s_["tables"], 1)
                        act.wait_ge(s_["zero"], 2)
                        steps(body, act, () if diff else (ch,), () if diff else (16,))

                    @block.vector
                    def _(dve):
                        ch = Chain(dve, s_["dve"])

                        def maxes(s, qb):
                            n, N, b = (s - 1) * 4 + qb, (qb + 1) * P, qb % 2
                            dve.wait_ge(s_["z_done"], n + 1)
                            if not isinstance(n, int) or n >= 2:
                                dve.wait_ge(s_["p_done"], n - 1)
                            vec.reduce_max(nmx[:, b, :], Z[b][:, :, 0:N], AX.X, negate=True).then_inc(s_["nm_done"], 1)

                        def combine(s, qb):
                            n, N, b = (s - 1) * 4 + qb, (qb + 1) * P, qb % 2
                            dve.wait_ge(s_["p_done"], n + 1)
                            ch.link(vec.reciprocal(lrec[:, b, :], lsum[:, b, :]))
                            ch.link(vec.tensor_tensor(lrec[:, b, 1:2], lrec[:, b, 1:2], neglam, ALU.mult))
                            if not isinstance(n, int) or n >= 2:
                                dve.wait_ge(s_["t_done"], n - 1)
                            ch.link(vec.tensor_scalar(tB[b][:, 1, 0:N], tA[b][:, 1, 0:N], lrec[:, b, 1:2], None, ALU.mult))
                            vec.scalar_tensor_tensor(tB[b][:, 0, 0:N], tA[b][:, 0, 0:N], lrec[:, b, 0:1],
                                                     tB[b][:, 1, 0:N], ALU.mult, ALU.add).then_inc(s_["a_done"], 1)

                        def rotate(s, b, g):
                            dve.wait_ge(s_["k_evac"] if g else s_["q_evac"], s + 1)
                            mask = [8 + i for i in range(8)] + list(range(8)) + list(range(16, 32))
                            rc = tB[0][:, 1, :]
                            if not isinstance(s, int) or s >= 1:
                                dve.wait_ge(s_["a_done"], (s - 1) * 4 + 2 + 2 * g)
                            if g:
                                dve.wait_ge(s_["q_ready"], s + 1)
                            vec.tensor_tensor(rc, raw, cosT, ALU.mult)
                            ch.link(vec.stream_shuffle(shf, raw, mask))
                            ch.link(vec.tensor_tensor(shf, shf, sinT, ALU.mult))
                            if not isinstance(s, int) or s >= 2:
                                dve.wait_ge(s_["z_done"], (s - 1) * 4)
                            if g:
                                vec.tensor_tensor(kT[b], rc, shf, ALU.add).then_inc(s_["k_ready"], 1)
                                return
                            for h in range(2):
                                rows = slice(h * H64, (h + 1) * H64)
                                last = vec.tensor_tensor(qz[b][rows, h, :], rc[rows, :], shf[rows, :], ALU.add)
                            last.then_inc(s_["q_ready"], 1)

                        def vector_row(s, extra=0):
                            static = isinstance(s, int)
                            m = s + extra
                            dve.wait_ge(s_["used"], (m + 1) * KC)
                            slot = (G_A, SH_M, None, None, None, None, None, None, SC_M, G_M)[m] if static else s - 2 + NV
                            row = modrow[:, bass.ds(slot, 1), :].rearrange("p v n -> p (v n)")
                            vec.tensor_tensor(row, PB[1][:, 0:QV], row, ALU.add).then_inc(s_["row"], 1)

                        def o_norm(s):
                            dve.wait_ge(s_["rstd"], s - 1)
                            dst = oT[:, bass.ds(s - 2, 1), :].rearrange("p c n -> p (c n)")
                            vec.scalar_tensor_tensor(dst, osb, subg, A[:, 24064:24576], ALU.mult,
                                                     ALU.mult).then_inc(s_["o_done"], 1)

                        def suffix(s, qb):
                            n, N, b = (s - 1) * 4 + qb, (qb + 1) * P, qb % 2
                            dve.wait_ge(s_["sp_done"], n + 1)
                            ch.link(vec.scalar_tensor_tensor(tA[b][:, :, 0:N], Z[b][:, :, 0:N], 0.0, tA[b][:, :, 0:N],
                                                             ALU.max, ALU.add))
                            if not isinstance(n, int) or n >= 2:
                                dve.wait_ge(s_["a_done"], n - 1)
                            for h in range(2):
                                src = tA[b][:, h, 0:N][:, ::-1]
                                last = vec.tensor_tensor_scan(tB[b][:, h, 0:N][:, ::-1], src, src, 0.0, ALU.add, ALU.bypass)
                            ch.link(last)
                            vec.tensor_tensor(tB[b][:, :, 0:N], Z[b][:, :, 0:N], tB[b][:, :, 0:N],
                                              ALU.subtract).then_inc(s_["d_done"], 1)

                        def a_transposed(s, qb):
                            n = (s - 1) * 4 + qb
                            if qb == 0 and (not isinstance(s, int) or s >= 2):
                                dve.wait_ge(s_["pv_done"], s - 1)
                            for h in range(2):
                                dve.wait_ge(s_["t_done"], n * 2 + h + 1)
                                vec.tensor_copy(aT[h][:, 0:qb + 1, qb * P:(qb + 1) * P],
                                                (TR, O)[h][:, 0:(qb + 1) * P].rearrange("p (k q) -> p k q", q=P)
                                                ).then_inc(s_["tr_evac"], 1)

                        def body(s, b, use):
                            proj, attend, weigh = doing(s)
                            if diff:
                                if attend:
                                    maxes(s, 0)
                                    maxes(s, 1)
                                    combine(s, 0)
                                    combine(s, 1)
                                if proj:
                                    rotate(s, b, 0)
                                if attend:
                                    maxes(s, 2)
                                if weigh:
                                    o_norm(s)
                                if attend:
                                    combine(s, 2)
                                    maxes(s, 3)
                                    combine(s, 3)
                                if proj:
                                    rotate(s, b, 1)
                                    vector_row(s)
                                elif attend:
                                    vector_row(s)
                                    vector_row(s, 1)
                            elif attend:
                                suffix(s, 0)
                                suffix(s, 1)
                                a_transposed(s, 0)
                                a_transposed(s, 1)
                                suffix(s, 2)
                                suffix(s, 3)
                                a_transposed(s, 2)
                                a_transposed(s, 3)

                        if diff:
                            rope_angles(dve, ch)
                            dve.wait_ge(s_["zero"], 2)
                            dve.wait_ge(s_["tables"], 1)
                            ch.link(vec.tensor_scalar(sinT, sinT, cst[:, C_SGN:C_SGN + 1], None, ALU.mult))
                            ch.link(vec.tensor_scalar(cosT, cosT, cst[:, C_ROT:C_ROT + 1], cst[:, C_PASS:C_PASS + 1],
                                                      ALU.mult, ALU.add))
                        steps(body, dve, (ch,), (32,) if diff else (16,))

        def wslot(b):
            A = arena[:, b * 12288:(b + 1) * 12288]
            return (A[:, 0:8192].rearrange("p (g k f) -> p g k f", g=2, k=KC),
                    A[:, 8192:12288].rearrange("p (c d) -> p c d", c=FC))

        def load_expert(sp, L, e, b, s_gu, s_dn, wait_gu=None, wait_dn=None):
            gu, dn = wslot(b)
            if wait_gu is not None:
                wait_gu()
            for g, w in enumerate((w_gate, w_up)):
                src = w[L][bass.ds(e, 1), :, :].rearrange("e (k p) f -> p (e k) f", p=P)
                sp.dma_start(gu[:, g, :, :], src).then_inc(s_gu[b], 16)
            if wait_dn is not None:
                wait_dn()
            src = w_down[L][bass.ds(e, 1), :, :].rearrange("e (k p) f -> p (e k) f", p=P)
            sp.dma_start(dn[:, :, :], src).then_inc(s_dn[b], 16)

        def out_projection(tag, L, s_gu, s_dn):
            oT = region[:, 0:4096].rearrange("p (k n) -> p k n", k=KC)
            wo = region[:, 4096:12288].rearrange("p (k n) -> p k n", k=KC)
            with ExitStack() as ph:
                ps = [bank(f"{tag}_ps{i}", [P, S], ph) for i in range(4)]
                tmp = [hT[:, i, :] for i in range(2)]
                s_mm, s_g, s_x, = (sem(f"{tag}_{n}") for n in ("mm", "gated", "x"))
                halves = [(t, h) for t in range(TT) for h in range(2)]
                with nc.Block() as block:
                    @block.sync
                    def _(sp):
                        for b in range(2):
                            load_expert(sp, L, b, b, s_gu, s_dn)

                    @block.tensor
                    def _(pe):
                        for n, (t, h) in enumerate(halves):
                            if n >= 4:
                                pe.wait_ge(s_g, n - 3)
                            for k in range(KC):
                                last = pe_e.matmul(ps[n % 4][:, :], oT[:, k, t * P:(t + 1) * P],
                                                   wo[:, k, h * S:(h + 1) * S], start=(k == 0), stop=(k == KC - 1))
                            last.then_inc(s_mm, 1)

                    @block.vector
                    def _(dve):
                        for n, (t, h) in enumerate(halves):
                            dve.wait_ge(s_mm, n + 1)
                            if n >= 2:
                                dve.wait_ge(s_x, n - 1)
                            vec.tensor_tensor(tmp[n % 2], ps[n % 4][:, :], gbc[:, h * S:(h + 1) * S],
                                              ALU.mult).then_inc(s_g, 1)
                            dve.wait_ge(s_g, n + 1)
                            xs = x[:, t, h * S:(h + 1) * S]
                            vec.tensor_tensor(xs, xs, tmp[n % 2], ALU.add).then_inc(s_x, 1)

        def router(tag):
            W = [region[:, 6144 + i * 128:6144 + (i + 1) * 128] for i in range(14)]

            def tile(i):
                return W[i].rearrange("p (t e) -> p t e", t=TT)

            part = region[:, 8192:8704]
            maskb = region[:, 8704:8768].bitcast(BF16).rearrange("p (t e) -> p t e", t=TT)
            m8 = region[:, 8768:8896].rearrange("p (g n) -> p g n", n=EG)
            v16 = [region[:, 8896 + i * 16:8912 + i * 16] for i in range(4)]
            v4 = [region[:, 8960 + i * 4:8964 + i * 4] for i in range(12)]
            ov = [region[0:1, 9216 + i * 768:9216 + i * 768 + NOV * NB * E].rearrange("p (j n) -> p j n", j=NOV)
                  for i in range(2)]
            fl, pre, cf = (region[:, 10752 + i * 96:10752 + i * 96 + 96] for i in range(3))
            ovf = region[0:1, 11100:11116].rearrange("p (a b) -> p a b", a=2)
            with ExitStack() as ph:
                psP, psL, psR, psC = (bank(f"{tag}_ps{i}", [P, S], ph) for i in range(4))
                s_lp, s_part, s_lg, s_exp, s_mx, s_mask, s_pos, s_ch = (sem(f"{tag}_{n}") for n in (
                    "partial", "part_out", "logits", "exp", "max", "mask", "pos", "dve"))
                with nc.Block() as block:
                    @block.tensor
                    def _(pe):
                        for r in range(2):
                            for j in range(4):
                                k = 2 * j + r
                                last = pe_e.matmul(psP[32 * j:32 * j + 32, :], wrt[:, k, :], hT[:, k, :],
                                                   start=(r == 0), stop=(r == 1))
                        last.then_inc(s_lp, 1)
                        pe.wait_ge(s_part, 1)
                        for t in range(TT):
                            last = pe_e.matmul(psL[:, t * E:(t + 1) * E], part[:, t * P:(t + 1) * P],
                                               cst[:, C_FOLD:C_FOLD + E], start=True, stop=True)
                        last.then_inc(s_lg, 1)
                        pe.wait_ge(s_mask, 1)
                        for t in range(TT):
                            for u in range(t + 1):
                                pe_e.matmul(psR[:, t * E:(t + 1) * E], trib if u == t else onesb, maskb[:, u, :],
                                            start=(u == 0), stop=(u == t))
                        for u in range(TT):
                            last = pe_e.matmul(psC[:, 0:E], onesb, maskb[:, u, :], start=(u == 0), stop=(u == TT - 1))
                        last.then_inc(s_pos, 1)

                    @block.scalar
                    def _(act):
                        act.wait_ge(s_lp, 1)
                        act_e.activation(part, psP[:, :], ACT.Copy).then_inc(s_part, 1)
                        act.wait_ge(s_mx, 1)
                        act_e.activation(W[0], W[0], ACT.Exp).then_inc(s_exp, 1)

                    @block.vector
                    def _(dve):
                        ch = Chain(dve, s_ch)

                        def per_tile(v):
                            return v.unsqueeze(2).to_broadcast([P, TT, E])

                        dve.wait_ge(s_lg, 1)
                        ch.link(vec.tensor_copy(tile(1), psL[:, 0:TT * E].rearrange("p (t e) -> p t e", t=TT)))
                        ch.link(vec.reduce_max(v4[0], tile(1), AX.X))
                        vec.tensor_tensor(tile(0), tile(1), per_tile(v4[0]), ALU.subtract).then_inc(s_mx, 1)
                        dve.wait_ge(s_exp, 1)
                        ch.link(vec.tensor_reduce(v4[1], tile(0), AX.X, ALU.add))
                        ch.link(vec.reciprocal(v4[1], v4[1]))
                        ch.link(vec.tensor_tensor(tile(0), tile(0), per_tile(v4[1]), ALU.mult))
                        ch.link(vec.tensor_tensor(tile(1), tile(0), brt[:, :].unsqueeze(1).to_broadcast([P, TT, E]), ALU.add))
                        sel = W[1].rearrange("p (g n) -> p g n", n=EG)
                        for g in range(TT * NG):
                            last = vec.max(m8[:, g, :], sel[:, g, :])
                        ch.link(last)
                        ch.link(vec.tensor_tensor(v16[0], m8[:, :, 0:1].rearrange("p g o -> p (g o)"),
                                                  m8[:, :, 1:2].rearrange("p g o -> p (g o)"), ALU.add))

                        def first_largest(dst, src, rev, n, a, v):
                            def b(c):
                                return c.unsqueeze(2).to_broadcast([P, TT, n])
                            ch.link(vec.reduce_max(v, src, AX.X))
                            ch.link(vec.tensor_tensor(a, src, b(v), ALU.is_equal))
                            ch.link(vec.tensor_tensor(a, a, rev.unsqueeze(1).to_broadcast([P, TT, n]), ALU.mult))
                            ch.link(vec.reduce_max(v, a, AX.X))
                            ch.link(vec.tensor_tensor(dst, a, b(v), ALU.is_equal))

                        g4 = [v.rearrange("p (t g) -> p t g", t=TT) for v in v16]
                        first_largest(g4[1], g4[0], cst[:, C_GRV:C_GRV + NG], NG, g4[2], v4[2])
                        ch.link(vec.tensor_tensor(W[1].rearrange("p (g n) -> p g n", n=EG), sel,
                                                  v16[1].unsqueeze(2).to_broadcast([P, TT * NG, EG]), ALU.mult))
                        ch.link(vec.tensor_scalar(v16[3], v16[1], BIG, -BIG, ALU.mult, ALU.add))
                        ch.link(vec.tensor_tensor(W[1].rearrange("p (g n) -> p g n", n=EG), sel,
                                                  v16[3].unsqueeze(2).to_broadcast([P, TT * NG, EG]), ALU.add))
                        rev = cst[:, C_REV:C_REV + E]
                        first_largest(tile(2), tile(1), rev, E, tile(4), v4[3])
                        ch.link(vec.scalar_tensor_tensor(W[1], W[2], -3 * BIG, W[1], ALU.mult, ALU.add))
                        first_largest(tile(3), tile(1), rev, E, tile(4), v4[4])
                        vec.tensor_tensor(maskb[:, :, :], tile(2), tile(3), ALU.add).then_inc(s_mask, 1)
                        for n in range(2):
                            ch.link(vec.tensor_tensor(tile(4), tile(2 + n), tile(0), ALU.mult))
                            ch.link(vec.tensor_reduce(v4[5 + n], tile(4), AX.X, ALU.add))
                        ch.link(vec.tensor_tensor(v4[7], v4[5], v4[6], ALU.add))
                        ch.link(vec.reciprocal(v4[7], v4[7]))
                        for n in range(2):
                            ch.link(vec.tensor_tensor(gates[:, n, :], v4[5 + n], v4[7], ALU.mult))
                        ch.link(vec.tensor_tensor(W[5], W[2], W[3], ALU.add))
                        ch.link(vec.tensor_scalar(W[5], W[5], -10000.0, 10000.0, ALU.mult, ALU.add))
                        dve.wait_ge(s_pos, 1)
                        ch.link(vec.tensor_copy(W[6], psR[:, 0:TT * E]))
                        ch.link(vec.tensor_tensor(posm[:, :, :], tile(6), tile(5), ALU.add))
                        for b in range(NB):
                            ch.link(vec.tensor_scalar(fl[:, b * E:(b + 1) * E], psC[:, 0:E], float(P * (b + 1)), None,
                                                      ALU.is_gt))
                        ch.link(vec.tensor_tensor_scan(pre, fl, fl, 0.0, ALU.add, ALU.bypass))
                        for b in range(NB):
                            ch.link(vec.tensor_scalar(cf[:, b * E:(b + 1) * E], pre[:, b * E:(b + 1) * E], float(P),
                                                      float((E - 1) * P - (b + 1) * P), ALU.mult, ALU.add))
                        for b in reversed(range(NB)):
                            below = cf[:, (b - 1) * E:b * E] if b else cst[:, C_E:C_E + E]
                            ch.link(vec.tensor_tensor(cf[:, b * E:(b + 1) * E], cf[:, b * E:(b + 1) * E], below, ALU.subtract))
                        ch.link(vec.tensor_tensor(tile(7), tile(6), cst[:, C_E:C_E + E].unsqueeze(1).to_broadcast([P, TT, E]),
                                                  ALU.add))
                        for b in range(NB):
                            ch.link(vec.tensor_scalar(tile(8), tile(6), float(P * (b + 1)), None, ALU.is_ge))
                            ch.link(vec.tensor_tensor(tile(8), tile(8), cf[:, b * E:(b + 1) * E].unsqueeze(1)
                                                      .to_broadcast([P, TT, E]), ALU.mult))
                            ch.link(vec.tensor_tensor(tile(7), tile(7), tile(8), ALU.add))
                        for n in range(2):
                            ch.link(vec.tensor_tensor(tile(4), tile(2 + n), tile(7), ALU.mult))
                            ch.link(vec.tensor_reduce(v4[8 + n], tile(4), AX.X, ALU.add))
                            ch.link(vec.tensor_copy(slots[:, n, :], v4[8 + n]))
                        ch.link(vec.tensor_copy(counts[:, :], psC[0:1, 0:E]))
                        n = NB * E

                        def row(a):
                            return a.unsqueeze(1).to_broadcast([1, NOV, n])
                        ch.link(vec.tensor_tensor(ov[0], row(pre[0:1, :]), cst[0:1, C_OVJ:C_OVJ + NOV].unsqueeze(2)
                                                  .to_broadcast([1, NOV, n]), ALU.is_equal))
                        ch.link(vec.tensor_tensor(ov[0], ov[0], row(fl[0:1, :]), ALU.mult))
                        for i, col in enumerate((C_OVE, C_OVB)):
                            ch.link(vec.tensor_tensor(ov[1], ov[0], row(cst[0:1, col:col + n]), ALU.mult))
                            ch.link(vec.tensor_reduce(ovf[:, i, 0:NOV], ov[1], AX.X, ALU.add))
                        ch.link(vec.tensor_copy(ovf[:, 0, NOV:NOV + 1], pre[0:1, n - 1:n]))
                        ch.link(vec.tensor_copy(ovf[:, 1, NOV:NOV + 1], pre[0:1, n - 1:n]))
                        ch.link(vec.tensor_copy(overs[:, :, :], ovf))

        def experts(tag, L, s_gu, s_dn):
            parts = norm_parts()
            R = region
            xg = [R[:, 6144 + i * 1024:7168 + i * 1024].rearrange("p (k n) -> p k n", k=KC) for i in range(2)]
            ysb = [R[:, 8192 + i * 1024:9216 + i * 1024] for i in range(2)]
            Ssel = [R[:, 10240 + i * 256:10496 + i * 256].bitcast(BF16).rearrange("p (t n) -> p t n", t=TT) for i in range(2)]
            hs, hid, hidT = (R[:, 10752 + i * 512:11264 + i * 512] for i in range(3))
            xt = hT[:, 0:2, :].rearrange("p a b -> p (a b)").rearrange("p (k n) -> p k n", k=KC)
            gs, sh = modvec(L, SC_M), modvec(L, SH_M)
            with ExitStack() as ph:
                GX = bank(tag + "_GX", [P, KC, P], ph)
                G, U, TR = (bank(f"{tag}_{n}", [P, S], ph) for n in ("G", "U", "TR"))
                Y = bank(tag + "_Y", [P, 2, S], ph)
                s_ = {n: sem(f"{tag}_{n}") for n in ("sel gx xa xg gu hs hid tr hidT dn y "
                                                       "osel ogx oxa oxg ogu ohs ohid otr ohidT odn oy ow odone ostored onext dve").split()}
                s_y = [sem(f"{tag}_yw{i}") for i in range(2)]

                def select(dve, e, b, first, name):
                    col = posm[:, :, bass.ds(e, 1)].to_broadcast([P, TT, P])
                    iota = cst[:, C_IOTA:C_IOTA + P].unsqueeze(1).to_broadcast([P, TT, P])
                    return vec.tensor_tensor(Ssel[b][:, :, :], iota, col, ALU.is_equal)

                def gather(b, n):
                    for k in range(KC):
                        for t in range(TT):
                            for q in range(3):
                                last = pe_e.matmul(GX[:, k, 0:n], parts[:, q, t, k * P:(k + 1) * P], Ssel[b][:, t, 0:n],
                                                   start=(t == 0 and q == 0), stop=(t == TT - 1 and q == 2))
                    return last

                def modulate(dve, b, n, s_xa, s_xg, count):
                    def feature(v):
                        return v.unsqueeze(2).to_broadcast([P, KC, n])
                    vec.tensor_tensor(xt[:, :, 0:n], GX[:, :, 0:n], feature(gs), ALU.mult).then_inc(s_xa, 1)
                    dve.wait_ge(s_xa, count)
                    vec.tensor_tensor(xg[b][:, :, 0:n], xt[:, :, 0:n], feature(sh), ALU.add).then_inc(s_xg, 1)

                def gate_up_small(b, xb):
                    gu = wslot(b)[0]
                    for k in range(KC):
                        for h in range(2):
                            last = pe_e.matmul(G[h * H64:(h + 1) * H64, :].rearrange("p (g f) -> p g f", g=2),
                                               xg[xb][:, k, 0:H64], gu[:, :, k, h * (F // 2):(h + 1) * (F // 2)],
                                               start=(k == 0), stop=(k == KC - 1))
                    return last

                def gate_up_full(b, xb):
                    gu = wslot(b)[0]
                    for g, ps in enumerate((G, U)):
                        for k in range(KC):
                            last = pe_e.matmul(ps[:, :], xg[xb][:, k, :], gu[:, g, k, :], start=(k == 0), stop=(k == KC - 1))
                    return last

                def hidden_transposes(n):
                    for c in range(n):
                        last = pe_e.transpose(TR[:, c * P:(c + 1) * P], hid[:, c * P:(c + 1) * P], ident)
                    return last

                def down_small(b):
                    dn = wslot(b)[1]
                    for f in range(FC):
                        lhsT = hidT[:, (f % 2) * P + (f // 2) * H64:(f % 2) * P + (f // 2) * H64 + H64]
                        for h in range(2):
                            last = pe_e.matmul(Y[h * H64:(h + 1) * H64, 0, :], lhsT, dn[:, f, h * S:(h + 1) * S],
                                               start=(f == 0), stop=(f == FC - 1))
                    return last

                def down_full(b):
                    dn = wslot(b)[1]
                    for h in range(2):
                        for f in range(FC):
                            last = pe_e.matmul(Y[:, h, :], hidT[:, f * P:(f + 1) * P], dn[:, f, h * S:(h + 1) * S],
                                               start=(f == 0), stop=(f == FC - 1))
                    return last

                def experts_loop(eng, body, first=None):
                    body(0, 0, 0)
                    body(1, 1, 0)
                    with eng.Fori(0, E // 2 - 1) as i:
                        body(i * 2 + 2, 0, i + 1)
                        body(i * 2 + 3, 1, i + 1)

                def late(e, n=1):
                    return not isinstance(e, int) or e >= n

                def either(eng, c, waits, full, small):
                    with eng.If(c > H64):
                        for s, v in waits:
                            eng.wait_ge(s, v)
                        full()
                    with eng.Else():
                        for s, v in waits:
                            eng.wait_ge(s, v)
                        small()

                def count_of(eng, e):
                    return eng.value_load(counts[0:1, bass.ds(e, 1)], min_val=0, max_val=S)

                def tail(eng, body):
                    n = eng.value_load(overs[0:1, 0, NOV:NOV + 1], min_val=0, max_val=NOV)
                    with eng.Fori(0, NOV) as j:
                        with eng.If(j < n):
                            e = eng.value_load(overs[0:1, 0, bass.ds(j, 1)], min_val=0, max_val=E - 1)
                            k = eng.value_load(overs[0:1, 1, bass.ds(j, 1)], min_val=0, max_val=NB)
                            body(j, e, k)
                        with eng.Else():
                            pass

                with nc.Block() as block:
                    @block.sync
                    def _(sp):
                        def store(e, b, full):
                            for h in range(2):
                                if full:
                                    dst = ybuf[bass.ds(e * P, P), h * S:(h + 1) * S]
                                    src = ysb[b][:, h * S:(h + 1) * S]
                                else:
                                    dst = ybuf[bass.ds(e * P, H64), h * S:(h + 1) * S]
                                    src = ysb[b][h * H64:(h + 1) * H64, 0:S]
                                sp.dma_start(dst, src).then_inc(s_y[b], 16)

                        def body(e, b, use):
                            either(sp, count_of(sp, e), [(s_["y"], e + 1)],
                                   lambda: store(e, b, True), lambda: store(e, b, False))

                        def loads(e, b):
                            load_expert(sp, L, e, b, s_gu, s_dn,
                                        lambda: sp.wait_ge(s_["gu"], e - 1),
                                        lambda: sp.wait_ge(s_["dn"], e - 1))

                        with sp.Fori(0, E // 2 - 1) as i:
                            for b in range(2):
                                loads(i * 2 + 2 + b, b)
                                body(i * 2 + b, b, i)
                        for b in range(2):
                            body(E - 2 + b, b, E // 2 - 1)
                        for b in range(2):
                            sp.wait_ge(s_y[b], 16 * E)

                        def extra(j, e, k):
                            gu, dn = wslot(0)
                            for g, w in enumerate((w_gate, w_up)):
                                sp.dma_start(gu[:, g, :, :], w[L][bass.ds(e, 1), :, :].rearrange("e (k p) f -> p (e k) f", p=P)
                                             ).then_inc(s_["ow"], 16)
                            sp.dma_start(dn[:, :, :], w_down[L][bass.ds(e, 1), :, :].rearrange("e (k p) f -> p (e k) f", p=P)
                                         ).then_inc(s_["ow"], 16)
                            sp.wait_ge(s_["oy"], j + 1)
                            sp.dma_start(ybuf[bass.ds(j * P + E * P, P), :], ysb[0]).then_inc(s_["odone"], 16)
                            sp.wait_ge(s_["odone"], j * 16 + 16)
                            sp.sem_inc(s_["ostored"], 1)

                        tail(sp, extra)

                    @block.tensor
                    def _(pe):
                        def gathering(e, b):
                            either(pe, count_of(pe, e), [(s_["sel"], e + 1)] + [(s_["xa"], e)] * late(e),
                                   lambda: gather(b, P).then_inc(s_["gx"], 1),
                                   lambda: gather(b, H64).then_inc(s_["gx"], 1))

                        def body(e, b, use, last=False):
                            c = count_of(pe, e)
                            either(pe, c, [(s_gu[b], use * 32 + 32), (s_["xg"], e + 1)] + [(s_["hid"], e)] * late(e),
                                   lambda: gate_up_full(b, b).then_inc(s_["gu"], 1),
                                   lambda: gate_up_small(b, b).then_inc(s_["gu"], 1))
                            if not last:
                                gathering(e + 1, 1 - b)
                            either(pe, c, [(s_["hid"], e + 1)] + [(s_["hidT"], e)] * late(e),
                                   lambda: hidden_transposes(FC).then_inc(s_["tr"], 1),
                                   lambda: hidden_transposes(2).then_inc(s_["tr"], 1))
                            either(pe, c, [(s_dn[b], use * 16 + 16), (s_["hidT"], e + 1)] + [(s_["y"], e)] * late(e),
                                   lambda: down_full(b).then_inc(s_["dn"], 1),
                                   lambda: down_small(b).then_inc(s_["dn"], 1))

                        gathering(0, 0)
                        body(0, 0, 0)
                        body(1, 1, 0)
                        with pe.Fori(0, E // 2 - 2) as i:
                            body(i * 2 + 2, 0, i + 1)
                            body(i * 2 + 3, 1, i + 1)
                        body(E - 2, 0, E // 2 - 1)
                        body(E - 1, 1, E // 2 - 1, True)

                        def extra(j, e, k):
                            pe.wait_ge(s_["osel"], j + 1)
                            gather(0, P).then_inc(s_["ogx"], 1)
                            pe.wait_ge(s_["ow"], j * 48 + 48)
                            pe.wait_ge(s_["oxg"], j + 1)
                            gate_up_full(0, 0).then_inc(s_["ogu"], 1)
                            pe.wait_ge(s_["ohid"], j + 1)
                            hidden_transposes(FC).then_inc(s_["otr"], 1)
                            pe.wait_ge(s_["ohidT"], j + 1)
                            down_full(0).then_inc(s_["odn"], 1)

                        tail(pe, extra)

                    @block.scalar
                    def _(act):
                        def body(e, b, use):
                            c = count_of(act, e)
                            either(act, c, [(s_["gu"], e + 1)] + [(s_["hid"], e)] * late(e),
                                   lambda: act_e.activation(hs[:, :], G[:, :], ACT.Silu).then_inc(s_["hs"], 1),
                                   lambda: act_e.activation(hs[:, 0:F // 2], G[:, 0:F // 2], ACT.Silu).then_inc(s_["hs"], 1))
                            either(act, c, [(s_["tr"], e + 1)] + [(s_["dn"], e)] * late(e),
                                   lambda: act_e.activation(hidT[:, :], TR[:, :], ACT.Copy).then_inc(s_["hidT"], 1),
                                   lambda: act_e.activation(hidT[:, 0:2 * P], TR[:, 0:2 * P], ACT.Copy).then_inc(s_["hidT"], 1))
                            both = Y[:, :, :].rearrange("p a b -> p (a b)")
                            either(act, c, [(s_["dn"], e + 1)] + [(s_y[b], use * 32)] * late(e, 2),
                                   lambda: act_e.activation(ysb[b], both, ACT.Copy).then_inc(s_["y"], 1),
                                   lambda: act_e.activation(ysb[b][:, 0:S], Y[:, 0, :], ACT.Copy).then_inc(s_["y"], 1))

                        experts_loop(act, body)

                        def extra(j, e, k):
                            act.wait_ge(s_["ogu"], j + 1)
                            act_e.activation(hs[:, :], G[:, :], ACT.Silu).then_inc(s_["ohs"], 1)
                            act.wait_ge(s_["otr"], j + 1)
                            act_e.activation(hidT[:, :], TR[:, :], ACT.Copy).then_inc(s_["ohidT"], 1)
                            act.wait_ge(s_["odn"], j + 1)
                            for b in range(2):
                                act.wait_ge(s_y[b], 16 * E)
                            act_e.activation(ysb[0], Y[:, :, :].rearrange("p a b -> p (a b)"), ACT.Copy).then_inc(s_["oy"], 1)

                        tail(act, extra)

                    @block.vector
                    def _(dve):
                        def selecting(e, b):
                            if late(e, 2):
                                dve.wait_ge(s_["gx"], e - 1)
                            select(dve, e, b, 0, None).then_inc(s_["sel"], 1)

                        def modulating(e, b):
                            waits = [(s_["gx"], e + 1)] + [(s_["gu"], e - 1)] * late(e, 2) + [(s_["xg"], e)] * late(e)
                            either(dve, count_of(dve, e), waits,
                                   lambda: modulate(dve, b, P, s_["xa"], s_["xg"], e + 1),
                                   lambda: modulate(dve, b, H64, s_["xa"], s_["xg"], e + 1))

                        def body(e, b, use, last=False):
                            c = count_of(dve, e)
                            if not last:
                                selecting(e + 1, 1 - b)
                            either(dve, c, [(s_["hs"], e + 1)] + [(s_["tr"], e)] * late(e),
                                   lambda: vec.tensor_tensor(hid[:, :], U[:, :], hs[:, :], ALU.mult).then_inc(s_["hid"], 1),
                                   lambda: vec.tensor_tensor(hid[:, 0:F // 2], G[:, F // 2:F], hs[:, 0:F // 2],
                                                             ALU.mult).then_inc(s_["hid"], 1))
                            if not last:
                                modulating(e + 1, 1 - b)

                        selecting(0, 0)
                        modulating(0, 0)
                        body(0, 0, 0)
                        body(1, 1, 0)
                        with dve.Fori(0, E // 2 - 2) as i:
                            body(i * 2 + 2, 0, i + 1)
                            body(i * 2 + 3, 1, i + 1)
                        body(E - 2, 0, E // 2 - 1)
                        body(E - 1, 1, E // 2 - 1, True)

                        def extra(j, e, k):
                            dve.wait_ge(s_["gx"], E)
                            off = cst[:, bass.ds(k + C_128B, 1)]
                            vec.tensor_tensor(xt[:, 0:1, 0:TT].rearrange("p a b -> p (a b)"),
                                              posm[:, :, bass.ds(e, 1)].rearrange("p t o -> p (t o)"),
                                              off.to_broadcast([P, TT]), ALU.subtract).then_inc(s_["dve"], 1)
                            dve.wait_ge(s_["dve"], j * 1 + 1)
                            vec.tensor_tensor(Ssel[0][:, :, :], cst[:, C_IOTA:C_IOTA + P].unsqueeze(1).to_broadcast([P, TT, P]),
                                              xt[:, 0, 0:TT].unsqueeze(2).to_broadcast([P, TT, P]),
                                              ALU.is_equal).then_inc(s_["osel"], 1)
                            dve.wait_ge(s_["osel"], j + 1)
                            dve.wait_ge(s_["ogx"], j + 1)
                            modulate(dve, 0, P, s_["oxa"], s_["oxg"], j + 1)
                            dve.wait_ge(s_["ohs"], j + 1)
                            vec.tensor_tensor(hid[:, :], U[:, :], hs[:, :], ALU.mult).then_inc(s_["ohid"], 1)
                            dve.wait_ge(s_["odn"], j + 1)
                            dve.sem_inc(s_["onext"], 1)

                        dve.wait_ge(s_["dn"], E)
                        tail(dve, extra)

        def combine(tag, L):
            yt = [arena[:, i * D:(i + 1) * D] for i in range(8)]
            tmp = [arena[:, (8 + i) * D:(9 + i) * D] for i in range(2)]
            with ExitStack() as ph:
                s_yg = [sem(f"{tag}_y{i}") for i in range(8)]
                s_a, s_b, s_c, s_d = (sem(f"{tag}_{n}") for n in ("first", "sum", "gated", "x"))
                with nc.Block() as block:
                    @block.gpsimd
                    def _(pool):
                        for t in range(TT):
                            for n in range(2):
                                pool_e.indirect_dma_start(
                                    out=yt[2 * t + n], out_offset=None, in_=ybuf[:, :],
                                    in_offset=bass.IndirectOffsetOnAxis(ap=slots[:, n, t:t + 1], axis=0),
                                ).then_inc(s_yg[2 * t + n], 16)

                    @block.scalar
                    def _(act):
                        for t in range(TT):
                            act.wait_ge(s_yg[2 * t], 16)
                            if t >= 2:
                                act.wait_ge(s_d, t - 1)
                            act_e.activation(tmp[t % 2], yt[2 * t], ACT.Copy, scale=gates[:, 0, t:t + 1]).then_inc(s_a, 1)

                    @block.vector
                    def _(dve):
                        for t in range(TT):
                            dve.wait_ge(s_yg[2 * t + 1], 16)
                            dve.wait_ge(s_a, t + 1)
                            vec.scalar_tensor_tensor(tmp[t % 2], yt[2 * t + 1], gates[:, 1, t:t + 1], tmp[t % 2],
                                                     ALU.mult, ALU.add).then_inc(s_b, 1)
                            dve.wait_ge(s_b, t + 1)
                            vec.tensor_tensor(tmp[t % 2], tmp[t % 2], gbc[:, :], ALU.mult).then_inc(s_c, 1)
                            dve.wait_ge(s_c, t + 1)
                            vec.tensor_tensor(x[:, t, :], x[:, t, :], tmp[t % 2], ALU.add).then_inc(s_d, 1)

        vectors_to_columns("v0", 0, [SH_A, SC_A])
        for L in range(DEPTH):
            n = f"l{L}"
            if L > 0:
                vectors_to_columns(n + "va", L, [SH_A, SC_A])
            norm_transpose(n + "n1", L, SC_A, SH_A)
            attention(n + "at", L, L % 2 == 0)
            vector_broadcast(n + "ga", L, G_A)
            s_gu = [sem(f"{n}_wgu{i}") for i in range(2)]
            s_dn = [sem(f"{n}_wdn{i}") for i in range(2)]
            out_projection(n + "op", L, s_gu, s_dn)
            vectors_to_columns(n + "vm", L, [SH_M, SC_M])
            vector_broadcast(n + "gm", L, G_M)
            norm_transpose(n + "n2", L, SC_M, SH_M, norm_parts())
            router(n + "ro")
            experts(n + "ex", L, s_gu, s_dn)
            combine(n + "co", L)
            clear_semaphores()

        with ExitStack() as ph:
            gf = arena[:, 16384:17408]
            junk = arena[:, 17408:18432]
            s_g, s_ss, s_rs, s_n, s_o, s_w = (sem("fin_" + n) for n in ("g", "sumsq", "rstd", "normed", "scaled", "stored"))
            with nc.Block() as block:
                @block.sync
                def _(sp):
                    sp.dma_start(gf, final_g.partition_broadcast(P)).then_inc(s_g, 16)
                    for t in range(TT):
                        sp.wait_ge(s_o, t + 1)
                        sp.dma_start(out[0].rearrange("(t p) d -> t p d", p=P)[t], x[:, t, :]).then_inc(s_w, 16)
                    sp.wait_ge(s_w, 16 * TT)

                @block.scalar
                def _(act):
                    for t in range(TT):
                        act_e.activation(junk, x[:, t, :], ACT.Square, accum_out=ss[:, t:t + 1]).then_inc(s_ss, 1)
                        act.wait_ge(s_ss, t + 1)
                    act_e.activation(rstd, ss, ACT.Ln, scale=1.0 / D, bias=eps).then_inc(s_ss, 1)
                    act.wait_ge(s_ss, TT + 1)
                    act_e.activation(rstd, rstd, ACT.Exp, scale=-0.5).then_inc(s_rs, 1)

                @block.vector
                def _(dve):
                    dve.wait_ge(s_g, 16)
                    dve.wait_ge(s_rs, 1)
                    for t in range(TT):
                        vec.scalar_tensor_tensor(x[:, t, :], x[:, t, :], rstd[:, t:t + 1], gf, ALU.mult,
                                                 ALU.mult).then_inc(s_o, 1)


def constants():
    import numpy as np

    c = np.zeros((P, C_N), np.float32)
    r, n = np.arange(P)[:, None], np.arange(P)[None, :]
    c[:, C_ID:C_ID + P] = r == n
    c[:, C_ONE:C_ONE + P] = 1
    for j in range(4):
        c[32 * j, C_SEL + j * P:C_SEL + (j + 1) * P] = 1
    c[:, C_IOTA:C_IOTA + P] = n
    c[:, C_FOLD:C_FOLD + E] = r % E == np.arange(E)[None, :]
    c[:, C_MC:C_MC + P] = np.where(n > r, -BIG, 0)
    c[:, C_MS:C_MS + P] = np.where(n >= r, -BIG, 0)
    c[:, C_TRI:C_TRI + P] = r < n
    c[:, C_E:C_E + E] = P * np.arange(E)
    c[:, C_REV:C_REV + E] = E - np.arange(E)
    c[:, C_GRV:C_GRV + NG] = NG - np.arange(NG)
    half = 8
    f = np.arange(P) % H64
    c[:, C_EPS] = EPS
    c[:, C_INVF] = np.power(np.float32(500000.0), -(f % half).astype(np.float32) * np.float32(2.0 / (2 * half)))
    c[:, C_SGN] = np.where(f < half, -1, np.where(f < 2 * half, 1, 0))
    c[:, C_ROT] = f < 2 * half
    c[:, C_PASS] = f >= 2 * half
    for b in range(NB):
        c[:, C_OVE + b * E:C_OVE + (b + 1) * E] = np.arange(E)
        c[:, C_OVB + b * E:C_OVB + (b + 1) * E] = b + 1
        c[:, C_128B + b + 1] = P * (b + 1)
    c[:, C_OVJ:C_OVJ + NOV] = np.arange(NOV) + 1
    return c


_INS = ["x", "c", "positions", "w_ada", "b_ada", "norm_g", "w_in", "w_out", "diff_lambda", "diff_subln_g",
        "w_router", "b_router", "w_gate", "w_up", "w_down", "final_norm_g"]


def kernel(**inputs):
    import numpy as np
    import concourse.bacc as bacc
    from concourse.bass_utils import run_bass_kernel_spmd

    nc = bacc.Bacc("TRN2", target_bir_lowering=False, num_devices=1)
    arrays, args = {}, []
    for name in _INS:
        a = np.ascontiguousarray(inputs[name])
        arrays[f"in_{name}"] = a
        args.append(nc.dram_tensor(f"in_{name}", a.shape, mybir.dt.from_np(a.dtype), kind="ExternalInput").ap())
    arrays["in_consts"] = constants()
    args.append(nc.dram_tensor("in_consts", (P, C_N), F32, kind="ExternalInput").ap())
    args.append(nc.dram_tensor("out_0", (1, S, D), F32, kind="ExternalOutput").ap())
    build_trunk(nc, *args)
    r = run_bass_kernel_spmd(nc, [arrays], core_ids=[0])
    return r.results[0]["out_0"]
```

```python
from contextlib import ExitStack

import concourse.bass as bass
from concourse import mybir

ALU = mybir.AluOpType
ACT = mybir.ActivationFunctionType
AX = mybir.AxisListType
F32 = mybir.dt.float32
BF16 = mybir.dt.bfloat16
I32 = mybir.dt.int32
U32 = mybir.dt.uint32

P = 128
D = 1024
S = 512
DEPTH = 2
KC = D // P
TT = S // P
H64 = P // 2
H32 = P // 4
E = 32
NG = 4
EG = E // NG
F = D // 2
FC = F // P
NV = 6
QV = D // 4
EPS = 1e-6
BIG = 1e30
STEPS = KC + 1
NOV = 7
NB = 3
YROWS = 40 * P
WA = 4
SH_A, SC_A, G_A, SH_M, SC_M, G_M = range(NV)

C_ID, C_ONE, C_SEL, C_IOTA, C_FOLD, C_MC, C_MS, C_TRI = 0, 128, 256, 768, 896, 928, 1056, 1184
C_E, C_REV, C_GRV, C_COL = 1312, 1344, 1376, 1380
C_EPS, C_INVF, C_SGN, C_ROT, C_PASS = range(C_COL, C_COL + 5)
C_OVE, C_OVB, C_OVJ, C_128B = 1385, 1481, 1577, 1584
C_N = 1680


class Chain:

    def __init__(self, eng, sem):
        self.eng, self.sem, self.base, self.n = eng, sem, 0, 0

    def link(self, ins):
        self.n += 1
        ins.then_inc(self.sem, 1)
        self.eng.wait_ge(self.sem, self.base + self.n)

    def enter(self, it, per):
        self.before = self.base + self.n
        self.base, self.n, self.per = self.before + it * per, 0, per

    def leave(self, turns):
        assert self.n == self.per, (self.n, self.per)
        self.base, self.n = self.before, turns * self.per


def build_trunk(nc, x_in, c_in, positions, w_ada, b_ada, norm_g, w_in, w_out, diff_lambda, diff_subln_g,
                w_router, b_router, w_gate, w_up, w_down, final_g, consts, out):
    with ExitStack() as ctx:
        def sb(name, shape, dt=F32):
            return ctx.enter_context(nc.sbuf_tensor(name, shape, dt))

        held = []

        def sem(name):
            held.append(nc.alloc_semaphore(name=name))
            return held[-1]

        def clear_semaphores():
            nc.clear_and_free_semaphores(held)
            held.clear()
            nc.all_engine_barrier()

        vec, act_e, pool_e, pe_e = nc.vector, nc.scalar, nc.gpsimd, nc.tensor

        x = sb("x_res", [P, TT, D])
        hT = sb("hT", [P, KC, S])
        cst = sb("cst", [P, C_N])
        cbf = sb("cbf", [P, 5 * P], BF16)
        modrow = sb("modrow", [P, DEPTH * NV, QV])
        modcol = sb("modcol", [P, DEPTH * NV, KC])
        gbc = sb("gbc", [P, D])
        veccol = sb("veccol", [P, 41])
        cact = sb("cact", [P, KC, 32])
        wrt = sb("wrt", [P, KC, E])
        brt = sb("brt", [P, E])
        small = sb("small", [P, 64])
        arena = sb("arena", [P, 2 * 12288])
        region = sb("region", [P, 12288])
        posm = sb("posm", [P, TT, E])
        slots = sb("slots", [P, 2, TT], U32)
        gates = sb("gates", [P, 2, TT])
        counts = sb("counts", [1, E], I32)
        overs = sb("overs", [1, 2, 8], I32)
        xrow = sb("xrow", [P, S])
        ybuf = nc.dram_tensor("ybuf", [YROWS, D], F32).ap()

        ident = cst[:, C_ID:C_ID + P]
        ones = cst[:, C_ONE:C_ONE + P]
        identb, onesb, maskc, masks, trib = (cbf[:, i * P:(i + 1) * P] for i in range(5))
        eps = cst[:, C_EPS:C_EPS + 1]
        neglam = small[:, 0:1]
        subg = small[:, 1:2]
        ss, rstd = small[:, 4:8], small[:, 8:12]
        nmx = small[:, 12:16].rearrange("p (a b) -> p a b", a=2)
        lsum = small[:, 16:20].rearrange("p (a b) -> p a b", a=2)
        lrec = small[:, 20:24].rearrange("p (a b) -> p a b", a=2)

        def modvec(L, v):
            return modcol[:, L * NV + v, :]

        def bank(name, shape, stack):
            return stack.enter_context(nc.psum_tensor(name, shape, F32))

        w_ada_rows = w_ada.rearrange("l (k p) n -> l k p n", p=P)

        def ada_products(pe, banks, wa, s_wa, s_used):
            for n, ps in enumerate(banks):
                for k in range(KC):
                    m = n * KC + k
                    pe.wait_ge(s_wa[m % WA], 16 * (m // WA + 1))
                    for j in range(4):
                        last = pe_e.matmul(ps[32 * j:32 * j + 32, 0:QV], cact[:, k, :],
                                           wa[m % WA][:, j * QV:(j + 1) * QV], start=(k == 0), stop=(k == KC - 1))
                    last.then_inc(s_used, 1)

        with ExitStack() as ph:
            psT = bank("su_psT", [P, 512], ph)
            psA = [bank(f"su_psA{i}", [P, 512], ph) for i in range(2)]
            s_cst, s_vec, s_x, s_bias, s_misc = sem("su_cst"), sem("su_vec"), sem("su_x"), sem("su_bias"), sem("su_misc")
            s_wa = [sem(f"su_wa{i}") for i in range(WA)]
            s_t, s_col, s_cact, s_row, s_use, s_ch, s_ach = (sem("su_" + n) for n in (
                "vecT", "veccol", "cact", "modrow", "waused", "dve", "act"))
            s_lam, s_lexp, s_z = sem("su_lam"), sem("su_lamexp"), sem("su_zero")
            vrows = region[0:41, 0:P]
            lamb = region[:, 128:384]
            lamt = region[:, 384:448]
            wa = [arena[:, 4096 + i * 1024:4096 + (i + 1) * 1024] for i in range(WA)]

            with nc.Block() as block:
                @block.sync
                def _(sp):
                    sp.dma_start(vrows[0:32, :], norm_g.rearrange("l i (k p) -> (l i k) p", p=P)).then_inc(s_vec, 16)
                    sp.dma_start(vrows[32:40, :], c_in.rearrange("a (k p) -> (a k) p", p=P)).then_inc(s_vec, 16)
                    sp.dma_start(vrows[40:41, :], diff_subln_g).then_inc(s_vec, 16)
                    sp.dma_start(cst[:, :], consts).then_inc(s_cst, 16)
                    for m in range(2 * KC):
                        v, k = m // KC, m % KC
                        if m >= WA:
                            sp.wait_ge(s_use, m - WA + 1)
                        sp.dma_start(wa[m % WA], w_ada_rows[0, k, :, v * D:(v + 1) * D]).then_inc(s_wa[m % WA], 16)
                    sp.wait_ge(s_x, 16)
                    sp.wait_ge(s_misc, 48)

                @block.gpsimd
                def _(pool):
                    pool.dma_start(x[:, :, :], x_in[0].rearrange("(t p) d -> p t d", p=P)).then_inc(s_x, 16)
                    for j in range(4):
                        src = b_ada.rearrange("l (v j n) -> j (l v) n", v=NV, j=4)[j]
                        pool.dma_start(modrow[32 * j:32 * j + 32, :, :], src.partition_broadcast(32)).then_inc(s_bias, 16)
                    pool.dma_start(lamb, diff_lambda.rearrange("a b c -> a (b c)")[0].partition_broadcast(P)).then_inc(s_lam, 16)
                    pool.dma_start(wrt[:, :, :], w_router.rearrange("(k p) e -> p k e", p=P)).then_inc(s_misc, 16)
                    pool.dma_start(brt[:, :], b_router.partition_broadcast(P)).then_inc(s_misc, 16)
                    pool.dma_start(region[:, 512:1024].bitcast(I32), positions[0].partition_broadcast(P)).then_inc(s_misc, 16)

                @block.tensor
                def _(pe):
                    pe.wait_ge(s_vec, 48)
                    pe.wait_ge(s_cst, 16)
                    pe_e.transpose(psT[:, 0:41], vrows, cst[0:41, C_ID:C_ID + 41]).then_inc(s_t, 1)
                    pe.wait_ge(s_cact, 1)
                    ada_products(pe, psA, wa, s_wa, s_use)

                @block.scalar
                def _(act):
                    ch = Chain(act, s_ach)
                    act.wait_ge(s_col, 1)
                    act_e.activation(cact[:, :, :], veccol[:, 32:40].unsqueeze(2).to_broadcast([P, KC, 32]),
                                     ACT.Silu).then_inc(s_cact, 1)
                    act.wait_ge(s_cst, 16)
                    for i, col in enumerate((C_ID, C_ONE, C_MC, C_MS, C_TRI)):
                        last = act_e.activation(cbf[:, i * P:(i + 1) * P], cst[:, col:col + P], ACT.Copy)
                    ch.link(last)
                    act.wait_ge(s_lexp, 1)
                    act_e.activation(small[:, 2:4], small[:, 2:4], ACT.Exp).then_inc(s_lexp, 1)

                @block.vector
                def _(dve):
                    ch = Chain(dve, s_ch)
                    dve.wait_ge(s_t, 1)
                    vec.tensor_copy(veccol[:, :], psT[:, 0:41]).then_inc(s_col, 1)
                    dve.wait_ge(s_lam, 16)
                    for i in range(2):
                        ch.link(vec.tensor_tensor(lamt, lamb[:, i * 128:i * 128 + 64],
                                                  lamb[:, i * 128 + 64:i * 128 + 128], ALU.mult))
                        ch.link(vec.tensor_reduce(small[:, 2 + i:3 + i], lamt, AX.X, ALU.add))
                    vec.memset(small[:, 4:64], 0.0).then_inc(s_lexp, 1)
                    dve.wait_ge(s_lexp, 2)
                    ch.link(vec.tensor_tensor(neglam, small[:, 3:4], small[:, 2:3], ALU.subtract))
                    lam_init = 0.8 - 0.6 * 1.0
                    ch.link(vec.tensor_scalar(neglam, neglam, -lam_init, None, ALU.add))
                    dve.wait_ge(s_col, 1)
                    ch.link(vec.tensor_scalar(subg, veccol[:, 40:41], 1.0 - lam_init, None, ALU.mult))
                    dve.wait_ge(s_bias, 64)
                    for v in range(2):
                        dve.wait_ge(s_use, (v + 1) * KC)
                        vec.tensor_tensor(modrow[:, v, :], psA[v][:, 0:QV], modrow[:, v, :], ALU.add).then_inc(s_row, 1)
                    dve.wait_ge(s_row, 2)


        def vectors_to_columns(tag, L, which):
            with ExitStack() as ph:
                ps = bank(tag + "_ps", [P, len(which), 2, P], ph)
                s_p, s_c, s_ch = sem(tag + "_T"), sem(tag + "_done"), sem(tag + "_dve")
                with nc.Block() as block:
                    @block.tensor
                    def _(pe):
                        for n, v in enumerate(which):
                            for i in range(2):
                                last = pe_e.transpose(ps[:, n, i, :], modrow[:, L * NV + v, i * P:(i + 1) * P], ident)
                        last.then_inc(s_p, 1)

                    @block.vector
                    def _(dve):
                        ch = Chain(dve, s_ch)
                        dve.wait_ge(s_p, 1)
                        for n, v in enumerate(which):
                            dst = modvec(L, v).rearrange("p (j i) -> p i j", i=2)
                            ch.link(vec.tensor_copy(dst, ps[:, n, :, 0:P:32]))
                            if v in (SC_A, SC_M):
                                g = veccol[:, (2 * L + (v == SC_M)) * KC:(2 * L + (v == SC_M)) * KC + KC]
                                ch.link(vec.scalar_tensor_tensor(modvec(L, v), modvec(L, v), 1.0, g, ALU.add, ALU.mult))

        def vector_broadcast(tag, L, v):
            with ExitStack() as ph:
                ps = bank(tag + "_ps", [P, 4, QV], ph)
                s_p, s_c = sem(tag + "_mm"), sem(tag + "_done")
                with nc.Block() as block:
                    @block.tensor
                    def _(pe):
                        for j in range(4):
                            sel = cst[:, C_SEL + j * P:C_SEL + (j + 1) * P]
                            last = pe_e.matmul(ps[:, j, :], sel, modrow[:, L * NV + v, :], start=True, stop=True)
                        last.then_inc(s_p, 1)

                    @block.vector
                    def _(dve):
                        dve.wait_ge(s_p, 1)
                        vec.tensor_copy(gbc[:, :].rearrange("p (j n) -> p j n", j=4), ps[:, :, :]).then_inc(s_c, 1)
                        dve.wait_ge(s_c, 1)


        def norm_transpose(tag, L, sc, sh, prefetch=None):
            with ExitStack() as ph:
                ps = [bank(f"{tag}_ps{i}", [P, KC, P], ph) for i in range(2)]
                s_rs, s_ach, s_xn, s_tr, s_ea, s_ed = (sem(f"{tag}_{n}") for n in (
                    "rstd", "act", "xn", "transposed", "evac_act", "evac_dve"))
                xn = [region[:, 8192 + i * D:8192 + (i + 1) * D] for i in range(2)]
                junk = region[:, 8192 + 2 * D:8192 + 3 * D]
                with nc.Block() as block:
                    if prefetch is not None:
                        block.sync(prefetch)

                    @block.scalar
                    def _(act):
                        ch = Chain(act, s_ach)
                        for t in range(TT):
                            ch.link(act_e.activation(junk, x[:, t, :], ACT.Square, accum_out=ss[:, t:t + 1]))
                        ch.link(act_e.activation(rstd, ss, ACT.Ln, scale=1.0 / D, bias=eps))
                        act_e.activation(rstd, rstd, ACT.Exp, scale=-0.5).then_inc(s_rs, 1)
                        for t in range(TT):
                            act.wait_ge(s_tr, t + 1)
                            for k in range(KC // 2):
                                last = act_e.activation(hT[:, k, t * P:(t + 1) * P], ps[t % 2][:, k, :], ACT.Identity,
                                                        scale=modvec(L, sc)[:, k:k + 1], bias=modvec(L, sh)[:, k:k + 1])
                            last.then_inc(s_ea, 1)

                    @block.vector
                    def _(dve):
                        dve.wait_ge(s_rs, 1)

                        def normalise(t):
                            if t >= 2:
                                dve.wait_ge(s_tr, t - 1)
                            vec.tensor_scalar(xn[t % 2], x[:, t, :], rstd[:, t:t + 1], None, ALU.mult).then_inc(s_xn, 1)

                        normalise(0)
                        for t in range(TT):
                            if t + 1 < TT:
                                normalise(t + 1)
                            dve.wait_ge(s_tr, t + 1)
                            for k in range(KC // 2, KC):
                                last = vec.tensor_scalar(hT[:, k, t * P:(t + 1) * P], ps[t % 2][:, k, :],
                                                         modvec(L, sc)[:, k:k + 1], modvec(L, sh)[:, k:k + 1],
                                                         ALU.mult, ALU.add)
                            last.then_inc(s_ed, 1)

                    @block.tensor
                    def _(pe):
                        for t in range(TT):
                            pe.wait_ge(s_xn, t + 1)
                            if t >= 2:
                                pe.wait_ge(s_ea, t - 1)
                                pe.wait_ge(s_ed, t - 1)
                            for k in range(KC):
                                last = pe_e.transpose(ps[t % 2][:, k, :], xn[t % 2][:, k * P:(k + 1) * P], ident)
                            last.then_inc(s_tr, 1)

        def attention(tag, L, diff):
            A = arena
            win = [A[:, i * 3072:(i + 1) * 3072].rearrange("p (k g n) -> p k g n", k=KC, g=3) for i in range(2)]
            wa = [A[:, 6144 + i * 1024:6144 + (i + 1) * 1024] for i in range(WA)]
            qz = [A[:, 10240 + i * 1024:10240 + (i + 1) * 1024].rearrange("p (h n) -> p h n", h=2) for i in range(2)]
            kT = [A[:, 12288 + i * 512:12288 + (i + 1) * 512] for i in range(2)]
            vn = [A[:, 13312 + i * 512:13312 + (i + 1) * 512].rearrange("p (t n) -> p t n", t=TT) for i in range(2)]
            vT = A[:, 14336:14848]
            aT = [A[:, 14848 + i * 2048:14848 + (i + 1) * 2048].rearrange("p (k q) -> p k q", k=TT) for i in range(2)]
            tA = [A[:, 18944 + i * 1024:18944 + (i + 1) * 1024].rearrange("p (h n) -> p h n", h=2) for i in range(2)]
            tB = [A[:, 20992 + i * 1024:20992 + (i + 1) * 1024].rearrange("p (h n) -> p h n", h=2) for i in range(2)]
            raw = A[:, 23040:23552]
            shf = A[:, 23552:24064]
            cosT, sinT, osb, osq = (A[:, 16896 + i * 512:16896 + (i + 1) * 512] for i in range(4))
            oT = region[:, 0:4096].rearrange("p (k n) -> p k n", k=KC)
            wo = region[:, 4096:12288].rearrange("p (k n) -> p k n", k=KC)
            NH = 1 if diff else 2
            with ExitStack() as ph:
                Z = [bank(f"{tag}_Z{i}", [P, 2, S], ph) for i in range(2)]
                PB = [bank(f"{tag}_P{i}", [P, S], ph) for i in range(2)]
                TR = bank(tag + "_TR", [P, S], ph)
                O = bank(tag + "_O", [P, S], ph)
                names = ("proj q_evac k_evac v_evac q_ready k_ready z_done nm_done p_done a_done t_done tr_evac vt_done "
                         "v_ready pv_done o_evac sp_done d_done used row ss_done rs_done rstd angles tables o_done dve act zero fill wo").split()
                s_ = {n: sem(f"{tag}_{n}") for n in names}
                s_win = [sem(f"{tag}_win{i}") for i in range(2)]
                s_wa = [sem(f"{tag}_wa{i}") for i in range(WA)]
                if not diff:
                    s_["q_ready"], s_["k_ready"] = s_["q_evac"], s_["k_evac"]
                z_free = s_["p_done"] if diff else s_["d_done"]
                ada = {0: [G_A], 1: [SH_M], STEPS - 1: [SC_M, G_M]} if diff else {}

                def steps(body, eng_obj, chains=(), per=()):
                    body(0, 0, 0)
                    body(1, 1, 0)
                    turns = (STEPS - 3) // 2
                    with eng_obj.Fori(0, turns) as i:
                        for c, n in zip(chains, per):
                            c.enter(i, n)
                        body(i * 2 + 2, 0, i + 1)
                        body(i * 2 + 3, 1, i + 1)
                    for c in chains:
                        c.leave(turns)
                    body(STEPS - 1, 0, turns + 1)
                    body(STEPS, 1, turns + 1)

                def rope_angles(dve, ch):
                    two_pi = (6.28125, 0.0019353071795864769)
                    magic = 12582912.0
                    ch.link(vec.tensor_copy(raw, region[:, 512:1024].bitcast(I32)))
                    ch.link(vec.tensor_scalar(raw, raw, cst[:, C_INVF:C_INVF + 1], None, ALU.mult))
                    ch.link(vec.tensor_scalar(shf, raw, 0.15915494309189535, magic, ALU.mult, ALU.add))
                    ch.link(vec.tensor_scalar(shf, shf, -magic, None, ALU.add))
                    for part in two_pi:
                        ch.link(vec.scalar_tensor_tensor(raw, shf, -part, raw, ALU.mult, ALU.add))
                    ch.link(vec.tensor_scalar(cosT, raw, 1.5707963267948966, None, ALU.add))
                    ch.link(vec.tensor_scalar(shf, cosT, 3.141592653589793, -6.283185307179586, ALU.is_gt, ALU.mult))
                    ch.link(vec.tensor_tensor(cosT, cosT, shf, ALU.add))
                    for dst, src in ((cosT, cosT), (sinT, raw)):
                        last = vec.tensor_scalar(dst, src, 3.1415925, -3.1415925, ALU.min, ALU.max)
                    last.then_inc(s_["angles"], 1)

                def doing(s):
                    if not isinstance(s, int):
                        return True, True, True
                    return s < KC, 1 <= s <= KC, s >= 2

                with nc.Block() as block:
                    @block.sync
                    def _(sp):
                        wv = w_in[L].rearrange("(k p) (g c n) -> p k g c n", p=P, g=3, c=KC)

                        def body(s, b, use):
                            if not doing(s)[0]:
                                return
                            if not isinstance(s, int) or s >= 2:
                                sp.wait_ge(s_["proj"], (s - 1) * 3)
                            for g in range(3):
                                src = wv[:, :, g, bass.ds(s, 1), :].rearrange("p k c n -> p k (c n)")
                                sp.dma_start(win[b][:, :, g, :], src).then_inc(s_win[b], 16)
                            if diff:
                                if isinstance(s, int) and s == 0:
                                    sp.wait_ge(s_["zero"], 3)
                                for n in range(YROWS // P // KC):
                                    rows = bass.ds(s * (YROWS // KC) + n * P, P)
                                    sp.dma_start(ybuf[rows, :], gbc[:, :]).then_inc(s_["fill"], 16)

                        steps(body, sp)
                        if diff:
                            sp.wait_ge(s_["fill"], 16 * YROWS // P)
                        sp.dma_start(wo, w_out[L].rearrange("(k p) n -> p k n", p=P)).then_inc(s_["wo"], 16)
                        sp.wait_ge(s_["wo"], 16)

                    @block.gpsimd
                    def _(pool):
                        for i in range(2):
                            pool_e.memset(qz[i][:, :, :], 0.0).then_inc(s_["zero"], 1)
                        if not diff:
                            return
                        pool_e.memset(gbc[:, :], 0.0).then_inc(s_["zero"], 1)
                        pool.sem_inc(s_["o_done"], 1)

                        def tile(vector, m0, k, row, col):
                            m = m0 + k
                            if not isinstance(m, int) or m >= WA:
                                pool.wait_ge(s_["used"], m - (WA - 1))
                            src = w_ada.rearrange("l r n -> (l r) n")[bass.ds(row, P), bass.ds(col, D)]
                            pool.dma_start(wa[k % WA], src).then_inc(s_wa[k % WA], 16)

                        def body(s, b, use):
                            static = isinstance(s, int)
                            vs = ada.get(s, []) if static else [None]
                            for n, v in enumerate(vs):
                                for k in range(KC):
                                    if static:
                                        tile(v, (s + n) * KC, k, k * P, v * D)
                                    else:
                                        tile(v, s * KC, k, D + k * P, (s - 2) * D)

                        steps(body, pool)

                    @block.tensor
                    def _(pe):
                        def project(s, b, use, g):
                            if g == 0:
                                pe.wait_ge(s_win[b], use * 48 + 48)
                                if not isinstance(s, int) or s >= 1:
                                    pe.wait_ge(s_["v_evac"], s)
                            elif g == 1:
                                if not isinstance(s, int) or s >= 1:
                                    pe.wait_ge(s_["k_evac"], s)
                                    if diff:
                                        pe.wait_ge(s_["row"], s)
                            else:
                                pe.wait_ge(s_["q_evac"], s + 1)
                            for k in range(KC):
                                last = pe_e.matmul(PB[g % 2][:, :], win[b][:, k, g, :], hT[:, k, :],
                                                   start=(k == 0), stop=(k == KC - 1))
                            last.then_inc(s_["proj"], 1)

                        def ada_half(s, b, half, extra=0):
                            if half == 0:
                                if isinstance(s, int) and s == STEPS - 1:
                                    pe.wait_ge(s_["row"], s + extra)
                                else:
                                    pe.wait_ge(s_["k_evac"], s + 1)
                            for k in range(4 * half, 4 * half + 4):
                                m = (s + extra) * KC + k
                                pe.wait_ge(s_wa[k % WA], ((s + extra) * 2 + half + 1) * 16)
                                for j in range(4):
                                    last = pe_e.matmul(PB[1][32 * j:32 * j + 32, 0:QV], cact[:, k, :],
                                                       wa[k % WA][:, j * QV:(j + 1) * QV],
                                                       start=(k == 0), stop=(k == KC - 1))
                                last.then_inc(s_["used"], 1)

                        def scores(s, cb, qb):
                            n = (s - 1) * 4 + qb
                            if qb == 0:
                                pe.wait_ge(s_["q_ready"], s)
                                pe.wait_ge(s_["k_ready"], s)
                            if not isinstance(n, int) or n >= 2:
                                pe.wait_ge(z_free, n - 1)
                            N = (qb + 1) * P
                            for h in range(2):
                                pe_e.matmul(Z[qb % 2][:, h, 0:N], qz[cb][:, h, qb * P:N], kT[cb][:, 0:N],
                                            start=True, stop=False)
                                last = pe_e.matmul(Z[qb % 2][:, h, qb * P:N], identb, maskc if diff else masks,
                                                   start=False, stop=True)
                            last.then_inc(s_["z_done"], 1)

                        def transposes(s, qb):
                            n = (s - 1) * 4 + qb
                            pe.wait_ge(s_["a_done"], n + 1)
                            if not isinstance(n, int) or n >= 1:
                                pe.wait_ge(s_["tr_evac"], n * NH)
                            if qb == 0:
                                pe.wait_ge(s_["v_ready"], s)
                                if NH == 2 and (not isinstance(s, int) or s >= 2):
                                    pe.wait_ge(s_["o_evac"], s - 1)
                            for h in range(NH):
                                src = tB[qb % 2] if diff else tA[qb % 2]
                                for kc in range(qb + 1):
                                    last = pe_e.transpose((TR, O)[h][:, kc * P:(kc + 1) * P],
                                                          src[:, h, kc * P:(kc + 1) * P], ident)
                                last.then_inc(s_["t_done"], 1)

                        def values(s, cb):
                            pe.wait_ge(s_["v_ready"], s - 1)
                            pe.wait_ge(s_["tr_evac"], (s - 1) * (4 * NH))
                            if diff:
                                pe.wait_ge(s_["o_done"], s - 1)
                            for kc in range(TT):
                                for h in range(NH):
                                    rows = slice(0, P) if diff else slice(h * H64, (h + 1) * H64)
                                    last = pe_e.matmul(O[rows, kc * P:S], vn[cb][:, kc, rows], aT[h][:, kc, kc * P:S],
                                                       start=(kc == 0), stop=(kc == TT - 1))
                            last.then_inc(s_["pv_done"], 1)

                        def square_sum(s):
                            pe.wait_ge(s_["o_evac"], s - 1)
                            pe_e.matmul(O[:, :], ones, osq, start=True, stop=True).then_inc(s_["ss_done"], 1)

                        def v_transpose(s):
                            pe.wait_ge(s_["v_evac"], s)
                            if not isinstance(s, int) or s >= 2:
                                pe.wait_ge(s_["tr_evac"], (s - 1) * (4 * NH))
                            for t in range(TT):
                                last = pe_e.transpose(TR[:, t * P:(t + 1) * P], vT[:, t * P:(t + 1) * P], ident)
                            last.then_inc(s_["vt_done"], 1)

                        def body(s, b, use):
                            proj, attend, weigh = doing(s)
                            cb = 1 - b
                            if attend:
                                scores(s, cb, 0)
                                scores(s, cb, 1)
                            if weigh:
                                values(s, b)
                            if attend:
                                v_transpose(s)
                            if proj:
                                project(s, b, use, 0)
                            if weigh and diff:
                                square_sum(s)
                            if attend:
                                transposes(s, 0)
                                scores(s, cb, 2)
                                transposes(s, 1)
                                scores(s, cb, 3)
                            if proj:
                                project(s, b, use, 1)
                            elif diff and attend:
                                ada_half(s, b, 0, 0)
                                ada_half(s, b, 1, 0)
                            if attend:
                                transposes(s, 2)
                            if diff and proj:
                                ada_half(s, b, 0)
                                ada_half(s, b, 1)
                            if proj:
                                project(s, b, use, 2)
                            elif diff and attend:
                                ada_half(s, b, 0, 1)
                                ada_half(s, b, 1, 1)
                            if attend:
                                transposes(s, 3)

                        pe.wait_ge(s_["zero"], 2)
                        steps(body, pe)

                    @block.scalar
                    def _(act):
                        ch = Chain(act, s_["act"])

                        def exps(s, qb):
                            n, N, b = (s - 1) * 4 + qb, (qb + 1) * P, qb % 2
                            act.wait_ge(s_["nm_done"], n + 1)
                            if not isinstance(n, int) or n >= 2:
                                act.wait_ge(s_["a_done"], n - 1)
                            for h in range(2):
                                last = act_e.activation(tA[b][:, h, 0:N], Z[b][:, h, 0:N], ACT.Exp,
                                                        bias=nmx[:, b, h:h + 1], accum_out=lsum[:, b, h:h + 1])
                            last.then_inc(s_["p_done"], 1)

                        def softplus_terms(s, qb):
                            n, N, b = (s - 1) * 4 + qb, (qb + 1) * P, qb % 2
                            act.wait_ge(s_["z_done"], n + 1)
                            if not isinstance(n, int) or n >= 2:
                                act.wait_ge(s_["t_done"], (n - 1) * 2)
                            ch.link(act_e.activation(tA[b][:, :, 0:N], Z[b][:, :, 0:N], ACT.Abs))
                            ch.link(act_e.activation(tA[b][:, :, 0:N], tA[b][:, :, 0:N], ACT.Exp, scale=-1.0))
                            act_e.activation(tA[b][:, :, 0:N], tA[b][:, :, 0:N], ACT.Ln, bias=1.0).then_inc(s_["sp_done"], 1)

                        def weights(s, qb):
                            n, N, b = (s - 1) * 4 + qb, (qb + 1) * P, qb % 2
                            act.wait_ge(s_["d_done"], n + 1)
                            act_e.activation(tA[b][:, :, 0:N], tB[b][:, :, 0:N], ACT.Exp).then_inc(s_["a_done"], 1)

                        def q_out(s, b):
                            act.wait_ge(s_["proj"], s * 3 + 1)
                            if diff:
                                if not isinstance(s, int) or s >= 1:
                                    act.wait_ge(s_["k_ready"], s)
                                act_e.activation(raw, PB[0][:, :], ACT.Copy, scale=0.125).then_inc(s_["q_evac"], 1)
                                return
                            if not isinstance(s, int) or s >= 2:
                                act.wait_ge(s_["z_done"], (s - 1) * 4)
                            for h in range(2):
                                rows = slice(h * H64, (h + 1) * H64)
                                last = act_e.activation(qz[b][rows, h, :], PB[0][rows, :], ACT.Copy, scale=0.125)
                            last.then_inc(s_["q_evac"], 1)

                        def k_out(s, b):
                            act.wait_ge(s_["proj"], s * 3 + 2)
                            if diff:
                                act.wait_ge(s_["q_ready"], s + 1)
                                act_e.activation(raw, PB[1][:, :], ACT.Copy).then_inc(s_["k_evac"], 1)
                                return
                            if not isinstance(s, int) or s >= 2:
                                act.wait_ge(s_["z_done"], (s - 1) * 4)
                            act_e.activation(kT[b], PB[1][:, :], ACT.Copy).then_inc(s_["k_evac"], 1)

                        def v_out(s, b):
                            act.wait_ge(s_["proj"], s * 3 + 3)
                            if not isinstance(s, int) or s >= 1:
                                act.wait_ge(s_["vt_done"], s)
                            act_e.activation(vT, PB[0][:, :], ACT.Copy).then_inc(s_["v_evac"], 1)

                        def v_natural(s, b):
                            act.wait_ge(s_["vt_done"], s)
                            if not isinstance(s, int) or s >= 2:
                                act.wait_ge(s_["pv_done"], s - 1)
                            act_e.activation(vn[b][:, :, :], TR[:, :].rearrange("p (t n) -> p t n", t=TT),
                                             ACT.Copy).then_inc(s_["v_ready"], 1)

                        def a_transposed(s, qb):
                            n = (s - 1) * 4 + qb
                            act.wait_ge(s_["t_done"], n + 1)
                            if qb == 0 and (not isinstance(s, int) or s >= 2):
                                act.wait_ge(s_["pv_done"], s - 1)
                            act_e.activation(aT[0][:, 0:qb + 1, qb * P:(qb + 1) * P],
                                             TR[:, 0:(qb + 1) * P].rearrange("p (k q) -> p k q", q=P),
                                             ACT.Copy).then_inc(s_["tr_evac"], 1)

                        def o_out(s):
                            act.wait_ge(s_["pv_done"], s - 1)
                            if diff:
                                act.wait_ge(s_["o_done"], s - 1)
                                act_e.activation(osb, O[:, :], ACT.Copy)
                                act_e.activation(osq, O[:, :], ACT.Square).then_inc(s_["o_evac"], 1)
                                return
                            act_e.activation(oT[:, bass.ds(s - 2, 1), :].rearrange("p c n -> p (c n)"), O[:, :],
                                             ACT.Copy).then_inc(s_["o_evac"], 1)

                        def o_rstd(s):
                            act.wait_ge(s_["ss_done"], s - 1)
                            act_e.activation(tR, O[:, :], ACT.Ln, scale=1.0 / P, bias=eps).then_inc(s_["rs_done"], 1)
                            act.wait_ge(s_["rs_done"], s - 1)
                            act_e.activation(tR, tR, ACT.Exp, scale=-0.5).then_inc(s_["rstd"], 1)

                        tR = A[:, 24064:24576]

                        def body(s, b, use):
                            proj, attend, weigh = doing(s)
                            first = exps if diff else softplus_terms
                            if attend:
                                first(s, 0)
                                first(s, 1)
                            if weigh:
                                o_out(s)
                            if attend:
                                v_natural(s, 1 - b)
                                if not diff:
                                    weights(s, 0)
                                    weights(s, 1)
                            if proj:
                                q_out(s, b)
                            if weigh and diff:
                                o_rstd(s)
                            if attend and diff:
                                a_transposed(s, 0)
                                first(s, 2)
                                a_transposed(s, 1)
                                first(s, 3)
                            if attend and not diff:
                                first(s, 2)
                                first(s, 3)
                                weights(s, 2)
                            if proj:
                                k_out(s, b)
                            if attend:
                                if diff:
                                    a_transposed(s, 2)
                                else:
                                    weights(s, 3)
                            if proj:
                                v_out(s, b)
                            if attend and diff:
                                a_transposed(s, 3)

                        if diff:
                            act.wait_ge(s_["zero"], 2)
                            act.wait_ge(s_["angles"], 1)
                            act_e.activation(sinT, sinT, ACT.Sin)
                            act_e.activation(cosT, cosT, ACT.Sin).then_inc(s_["tables"], 1)
                        act.wait_ge(s_["zero"], 2)
                        steps(body, act, () if diff else (ch,), () if diff else (16,))

                    @block.vector
                    def _(dve):
                        ch = Chain(dve, s_["dve"])

                        def maxes(s, qb):
                            n, N, b = (s - 1) * 4 + qb, (qb + 1) * P, qb % 2
                            dve.wait_ge(s_["z_done"], n + 1)
                            if not isinstance(n, int) or n >= 2:
                                dve.wait_ge(s_["p_done"], n - 1)
                            vec.reduce_max(nmx[:, b, :], Z[b][:, :, 0:N], AX.X, negate=True).then_inc(s_["nm_done"], 1)

                        def combine(s, qb):
                            n, N, b = (s - 1) * 4 + qb, (qb + 1) * P, qb % 2
                            dve.wait_ge(s_["p_done"], n + 1)
                            ch.link(vec.reciprocal(lrec[:, b, :], lsum[:, b, :]))
                            ch.link(vec.tensor_tensor(lrec[:, b, 1:2], lrec[:, b, 1:2], neglam, ALU.mult))
                            if not isinstance(n, int) or n >= 2:
                                dve.wait_ge(s_["t_done"], n - 1)
                            ch.link(vec.tensor_scalar(tB[b][:, 1, 0:N], tA[b][:, 1, 0:N], lrec[:, b, 1:2], None, ALU.mult))
                            vec.scalar_tensor_tensor(tB[b][:, 0, 0:N], tA[b][:, 0, 0:N], lrec[:, b, 0:1],
                                                     tB[b][:, 1, 0:N], ALU.mult, ALU.add).then_inc(s_["a_done"], 1)

                        def rotate(s, b, g):
                            dve.wait_ge(s_["k_evac"] if g else s_["q_evac"], s + 1)
                            mask = [8 + i for i in range(8)] + list(range(8)) + list(range(16, 32))
                            rc = tB[0][:, 1, :]
                            if not isinstance(s, int) or s >= 1:
                                dve.wait_ge(s_["a_done"], (s - 1) * 4 + 2 + 2 * g)
                            if g:
                                dve.wait_ge(s_["q_ready"], s + 1)
                            vec.tensor_tensor(rc, raw, cosT, ALU.mult)
                            ch.link(vec.stream_shuffle(shf, raw, mask))
                            ch.link(vec.tensor_tensor(shf, shf, sinT, ALU.mult))
                            if not isinstance(s, int) or s >= 2:
                                dve.wait_ge(s_["z_done"], (s - 1) * 4)
                            if g:
                                vec.tensor_tensor(kT[b], rc, shf, ALU.add).then_inc(s_["k_ready"], 1)
                                return
                            for h in range(2):
                                rows = slice(h * H64, (h + 1) * H64)
                                last = vec.tensor_tensor(qz[b][rows, h, :], rc[rows, :], shf[rows, :], ALU.add)
                            last.then_inc(s_["q_ready"], 1)

                        def vector_row(s, extra=0):
                            static = isinstance(s, int)
                            m = s + extra
                            dve.wait_ge(s_["used"], (m + 1) * KC)
                            slot = (G_A, SH_M, None, None, None, None, None, None, SC_M, G_M)[m] if static else s - 2 + NV
                            row = modrow[:, bass.ds(slot, 1), :].rearrange("p v n -> p (v n)")
                            vec.tensor_tensor(row, PB[1][:, 0:QV], row, ALU.add).then_inc(s_["row"], 1)

                        def o_norm(s):
                            dve.wait_ge(s_["rstd"], s - 1)
                            dst = oT[:, bass.ds(s - 2, 1), :].rearrange("p c n -> p (c n)")
                            vec.scalar_tensor_tensor(dst, osb, subg, A[:, 24064:24576], ALU.mult,
                                                     ALU.mult).then_inc(s_["o_done"], 1)

                        def suffix(s, qb):
                            n, N, b = (s - 1) * 4 + qb, (qb + 1) * P, qb % 2
                            dve.wait_ge(s_["sp_done"], n + 1)
                            ch.link(vec.scalar_tensor_tensor(tA[b][:, :, 0:N], Z[b][:, :, 0:N], 0.0, tA[b][:, :, 0:N],
                                                             ALU.max, ALU.add))
                            if not isinstance(n, int) or n >= 2:
                                dve.wait_ge(s_["a_done"], n - 1)
                            for h in range(2):
                                src = tA[b][:, h, 0:N][:, ::-1]
                                last = vec.tensor_tensor_scan(tB[b][:, h, 0:N][:, ::-1], src, src, 0.0, ALU.add, ALU.bypass)
                            ch.link(last)
                            vec.tensor_tensor(tB[b][:, :, 0:N], Z[b][:, :, 0:N], tB[b][:, :, 0:N],
                                              ALU.subtract).then_inc(s_["d_done"], 1)

                        def a_transposed(s, qb):
                            n = (s - 1) * 4 + qb
                            if qb == 0 and (not isinstance(s, int) or s >= 2):
                                dve.wait_ge(s_["pv_done"], s - 1)
                            for h in range(2):
                                dve.wait_ge(s_["t_done"], n * 2 + h + 1)
                                vec.tensor_copy(aT[h][:, 0:qb + 1, qb * P:(qb + 1) * P],
                                                (TR, O)[h][:, 0:(qb + 1) * P].rearrange("p (k q) -> p k q", q=P)
                                                ).then_inc(s_["tr_evac"], 1)

                        def body(s, b, use):
                            proj, attend, weigh = doing(s)
                            if diff:
                                if attend:
                                    maxes(s, 0)
                                    maxes(s, 1)
                                    combine(s, 0)
                                    combine(s, 1)
                                if proj:
                                    rotate(s, b, 0)
                                if attend:
                                    maxes(s, 2)
                                if weigh:
                                    o_norm(s)
                                if attend:
                                    combine(s, 2)
                                    maxes(s, 3)
                                    combine(s, 3)
                                if proj:
                                    rotate(s, b, 1)
                                    vector_row(s)
                                elif attend:
                                    vector_row(s)
                                    vector_row(s, 1)
                            elif attend:
                                suffix(s, 0)
                                suffix(s, 1)
                                a_transposed(s, 0)
                                a_transposed(s, 1)
                                suffix(s, 2)
                                suffix(s, 3)
                                a_transposed(s, 2)
                                a_transposed(s, 3)

                        if diff:
                            rope_angles(dve, ch)
                            dve.wait_ge(s_["zero"], 2)
                            dve.wait_ge(s_["tables"], 1)
                            ch.link(vec.tensor_scalar(sinT, sinT, cst[:, C_SGN:C_SGN + 1], None, ALU.mult))
                            ch.link(vec.tensor_scalar(cosT, cosT, cst[:, C_ROT:C_ROT + 1], cst[:, C_PASS:C_PASS + 1],
                                                      ALU.mult, ALU.add))
                        steps(body, dve, (ch,), (32,) if diff else (16,))

        def gate_up_slot(g):
            mem = region if g == 2 else arena[:, g * 12288:(g + 1) * 12288]
            return mem[:, 0:8192].rearrange("p (g k f) -> p g k f", g=2, k=KC)

        def down_slot(b):
            return arena[:, b * 12288 + 8192:(b + 1) * 12288].rearrange("p (c d) -> p c d", c=FC)

        def load_gate_up(sp, L, e, g, s_landed):
            for n, w in enumerate((w_gate, w_up)):
                src = w[L][bass.ds(e, 1), :, :].rearrange("e (k p) f -> p (e k) f", p=P)
                sp.dma_start(gate_up_slot(g)[:, n, :, :], src).then_inc(s_landed, 16)

        def load_down(sp, L, e, b, s_landed):
            src = w_down[L][bass.ds(e, 1), :, :].rearrange("e (k p) f -> p (e k) f", p=P)
            sp.dma_start(down_slot(b)[:, :, :], src).then_inc(s_landed, 16)

        def out_projection(tag, L, s_gu, s_dn):
            oT = region[:, 0:4096].rearrange("p (k n) -> p k n", k=KC)
            wo = region[:, 4096:12288].rearrange("p (k n) -> p k n", k=KC)
            with ExitStack() as ph:
                ps = [bank(f"{tag}_ps{i}", [P, S], ph) for i in range(4)]
                tmp = [hT[:, i, :] for i in range(2)]
                s_mm, s_g, s_x, = (sem(f"{tag}_{n}") for n in ("mm", "gated", "x"))
                halves = [(t, h) for t in range(TT) for h in range(2)]
                with nc.Block() as block:
                    @block.sync
                    def _(sp):
                        for b in range(2):
                            load_gate_up(sp, L, b, b, s_gu[b])
                            load_down(sp, L, b, b, s_dn[b])

                    @block.tensor
                    def _(pe):
                        for n, (t, h) in enumerate(halves):
                            if n >= 4:
                                pe.wait_ge(s_g, n - 3)
                            for k in range(KC):
                                last = pe_e.matmul(ps[n % 4][:, :], oT[:, k, t * P:(t + 1) * P],
                                                   wo[:, k, h * S:(h + 1) * S], start=(k == 0), stop=(k == KC - 1))
                            last.then_inc(s_mm, 1)

                    @block.vector
                    def _(dve):
                        for n, (t, h) in enumerate(halves):
                            dve.wait_ge(s_mm, n + 1)
                            if n >= 2:
                                dve.wait_ge(s_x, n - 1)
                            vec.tensor_tensor(tmp[n % 2], ps[n % 4][:, :], gbc[:, h * S:(h + 1) * S],
                                              ALU.mult).then_inc(s_g, 1)
                            dve.wait_ge(s_g, n + 1)
                            xs = x[:, t, h * S:(h + 1) * S]
                            vec.tensor_tensor(xs, xs, tmp[n % 2], ALU.add).then_inc(s_x, 1)

        late = region[:, 10752:12288]
        LW = {w: late[:, i * 128:(i + 1) * 128] for i, w in enumerate(("scores", "first", "second", "rank", "tmp", "row", "add"))}
        LT = {w: v.rearrange("p (t e) -> p t e", t=TT) for w, v in LW.items()}
        late_v4 = [late[:, 896 + i * 4:900 + i * 4] for i in range(5)]
        fl, pre, cf = (late[:, 928 + i * 96:1024 + i * 96] for i in range(3))
        cnt = late[:, 1216:1248]
        ovf = late[0:1, 1248:1264].rearrange("p (a b) -> p a b", a=2)

        def gate_weights(ch):
            for n, choice in enumerate(("first", "second")):
                ch.link(vec.tensor_tensor(LT["tmp"], LT[choice], LT["scores"], ALU.mult))
                ch.link(vec.tensor_reduce(late_v4[n], LT["tmp"], AX.X, ALU.add))
            ch.link(vec.tensor_tensor(late_v4[2], late_v4[0], late_v4[1], ALU.add))
            ch.link(vec.reciprocal(late_v4[2], late_v4[2]))
            for n in range(2):
                ch.link(vec.tensor_tensor(gates[:, n, :], late_v4[n], late_v4[2], ALU.mult))
            for b in range(NB):
                ch.link(vec.tensor_scalar(fl[:, b * E:(b + 1) * E], cnt, float(P * (b + 1)), None, ALU.is_gt))
            ch.link(vec.tensor_tensor_scan(pre, fl, fl, 0.0, ALU.add, ALU.bypass))

        def buffer_rows(ch):
            for b in range(NB):
                ch.link(vec.tensor_scalar(cf[:, b * E:(b + 1) * E], pre[:, b * E:(b + 1) * E], float(P),
                                          float((E - 1) * P - (b + 1) * P), ALU.mult, ALU.add))
            for b in reversed(range(NB)):
                below = cf[:, (b - 1) * E:b * E] if b else cst[:, C_E:C_E + E]
                ch.link(vec.tensor_tensor(cf[:, b * E:(b + 1) * E], cf[:, b * E:(b + 1) * E], below, ALU.subtract))
            ch.link(vec.tensor_tensor(LT["row"], LT["rank"], cst[:, C_E:C_E + E].unsqueeze(1).to_broadcast([P, TT, E]),
                                      ALU.add))
            for b in range(NB):
                ch.link(vec.tensor_scalar(LT["add"], LT["rank"], float(P * (b + 1)), None, ALU.is_ge))
                ch.link(vec.tensor_tensor(LT["add"], LT["add"], cf[:, b * E:(b + 1) * E].unsqueeze(1)
                                          .to_broadcast([P, TT, E]), ALU.mult))
                ch.link(vec.tensor_tensor(LT["row"], LT["row"], LT["add"], ALU.add))
            for n, choice in enumerate(("first", "second")):
                ch.link(vec.tensor_tensor(LT["tmp"], LT[choice], LT["row"], ALU.mult))
                ch.link(vec.tensor_reduce(late_v4[3 + n], LT["tmp"], AX.X, ALU.add))
                ch.link(vec.tensor_copy(slots[:, n, :], late_v4[3 + n]))

        def later_blocks(ch, L):
            n = NB * E
            ov = [m[0:1, 0:NOV * n].rearrange("p (j n) -> p j n", j=NOV)
                  for m in (modrow[:, L * NV:L * NV + G_M, :].rearrange("p v n -> p (v n)"), late)]

            def row(a):
                return a.unsqueeze(1).to_broadcast([1, NOV, n])
            ch.link(vec.tensor_tensor(ov[0], row(pre[0:1, :]), cst[0:1, C_OVJ:C_OVJ + NOV].unsqueeze(2)
                                      .to_broadcast([1, NOV, n]), ALU.is_equal))
            ch.link(vec.tensor_tensor(ov[0], ov[0], row(fl[0:1, :]), ALU.mult))
            for i, col in enumerate((C_OVE, C_OVB)):
                ch.link(vec.tensor_tensor(ov[1], ov[0], row(cst[0:1, col:col + n]), ALU.mult))
                ch.link(vec.tensor_reduce(ovf[:, i, 0:NOV], ov[1], AX.X, ALU.add))
                ch.link(vec.tensor_copy(ovf[:, i, NOV:NOV + 1], pre[0:1, n - 1:n]))
            ch.link(vec.tensor_copy(overs[:, :, :], ovf))

        def router(tag):
            R = region[:, 8192:10752]
            W = [LW["scores"], R[:, 0:128], LW["first"], LW["second"], LW["tmp"], R[:, 128:256], LW["rank"]]

            def tile(i):
                return W[i].rearrange("p (t e) -> p t e", t=TT)

            part = R[:, 256:768]
            maskb = R[:, 768:832].bitcast(BF16).rearrange("p (t e) -> p t e", t=TT)
            m8 = R[:, 832:960].rearrange("p (g n) -> p g n", n=EG)
            v16 = [R[:, 960 + i * 16:976 + i * 16] for i in range(4)]
            v4 = [R[:, 1024 + i * 4:1028 + i * 4] for i in range(5)]
            with ExitStack() as ph:
                psP, psL, psR, psC = (bank(f"{tag}_ps{i}", [P, S], ph) for i in range(4))
                s_lp, s_part, s_lg, s_exp, s_mx, s_mask, s_pos, s_ch = (sem(f"{tag}_{n}") for n in (
                    "partial", "part_out", "logits", "exp", "max", "mask", "pos", "dve"))
                with nc.Block() as block:
                    @block.tensor
                    def _(pe):
                        for r in range(2):
                            for j in range(4):
                                k = 2 * j + r
                                last = pe_e.matmul(psP[32 * j:32 * j + 32, :], wrt[:, k, :], hT[:, k, :],
                                                   start=(r == 0), stop=(r == 1))
                        last.then_inc(s_lp, 1)
                        pe.wait_ge(s_part, 1)
                        for t in range(TT):
                            last = pe_e.matmul(psL[:, t * E:(t + 1) * E], part[:, t * P:(t + 1) * P],
                                               cst[:, C_FOLD:C_FOLD + E], start=True, stop=True)
                        last.then_inc(s_lg, 1)
                        pe.wait_ge(s_mask, 1)
                        for t in range(TT):
                            for u in range(t + 1):
                                pe_e.matmul(psR[:, t * E:(t + 1) * E], trib if u == t else onesb, maskb[:, u, :],
                                            start=(u == 0), stop=(u == t))
                        for u in range(TT):
                            last = pe_e.matmul(psC[:, 0:E], onesb, maskb[:, u, :], start=(u == 0), stop=(u == TT - 1))
                        last.then_inc(s_pos, 1)

                    @block.scalar
                    def _(act):
                        act.wait_ge(s_lp, 1)
                        act_e.activation(part, psP[:, :], ACT.Copy).then_inc(s_part, 1)
                        act.wait_ge(s_mx, 1)
                        act_e.activation(W[0], W[0], ACT.Exp).then_inc(s_exp, 1)

                    @block.vector
                    def _(dve):
                        ch = Chain(dve, s_ch)

                        def per_tile(v):
                            return v.unsqueeze(2).to_broadcast([P, TT, E])

                        dve.wait_ge(s_lg, 1)
                        ch.link(vec.tensor_copy(tile(1), psL[:, 0:TT * E].rearrange("p (t e) -> p t e", t=TT)))
                        ch.link(vec.reduce_max(v4[0], tile(1), AX.X))
                        vec.tensor_tensor(tile(0), tile(1), per_tile(v4[0]), ALU.subtract).then_inc(s_mx, 1)
                        dve.wait_ge(s_exp, 1)
                        ch.link(vec.tensor_reduce(v4[1], tile(0), AX.X, ALU.add))
                        ch.link(vec.reciprocal(v4[1], v4[1]))
                        ch.link(vec.tensor_tensor(tile(0), tile(0), per_tile(v4[1]), ALU.mult))
                        ch.link(vec.tensor_tensor(tile(1), tile(0), brt[:, :].unsqueeze(1).to_broadcast([P, TT, E]), ALU.add))
                        sel = W[1].rearrange("p (g n) -> p g n", n=EG)
                        for g in range(TT * NG):
                            last = vec.max(m8[:, g, :], sel[:, g, :])
                        ch.link(last)
                        ch.link(vec.tensor_tensor(v16[0], m8[:, :, 0:1].rearrange("p g o -> p (g o)"),
                                                  m8[:, :, 1:2].rearrange("p g o -> p (g o)"), ALU.add))

                        def first_largest(dst, src, rev, n, a, v):
                            def b(c):
                                return c.unsqueeze(2).to_broadcast([P, TT, n])
                            ch.link(vec.reduce_max(v, src, AX.X))
                            ch.link(vec.tensor_tensor(a, src, b(v), ALU.is_equal))
                            ch.link(vec.tensor_tensor(a, a, rev.unsqueeze(1).to_broadcast([P, TT, n]), ALU.mult))
                            ch.link(vec.reduce_max(v, a, AX.X))
                            ch.link(vec.tensor_tensor(dst, a, b(v), ALU.is_equal))

                        g4 = [v.rearrange("p (t g) -> p t g", t=TT) for v in v16]
                        first_largest(g4[1], g4[0], cst[:, C_GRV:C_GRV + NG], NG, g4[2], v4[2])
                        ch.link(vec.tensor_tensor(W[1].rearrange("p (g n) -> p g n", n=EG), sel,
                                                  v16[1].unsqueeze(2).to_broadcast([P, TT * NG, EG]), ALU.mult))
                        ch.link(vec.tensor_scalar(v16[3], v16[1], BIG, -BIG, ALU.mult, ALU.add))
                        ch.link(vec.tensor_tensor(W[1].rearrange("p (g n) -> p g n", n=EG), sel,
                                                  v16[3].unsqueeze(2).to_broadcast([P, TT * NG, EG]), ALU.add))
                        rev = cst[:, C_REV:C_REV + E]
                        first_largest(tile(2), tile(1), rev, E, tile(4), v4[3])
                        ch.link(vec.scalar_tensor_tensor(W[1], W[2], -3 * BIG, W[1], ALU.mult, ALU.add))
                        first_largest(tile(3), tile(1), rev, E, tile(4), v4[4])
                        vec.tensor_tensor(maskb[:, :, :], tile(2), tile(3), ALU.add).then_inc(s_mask, 1)
                        ch.link(vec.tensor_tensor(W[5], W[2], W[3], ALU.add))
                        ch.link(vec.tensor_scalar(W[5], W[5], -10000.0, 10000.0, ALU.mult, ALU.add))
                        dve.wait_ge(s_pos, 1)
                        ch.link(vec.tensor_copy(W[6], psR[:, 0:TT * E]))
                        ch.link(vec.tensor_tensor(posm[:, :, :], tile(6), tile(5), ALU.add))
                        ch.link(vec.tensor_copy(counts[:, :], psC[0:1, 0:E]))
                        ch.link(vec.tensor_copy(cnt, psC[:, 0:E]))

        def experts(tag, L, s_gu, s_dn):
            R, T = region[:, 8192:10752], hT[:, :, :].rearrange("p a b -> p (a b)")
            xg = [T[:, i * 1024:(i + 1) * 1024].rearrange("p (k n) -> p k n", k=KC) for i in range(2)]
            ysb = [T[:, 2048 + i * 1024:3072 + i * 1024] for i in range(2)]
            Ssel = [R[:, i * 512:(i + 1) * 512].rearrange("p (t n) -> p t n", t=TT) for i in range(2)]
            hs, hid, hidT = (R[:, 1024 + i * 512:1536 + i * 512] for i in range(3))
            gs, sh = modvec(L, SC_M), modvec(L, SH_M)
            shifted = small[:, 24:28]
            with ExitStack() as ph:
                GX = bank(tag + "_GX", [P, KC, P], ph)
                G, U, TR = (bank(f"{tag}_{n}", [P, S], ph) for n in ("G", "U", "TR"))
                Y = bank(tag + "_Y", [P, 2, S], ph)
                XR = bank(tag + "_XR", [P, S], ph)
                s_ = {n: sem(f"{tag}_{n}") for n in ("sel rows xr gx xg gu hs hid tr hidT dn y overs late "
                                                       "osel ogx oxg ogu ohs ohid otr ohidT odn oy ow odone ostored onext dve").split()}
                s_y = [sem(f"{tag}_yw{i}") for i in range(2)]

                def select(b, ranks):
                    for t in range(TT):
                        last = vec.tensor_scalar(Ssel[b][:, t, :], cst[:, C_IOTA:C_IOTA + P], ranks(t), rstd[:, t:t + 1],
                                                 ALU.is_equal, ALU.mult)
                    return last

                def gather(b):
                    for k in range(KC):
                        for t in range(TT):
                            last = pe_e.matmul(GX[:, k, :], x[:, t, k * P:(k + 1) * P], Ssel[b][:, t, :],
                                               start=(t == 0), stop=(t == TT - 1))
                    return last

                def gather_rows(b, n):
                    w = D * n // P
                    for t in range(TT):
                        for j in range(P // n):
                            last = pe_e.matmul(XR[j * n:(j + 1) * n, 0:w], Ssel[b][:, t, 0:n], x[:, t, j * w:(j + 1) * w],
                                               start=(t == 0), stop=(t == TT - 1))
                    return last

                def row_transposes(n):
                    for c in range(n * KC // P):
                        last = pe_e.transpose(GX[:, c, :], xrow[:, c * P:(c + 1) * P], ident)
                    return last

                def modulate(b, n):
                    per = n * KC // P
                    for k in range(KC):
                        src = GX[:, k % per, k // per * n:(k // per + 1) * n]
                        last = vec.tensor_scalar(xg[b][:, k, 0:n], src, gs[:, k:k + 1], sh[:, k:k + 1],
                                                 ALU.mult, ALU.add)
                    return last

                def gate_up_small(g, xb):
                    gu = gate_up_slot(g)
                    for k in range(KC):
                        for h in range(2):
                            last = pe_e.matmul(G[h * H64:(h + 1) * H64, :].rearrange("p (g f) -> p g f", g=2),
                                               xg[xb][:, k, 0:H64], gu[:, :, k, h * (F // 2):(h + 1) * (F // 2)],
                                               start=(k == 0), stop=(k == KC - 1))
                    return last

                def gate_up_tiny(g, xb):
                    gu = gate_up_slot(g)
                    for k in range(KC):
                        for j in range(4):
                            last = pe_e.matmul(G[j * H32:(j + 1) * H32, 0:F // 2].rearrange("p (g f) -> p g f", g=2),
                                               xg[xb][:, k, 0:H32], gu[:, :, k, j * P:(j + 1) * P],
                                               start=(k == 0), stop=(k == KC - 1))
                    return last

                def gate_up_full(g, xb):
                    gu = gate_up_slot(g)
                    for w, ps in enumerate((G, U)):
                        for k in range(KC):
                            last = pe_e.matmul(ps[:, :], xg[xb][:, k, :], gu[:, w, k, :], start=(k == 0), stop=(k == KC - 1))
                    return last

                def hidden_transposes(n):
                    for c in range(n):
                        last = pe_e.transpose(TR[:, c * P:(c + 1) * P], hid[:, c * P:(c + 1) * P], ident)
                    return last

                def down_small(b):
                    dn = down_slot(b)
                    for f in range(FC):
                        lhsT = hidT[:, (f % 2) * P + (f // 2) * H64:(f % 2) * P + (f // 2) * H64 + H64]
                        for h in range(2):
                            last = pe_e.matmul(Y[h * H64:(h + 1) * H64, 0, :], lhsT, dn[:, f, h * S:(h + 1) * S],
                                               start=(f == 0), stop=(f == FC - 1))
                    return last

                def down_tiny(b):
                    dn = down_slot(b)
                    for f in range(FC):
                        for j in range(4):
                            last = pe_e.matmul(Y[j * H32:(j + 1) * H32, 0, 0:QV], hidT[:, f * H32:(f + 1) * H32],
                                               dn[:, f, j * QV:(j + 1) * QV], start=(f == 0), stop=(f == FC - 1))
                    return last

                def down_full(b):
                    dn = down_slot(b)
                    for h in range(2):
                        for f in range(FC):
                            last = pe_e.matmul(Y[:, h, :], hidT[:, f * P:(f + 1) * P], dn[:, f, h * S:(h + 1) * S],
                                               start=(f == 0), stop=(f == FC - 1))
                    return last

                def experts_loop(eng, body):
                    for e in range(2):
                        body(e, e, 0, e, 0)
                    turns = (E - 3) // 6
                    with eng.Fori(0, turns) as i:
                        for r in range(2, 8):
                            body(i * 6 + r, r % 2, i * 3 + r // 2, r % 3, i * 2 + r // 3)
                    for e in range(2 + 6 * turns, E):
                        body(e, e % 2, e // 2, e % 3, e // 3)

                def since(e, n=1):
                    return not isinstance(e, int) or e >= n

                def one_of(eng, c, waits, full, small, tiny):
                    def form(run):
                        for s, v in waits:
                            eng.wait_ge(s, v)
                        run()

                    with eng.If(c > H32):
                        with eng.If(c > H64):
                            form(full)
                        with eng.Else():
                            form(small)
                    with eng.Else():
                        form(tiny)

                def count_of(eng, e):
                    return eng.value_load(counts[0:1, bass.ds(e, 1)], min_val=0, max_val=S)

                def tail(eng, body):
                    eng.wait_ge(s_["overs"], 1)
                    n = eng.value_load(overs[0:1, 0, NOV:NOV + 1], min_val=0, max_val=NOV)
                    with eng.If(n > 0):
                        with eng.Fori(0, NOV) as j:
                            with eng.If(j < n):
                                e = eng.value_load(overs[0:1, 0, bass.ds(j, 1)], min_val=0, max_val=E - 1)
                                k = eng.value_load(overs[0:1, 1, bass.ds(j, 1)], min_val=0, max_val=NB)
                                body(j, e, k)
                            with eng.Else():
                                pass
                    with eng.Else():
                        pass

                with nc.Block() as block:
                    @block.sync
                    def _(sp):
                        def store(e, b, groups):
                            n, per = P // groups, 4 // groups
                            for q in range(4):
                                src = ysb[b][q // per * n:(q // per + 1) * n, q % per * QV:(q % per + 1) * QV]
                                sp.dma_start(ybuf[bass.ds(e * P, n), q * QV:(q + 1) * QV], src).then_inc(s_y[b], 16)

                        def body(e, b, use, g, guse):
                            if not isinstance(e, int) or e + 3 < E:
                                sp.wait_ge(s_["gu"], e + 1)
                                load_gate_up(sp, L, e + 3, g, s_gu[g])
                            if not isinstance(e, int) or e + 2 < E:
                                sp.wait_ge(s_["dn"], e + 1)
                                load_down(sp, L, e + 2, b, s_dn[b])
                            one_of(sp, count_of(sp, e), [(s_["y"], e + 1)],
                                   lambda: store(e, b, 1), lambda: store(e, b, 2), lambda: store(e, b, 4))

                        experts_loop(sp, body)
                        for b in range(2):
                            sp.wait_ge(s_y[b], 32 * E)

                        def extra(j, e, k):
                            load_gate_up(sp, L, e, 0, s_["ow"])
                            load_down(sp, L, e, 0, s_["ow"])
                            sp.wait_ge(s_["oy"], j + 1)
                            sp.dma_start(ybuf[bass.ds(j * P + E * P, P), :], ysb[0]).then_inc(s_["odone"], 16)
                            sp.wait_ge(s_["odone"], j * 16 + 16)
                            sp.sem_inc(s_["ostored"], 1)

                        tail(sp, extra)

                    @block.tensor
                    def _(pe):
                        def gathering(e, c, b):
                            one_of(pe, c, [(s_["sel"], e + 1)] + [(s_["xg"], e)] * since(e),
                                   lambda: gather(b).then_inc(s_["rows"], 1),
                                   lambda: gather_rows(b, H64).then_inc(s_["rows"], 1),
                                   lambda: gather_rows(b, H32).then_inc(s_["rows"], 1))

                        def turning(e, c):
                            one_of(pe, c, [(s_["xr"], e + 1)],
                                   lambda: pe.sem_inc(s_["gx"], 1),
                                   lambda: row_transposes(H64).then_inc(s_["gx"], 1),
                                   lambda: row_transposes(H32).then_inc(s_["gx"], 1))

                        def body(e, b, use, g, guse):
                            last = isinstance(e, int) and e == E - 1
                            c = count_of(pe, e)
                            one_of(pe, c, [(s_gu[g], guse * 32 + 32), (s_["xg"], e + 1)] + [(s_["hid"], e)] * since(e),
                                   lambda: gate_up_full(g, b).then_inc(s_["gu"], 1),
                                   lambda: gate_up_small(g, b).then_inc(s_["gu"], 1),
                                   lambda: gate_up_tiny(g, b).then_inc(s_["gu"], 1))
                            if not last:
                                cn = count_of(pe, e + 1)
                                gathering(e + 1, cn, 1 - b)
                            one_of(pe, c, [(s_["hid"], e + 1)] + [(s_["hidT"], e)] * since(e),
                                   lambda: hidden_transposes(FC).then_inc(s_["tr"], 1),
                                   lambda: hidden_transposes(2).then_inc(s_["tr"], 1),
                                   lambda: hidden_transposes(1).then_inc(s_["tr"], 1))
                            if not last:
                                turning(e + 1, cn)
                            one_of(pe, c, [(s_dn[b], use * 16 + 16), (s_["hidT"], e + 1)] + [(s_["y"], e)] * since(e),
                                   lambda: down_full(b).then_inc(s_["dn"], 1),
                                   lambda: down_small(b).then_inc(s_["dn"], 1),
                                   lambda: down_tiny(b).then_inc(s_["dn"], 1))

                        c0 = count_of(pe, 0)
                        gathering(0, c0, 0)
                        turning(0, c0)
                        experts_loop(pe, body)

                        def extra(j, e, k):
                            pe.wait_ge(s_["osel"], j + 1)
                            gather(0).then_inc(s_["ogx"], 1)
                            pe.wait_ge(s_["ow"], j * 48 + 48)
                            pe.wait_ge(s_["oxg"], j + 1)
                            gate_up_full(0, 0).then_inc(s_["ogu"], 1)
                            pe.wait_ge(s_["ohid"], j + 1)
                            hidden_transposes(FC).then_inc(s_["otr"], 1)
                            pe.wait_ge(s_["ohidT"], j + 1)
                            down_full(0).then_inc(s_["odn"], 1)

                        tail(pe, extra)

                    @block.scalar
                    def _(act):
                        def rows_out(e, c):
                            one_of(act, c, [(s_["rows"], e + 1)] + [(s_["gx"], e)] * since(e),
                                   lambda: act.sem_inc(s_["xr"], 1),
                                   lambda: act_e.activation(xrow[:, :], XR[:, :], ACT.Copy).then_inc(s_["xr"], 1),
                                   lambda: act_e.activation(xrow[:, 0:QV], XR[:, 0:QV], ACT.Copy).then_inc(s_["xr"], 1))

                        def body(e, b, use, g, guse):
                            c = count_of(act, e)
                            one_of(act, c, [(s_["gu"], e + 1)] + [(s_["hid"], e)] * since(e),
                                   lambda: act_e.activation(hs[:, :], G[:, :], ACT.Silu).then_inc(s_["hs"], 1),
                                   lambda: act_e.activation(hs[:, 0:F // 2], G[:, 0:F // 2], ACT.Silu).then_inc(s_["hs"], 1),
                                   lambda: act_e.activation(hs[:, 0:P], G[:, 0:P], ACT.Silu).then_inc(s_["hs"], 1))
                            if not (isinstance(e, int) and e == E - 1):
                                rows_out(e + 1, count_of(act, e + 1))
                            one_of(act, c, [(s_["tr"], e + 1)] + [(s_["dn"], e)] * since(e),
                                   lambda: act_e.activation(hidT[:, :], TR[:, :], ACT.Copy).then_inc(s_["hidT"], 1),
                                   lambda: act_e.activation(hidT[:, 0:2 * P], TR[:, 0:2 * P], ACT.Copy).then_inc(s_["hidT"], 1),
                                   lambda: act_e.activation(hidT[:, 0:P], TR[:, 0:P], ACT.Copy).then_inc(s_["hidT"], 1))
                            both = Y[:, :, :].rearrange("p a b -> p (a b)")
                            one_of(act, c, [(s_["dn"], e + 1)] + [(s_y[b], use * 64)] * since(e, 2),
                                   lambda: act_e.activation(ysb[b], both, ACT.Copy).then_inc(s_["y"], 1),
                                   lambda: act_e.activation(ysb[b][:, 0:S], Y[:, 0, :], ACT.Copy).then_inc(s_["y"], 1),
                                   lambda: act_e.activation(ysb[b][:, 0:QV], Y[:, 0, 0:QV], ACT.Copy).then_inc(s_["y"], 1))

                        rows_out(0, count_of(act, 0))
                        experts_loop(act, body)

                        def extra(j, e, k):
                            act.wait_ge(s_["ogu"], j + 1)
                            act_e.activation(hs[:, :], G[:, :], ACT.Silu).then_inc(s_["ohs"], 1)
                            act.wait_ge(s_["otr"], j + 1)
                            act_e.activation(hidT[:, :], TR[:, :], ACT.Copy).then_inc(s_["ohidT"], 1)
                            act.wait_ge(s_["odn"], j + 1)
                            for b in range(2):
                                act.wait_ge(s_y[b], 32 * E)
                            act_e.activation(ysb[0], Y[:, :, :].rearrange("p a b -> p (a b)"), ACT.Copy).then_inc(s_["oy"], 1)

                        tail(act, extra)

                    @block.vector
                    def _(dve):
                        ch = Chain(dve, s_["late"])

                        def selecting(e, b):
                            if since(e, 2):
                                dve.wait_ge(s_["gx"], e - 1)
                            select(b, lambda t: posm[:, t, bass.ds(e, 1)]).then_inc(s_["sel"], 1)

                        def modulating(e, b):
                            waits = [(s_["gx"], e + 1)] + [(s_["gu"], e - 1)] * since(e, 2)
                            one_of(dve, count_of(dve, e), waits,
                                   lambda: modulate(b, P).then_inc(s_["xg"], 1),
                                   lambda: modulate(b, H64).then_inc(s_["xg"], 1),
                                   lambda: modulate(b, H32).then_inc(s_["xg"], 1))

                        def body(e, b, use, g, guse):
                            last = isinstance(e, int) and e == E - 1
                            c = count_of(dve, e)
                            if not last:
                                selecting(e + 1, 1 - b)
                            one_of(dve, c, [(s_["hs"], e + 1)] + [(s_["tr"], e)] * since(e),
                                   lambda: vec.tensor_tensor(hid[:, :], U[:, :], hs[:, :], ALU.mult).then_inc(s_["hid"], 1),
                                   lambda: vec.tensor_tensor(hid[:, 0:F // 2], G[:, F // 2:F], hs[:, 0:F // 2],
                                                             ALU.mult).then_inc(s_["hid"], 1),
                                   lambda: vec.tensor_tensor(hid[:, 0:P], G[:, P:2 * P], hs[:, 0:P],
                                                             ALU.mult).then_inc(s_["hid"], 1))
                            if not last:
                                modulating(e + 1, 1 - b)
                            if isinstance(e, int) and e == 0:
                                gate_weights(ch)
                            if isinstance(e, int) and e == 1:
                                buffer_rows(ch)
                            if isinstance(e, int) and e == E - 6:
                                later_blocks(ch, L)
                                dve.sem_inc(s_["overs"], 1)

                        selecting(0, 0)
                        modulating(0, 0)
                        experts_loop(dve, body)

                        def extra(j, e, k):
                            dve.wait_ge(s_["gx"], E)
                            off = cst[:, bass.ds(k + C_128B, 1)]
                            vec.tensor_tensor(shifted, posm[:, :, bass.ds(e, 1)].rearrange("p t o -> p (t o)"),
                                              off.to_broadcast([P, TT]), ALU.subtract).then_inc(s_["dve"], 1)
                            dve.wait_ge(s_["dve"], j * 1 + 1)
                            select(0, lambda t: shifted[:, t:t + 1]).then_inc(s_["osel"], 1)
                            dve.wait_ge(s_["ogx"], j + 1)
                            modulate(0, P).then_inc(s_["oxg"], 1)
                            dve.wait_ge(s_["ohs"], j + 1)
                            vec.tensor_tensor(hid[:, :], U[:, :], hs[:, :], ALU.mult).then_inc(s_["ohid"], 1)
                            dve.wait_ge(s_["odn"], j + 1)
                            dve.sem_inc(s_["onext"], 1)

                        dve.wait_ge(s_["dn"], E)
                        tail(dve, extra)

        def combine(tag, L):
            yt = [arena[:, i * D:(i + 1) * D] for i in range(8)]
            tmp = [arena[:, (8 + i) * D:(9 + i) * D] for i in range(2)]
            with ExitStack() as ph:
                s_yg = [sem(f"{tag}_y{i}") for i in range(8)]
                s_a, s_b, s_c, s_d = (sem(f"{tag}_{n}") for n in ("first", "sum", "gated", "x"))
                with nc.Block() as block:
                    @block.gpsimd
                    def _(pool):
                        for t in range(TT):
                            for n in range(2):
                                pool_e.indirect_dma_start(
                                    out=yt[2 * t + n], out_offset=None, in_=ybuf[:, :],
                                    in_offset=bass.IndirectOffsetOnAxis(ap=slots[:, n, t:t + 1], axis=0),
                                ).then_inc(s_yg[2 * t + n], 16)

                    @block.scalar
                    def _(act):
                        for t in range(TT):
                            act.wait_ge(s_yg[2 * t], 16)
                            if t >= 2:
                                act.wait_ge(s_d, t - 1)
                            act_e.activation(tmp[t % 2], yt[2 * t], ACT.Copy, scale=gates[:, 0, t:t + 1]).then_inc(s_a, 1)

                    @block.vector
                    def _(dve):
                        for t in range(TT):
                            dve.wait_ge(s_yg[2 * t + 1], 16)
                            dve.wait_ge(s_a, t + 1)
                            vec.scalar_tensor_tensor(tmp[t % 2], yt[2 * t + 1], gates[:, 1, t:t + 1], tmp[t % 2],
                                                     ALU.mult, ALU.add).then_inc(s_b, 1)
                            dve.wait_ge(s_b, t + 1)
                            vec.tensor_tensor(tmp[t % 2], tmp[t % 2], gbc[:, :], ALU.mult).then_inc(s_c, 1)
                            dve.wait_ge(s_c, t + 1)
                            vec.tensor_tensor(x[:, t, :], x[:, t, :], tmp[t % 2], ALU.add).then_inc(s_d, 1)

        vectors_to_columns("v0", 0, [SH_A, SC_A])
        for L in range(DEPTH):
            n = f"l{L}"
            if L > 0:
                vectors_to_columns(n + "va", L, [SH_A, SC_A])
            norm_transpose(n + "n1", L, SC_A, SH_A)
            attention(n + "at", L, L % 2 == 0)
            vector_broadcast(n + "ga", L, G_A)
            s_gu = [sem(f"{n}_wgu{i}") for i in range(3)]
            s_dn = [sem(f"{n}_wdn{i}") for i in range(2)]
            out_projection(n + "op", L, s_gu, s_dn)
            vectors_to_columns(n + "vm", L, [SH_M, SC_M])
            vector_broadcast(n + "gm", L, G_M)
            norm_transpose(n + "n2", L, SC_M, SH_M, lambda sp: load_gate_up(sp, L, 2, 2, s_gu[2]))
            router(n + "ro")
            experts(n + "ex", L, s_gu, s_dn)
            combine(n + "co", L)
            clear_semaphores()

        with ExitStack() as ph:
            gf = arena[:, 16384:17408]
            junk = arena[:, 17408:18432]
            s_g, s_ss, s_rs, s_n, s_o, s_w = (sem("fin_" + n) for n in ("g", "sumsq", "rstd", "normed", "scaled", "stored"))
            with nc.Block() as block:
                @block.sync
                def _(sp):
                    sp.dma_start(gf, final_g.partition_broadcast(P)).then_inc(s_g, 16)
                    for t in range(TT):
                        sp.wait_ge(s_o, t + 1)
                        sp.dma_start(out[0].rearrange("(t p) d -> t p d", p=P)[t], x[:, t, :]).then_inc(s_w, 16)
                    sp.wait_ge(s_w, 16 * TT)

                @block.scalar
                def _(act):
                    for t in range(TT):
                        act_e.activation(junk, x[:, t, :], ACT.Square, accum_out=ss[:, t:t + 1]).then_inc(s_ss, 1)
                        act.wait_ge(s_ss, t + 1)
                    act_e.activation(rstd, ss, ACT.Ln, scale=1.0 / D, bias=eps).then_inc(s_ss, 1)
                    act.wait_ge(s_ss, TT + 1)
                    act_e.activation(rstd, rstd, ACT.Exp, scale=-0.5).then_inc(s_rs, 1)

                @block.vector
                def _(dve):
                    dve.wait_ge(s_g, 16)
                    dve.wait_ge(s_rs, 1)
                    for t in range(TT):
                        vec.scalar_tensor_tensor(x[:, t, :], x[:, t, :], rstd[:, t:t + 1], gf, ALU.mult,
                                                 ALU.mult).then_inc(s_o, 1)


def constants():
    import numpy as np

    c = np.zeros((P, C_N), np.float32)
    r, n = np.arange(P)[:, None], np.arange(P)[None, :]
    c[:, C_ID:C_ID + P] = r == n
    c[:, C_ONE:C_ONE + P] = 1
    for j in range(4):
        c[32 * j, C_SEL + j * P:C_SEL + (j + 1) * P] = 1
    c[:, C_IOTA:C_IOTA + P] = n
    c[:, C_FOLD:C_FOLD + E] = r % E == np.arange(E)[None, :]
    c[:, C_MC:C_MC + P] = np.where(n > r, -BIG, 0)
    c[:, C_MS:C_MS + P] = np.where(n >= r, -BIG, 0)
    c[:, C_TRI:C_TRI + P] = r < n
    c[:, C_E:C_E + E] = P * np.arange(E)
    c[:, C_REV:C_REV + E] = E - np.arange(E)
    c[:, C_GRV:C_GRV + NG] = NG - np.arange(NG)
    half = 8
    f = np.arange(P) % H64
    c[:, C_EPS] = EPS
    c[:, C_INVF] = np.power(np.float32(500000.0), -(f % half).astype(np.float32) * np.float32(2.0 / (2 * half)))
    c[:, C_SGN] = np.where(f < half, -1, np.where(f < 2 * half, 1, 0))
    c[:, C_ROT] = f < 2 * half
    c[:, C_PASS] = f >= 2 * half
    for b in range(NB):
        c[:, C_OVE + b * E:C_OVE + (b + 1) * E] = np.arange(E)
        c[:, C_OVB + b * E:C_OVB + (b + 1) * E] = b + 1
        c[:, C_128B + b + 1] = P * (b + 1)
    c[:, C_OVJ:C_OVJ + NOV] = np.arange(NOV) + 1
    return c


_INS = ["x", "c", "positions", "w_ada", "b_ada", "norm_g", "w_in", "w_out", "diff_lambda", "diff_subln_g",
        "w_router", "b_router", "w_gate", "w_up", "w_down", "final_norm_g"]


def kernel(**inputs):
    import numpy as np
    import concourse.bacc as bacc
    from concourse.bass_utils import run_bass_kernel_spmd

    nc = bacc.Bacc("TRN2", target_bir_lowering=False, num_devices=1)
    arrays, args = {}, []
    for name in _INS:
        a = np.ascontiguousarray(inputs[name])
        arrays[f"in_{name}"] = a
        args.append(nc.dram_tensor(f"in_{name}", a.shape, mybir.dt.from_np(a.dtype), kind="ExternalInput").ap())
    arrays["in_consts"] = constants()
    args.append(nc.dram_tensor("in_consts", (P, C_N), F32, kind="ExternalInput").ap())
    args.append(nc.dram_tensor("out_0", (1, S, D), F32, kind="ExternalOutput").ap())
    build_trunk(nc, *args)
    r = run_bass_kernel_spmd(nc, [arrays], core_ids=[0])
    return r.results[0]["out_0"]
```

```python
from contextlib import ExitStack

import concourse.bass as bass
from concourse import mybir

ALU = mybir.AluOpType
ACT = mybir.ActivationFunctionType
AX = mybir.AxisListType
F32 = mybir.dt.float32
F32R = mybir.dt.float32r
BF16 = mybir.dt.bfloat16
I32 = mybir.dt.int32
U32 = mybir.dt.uint32

P = 128
D = 1024
S = 512
DEPTH = 2
KC = D // P
TT = S // P
H64 = P // 2
H32 = P // 4
E = 32
NG = 4
EG = E // NG
F = D // 2
FC = F // P
NV = 6
QV = D // 4
EPS = 1e-6
BIG = 1e30
STEPS = KC + 1
NOV = 7
NB = 3
YROWS = 40 * P
WA = 4
SH_A, SC_A, G_A, SH_M, SC_M, G_M = range(NV)

C_ID, C_ONE, C_SEL, C_IOTA, C_FOLD, C_MC, C_MS, C_TRI = 0, 128, 256, 768, 896, 928, 1056, 1184
C_E, C_REV, C_GRV, C_COL = 1312, 1344, 1376, 1380
C_EPS, C_INVF, C_SGN, C_ROT, C_PASS = range(C_COL, C_COL + 5)
C_OVE, C_OVB, C_OVJ, C_128B = 1385, 1481, 1577, 1584
C_N = 1680


class Chain:

    def __init__(self, eng, sem):
        self.eng, self.sem, self.base, self.n = eng, sem, 0, 0

    def link(self, ins):
        self.n += 1
        ins.then_inc(self.sem, 1)
        self.eng.wait_ge(self.sem, self.base + self.n)

    def enter(self, it, per):
        self.before = self.base + self.n
        self.base, self.n, self.per = self.before + it * per, 0, per

    def leave(self, turns):
        assert self.n == self.per, (self.n, self.per)
        self.base, self.n = self.before, turns * self.per


def build_trunk(nc, x_in, c_in, positions, w_ada, b_ada, norm_g, w_in, w_out, diff_lambda, diff_subln_g,
                w_router, b_router, w_gate, w_up, w_down, final_g, consts, out):
    with ExitStack() as ctx:
        place = {}

        def sb(name, shape, dt=F32):
            tensor = ctx.enter_context(nc.sbuf_tensor(name, shape, dt))
            count = 1
            for n in shape[1:]:
                count *= n
            place[name] = nc.sbuf_base - 4 * count
            return tensor

        held = []

        def sem(name):
            held.append(nc.alloc_semaphore(name=name))
            return held[-1]

        def clear_semaphores():
            nc.clear_and_free_semaphores(held)
            held.clear()
            nc.all_engine_barrier()

        vec, act_e, pool_e, pe_e = nc.vector, nc.scalar, nc.gpsimd, nc.tensor

        x = sb("x_res", [P, TT, D])
        hT = sb("hT", [P, KC, S])
        cst = sb("cst", [P, C_N])
        cbf = sb("cbf", [P, 5 * P], BF16)
        modrow = sb("modrow", [P, DEPTH * NV, QV])
        modcol = sb("modcol", [P, DEPTH * NV, KC])
        gbc = sb("gbc", [P, D])
        veccol = sb("veccol", [P, 41])
        cact = sb("cact", [P, KC, 32])
        wrt = sb("wrt", [P, KC, E])
        brt = sb("brt", [P, E])
        small = sb("small", [P, 64])
        arena = sb("arena", [P, 2 * 12288])
        region = sb("region", [P, 12288])
        posm = sb("posm", [P, TT, E])
        slots = sb("slots", [P, 2, TT], U32)
        gates = sb("gates", [P, 2, TT])
        counts = sb("counts", [1, E], I32)
        overs = sb("overs", [1, 2, 8], I32)
        xrow = sb("xrow", [P, S])
        ybuf = nc.dram_tensor("ybuf", [YROWS, D], F32).ap()

        def as_float32r(name, shape, under, first):
            return nc.alloc_sbuf_tensor_at(name, shape, F32R, offset=place[under] + 4 * first)

        h_lo = as_float32r("h_low", [P, KC, S], "hT", 0)
        h_hi = as_float32r("h_high", [P, KC, S], "region", 4096)
        w_lo = [as_float32r(f"w_low{i}", [P, KC, 3, P], "arena", i * 3072) for i in range(2)]
        w_hi = as_float32r("w_high", [P, KC, 3, P], "region", 8192)

        ident = cst[:, C_ID:C_ID + P]
        ones = cst[:, C_ONE:C_ONE + P]
        identb, onesb, maskc, masks, trib = (cbf[:, i * P:(i + 1) * P] for i in range(5))
        eps = cst[:, C_EPS:C_EPS + 1]
        neglam = small[:, 0:1]
        subg = small[:, 1:2]
        ss, rstd = small[:, 4:8], small[:, 8:12]
        nmx = small[:, 12:16].rearrange("p (a b) -> p a b", a=2)
        lsum = small[:, 16:20].rearrange("p (a b) -> p a b", a=2)
        lrec = small[:, 20:24].rearrange("p (a b) -> p a b", a=2)

        def modvec(L, v):
            return modcol[:, L * NV + v, :]

        def bank(name, shape, stack):
            return stack.enter_context(nc.psum_tensor(name, shape, F32))

        w_ada_rows = w_ada.rearrange("l (k p) n -> l k p n", p=P)

        def ada_products(pe, banks, wa, s_wa, s_used):
            for n, ps in enumerate(banks):
                for k in range(KC):
                    m = n * KC + k
                    pe.wait_ge(s_wa[m % WA], 16 * (m // WA + 1))
                    for j in range(4):
                        last = pe_e.matmul(ps[32 * j:32 * j + 32, 0:QV], cact[:, k, :],
                                           wa[m % WA][:, j * QV:(j + 1) * QV], start=(k == 0), stop=(k == KC - 1))
                    last.then_inc(s_used, 1)

        with ExitStack() as ph:
            psT = bank("su_psT", [P, 512], ph)
            psA = [bank(f"su_psA{i}", [P, 512], ph) for i in range(2)]
            s_cst, s_vec, s_x, s_bias, s_misc = sem("su_cst"), sem("su_vec"), sem("su_x"), sem("su_bias"), sem("su_misc")
            s_wa = [sem(f"su_wa{i}") for i in range(WA)]
            s_t, s_col, s_cact, s_row, s_use, s_ch, s_ach = (sem("su_" + n) for n in (
                "vecT", "veccol", "cact", "modrow", "waused", "dve", "act"))
            s_lam, s_lexp, s_z = sem("su_lam"), sem("su_lamexp"), sem("su_zero")
            vrows = region[0:41, 0:P]
            lamb = region[:, 128:384]
            lamt = region[:, 384:448]
            wa = [arena[:, 4096 + i * 1024:4096 + (i + 1) * 1024] for i in range(WA)]

            with nc.Block() as block:
                @block.sync
                def _(sp):
                    sp.dma_start(vrows[0:32, :], norm_g.rearrange("l i (k p) -> (l i k) p", p=P)).then_inc(s_vec, 16)
                    sp.dma_start(vrows[32:40, :], c_in.rearrange("a (k p) -> (a k) p", p=P)).then_inc(s_vec, 16)
                    sp.dma_start(vrows[40:41, :], diff_subln_g).then_inc(s_vec, 16)
                    sp.dma_start(cst[:, :], consts).then_inc(s_cst, 16)
                    for m in range(2 * KC):
                        v, k = m // KC, m % KC
                        if m >= WA:
                            sp.wait_ge(s_use, m - WA + 1)
                        sp.dma_start(wa[m % WA], w_ada_rows[0, k, :, v * D:(v + 1) * D]).then_inc(s_wa[m % WA], 16)
                    sp.wait_ge(s_x, 16)
                    sp.wait_ge(s_misc, 48)

                @block.gpsimd
                def _(pool):
                    pool.dma_start(x[:, :, :], x_in[0].rearrange("(t p) d -> p t d", p=P)).then_inc(s_x, 16)
                    for j in range(4):
                        src = b_ada.rearrange("l (v j n) -> j (l v) n", v=NV, j=4)[j]
                        pool.dma_start(modrow[32 * j:32 * j + 32, :, :], src.partition_broadcast(32)).then_inc(s_bias, 16)
                    pool.dma_start(lamb, diff_lambda.rearrange("a b c -> a (b c)")[0].partition_broadcast(P)).then_inc(s_lam, 16)
                    pool.dma_start(wrt[:, :, :], w_router.rearrange("(k p) e -> p k e", p=P)).then_inc(s_misc, 16)
                    pool.dma_start(brt[:, :], b_router.partition_broadcast(P)).then_inc(s_misc, 16)
                    pool.dma_start(region[:, 512:1024].bitcast(I32), positions[0].partition_broadcast(P)).then_inc(s_misc, 16)

                @block.tensor
                def _(pe):
                    pe.wait_ge(s_vec, 48)
                    pe.wait_ge(s_cst, 16)
                    pe_e.transpose(psT[:, 0:41], vrows, cst[0:41, C_ID:C_ID + 41]).then_inc(s_t, 1)
                    pe.wait_ge(s_cact, 1)
                    ada_products(pe, psA, wa, s_wa, s_use)

                @block.scalar
                def _(act):
                    ch = Chain(act, s_ach)
                    act.wait_ge(s_col, 1)
                    act_e.activation(cact[:, :, :], veccol[:, 32:40].unsqueeze(2).to_broadcast([P, KC, 32]),
                                     ACT.Silu).then_inc(s_cact, 1)
                    act.wait_ge(s_cst, 16)
                    for i, col in enumerate((C_ID, C_ONE, C_MC, C_MS, C_TRI)):
                        last = act_e.activation(cbf[:, i * P:(i + 1) * P], cst[:, col:col + P], ACT.Copy)
                    ch.link(last)
                    act.wait_ge(s_lexp, 1)
                    act_e.activation(small[:, 2:4], small[:, 2:4], ACT.Exp).then_inc(s_lexp, 1)

                @block.vector
                def _(dve):
                    ch = Chain(dve, s_ch)
                    dve.wait_ge(s_t, 1)
                    vec.tensor_copy(veccol[:, :], psT[:, 0:41]).then_inc(s_col, 1)
                    dve.wait_ge(s_lam, 16)
                    for i in range(2):
                        ch.link(vec.tensor_tensor(lamt, lamb[:, i * 128:i * 128 + 64],
                                                  lamb[:, i * 128 + 64:i * 128 + 128], ALU.mult))
                        ch.link(vec.tensor_reduce(small[:, 2 + i:3 + i], lamt, AX.X, ALU.add))
                    vec.memset(small[:, 4:64], 0.0).then_inc(s_lexp, 1)
                    dve.wait_ge(s_lexp, 2)
                    ch.link(vec.tensor_tensor(neglam, small[:, 3:4], small[:, 2:3], ALU.subtract))
                    lam_init = 0.8 - 0.6 * 1.0
                    ch.link(vec.tensor_scalar(neglam, neglam, -lam_init, None, ALU.add))
                    dve.wait_ge(s_col, 1)
                    ch.link(vec.tensor_scalar(subg, veccol[:, 40:41], 1.0 - lam_init, None, ALU.mult))
                    dve.wait_ge(s_bias, 64)
                    for v in range(2):
                        dve.wait_ge(s_use, (v + 1) * KC)
                        vec.tensor_tensor(modrow[:, v, :], psA[v][:, 0:QV], modrow[:, v, :], ALU.add).then_inc(s_row, 1)
                    dve.wait_ge(s_row, 2)


        def columns_on_pe(ps, L, which):
            for n, v in enumerate(which):
                for i in range(2):
                    last = pe_e.transpose(ps[:, n, i, :], modrow[:, L * NV + v, i * P:(i + 1) * P], ident)
            return last

        def columns_out(ch, ps, L, which):
            for n, v in enumerate(which):
                dst = modvec(L, v).rearrange("p (j i) -> p i j", i=2)
                ch.link(vec.tensor_copy(dst, ps[:, n, :, 0:P:32]))
                if v in (SC_A, SC_M):
                    g = veccol[:, (2 * L + (v == SC_M)) * KC:(2 * L + (v == SC_M)) * KC + KC]
                    ch.link(vec.scalar_tensor_tensor(modvec(L, v), modvec(L, v), 1.0, g, ALU.add, ALU.mult))

        def broadcast_on_pe(ps, L, v):
            for j in range(4):
                sel = cst[:, C_SEL + j * P:C_SEL + (j + 1) * P]
                last = pe_e.matmul(ps[:, j, :], sel, modrow[:, L * NV + v, :], start=True, stop=True)
            return last

        def vectors_to_columns(tag, L, which):
            with ExitStack() as ph:
                ps = bank(tag + "_ps", [P, len(which), 2, P], ph)
                s_p, s_ch = sem(tag + "_T"), sem(tag + "_dve")
                with nc.Block() as block:
                    @block.tensor
                    def _(pe):
                        columns_on_pe(ps, L, which).then_inc(s_p, 1)

                    @block.vector
                    def _(dve):
                        dve.wait_ge(s_p, 1)
                        columns_out(Chain(dve, s_ch), ps, L, which)

        win = [arena[:, i * 3072:(i + 1) * 3072].rearrange("p (k g n) -> p k g n", k=KC, g=3) for i in range(2)]
        s_w_in = [[nc.alloc_semaphore(name=f"w_in{L}_{i}") for i in range(2)] for L in range(DEPTH)]

        def load_w_in(sp, L, s, b):
            wv = w_in[L].rearrange("(k p) (g c n) -> p k g c n", p=P, g=3, c=KC)
            for g in range(3):
                src = wv[:, :, g, bass.ds(s, 1), :].rearrange("p k c n -> p k (c n)")
                sp.dma_start(win[b][:, :, g, :], src).then_inc(s_w_in[L][b], 16)

        def load_first_w_in(sp, L):
            for b in range(2):
                load_w_in(sp, L, b, b)

        def norm_transpose(tag, L, sc, sh, prefetch=None):
            with ExitStack() as ph:
                ps = [bank(f"{tag}_ps{i}", [P, KC, P], ph) for i in range(2)]
                s_rs, s_ach, s_xn, s_tr, s_ea, s_ed = (sem(f"{tag}_{n}") for n in (
                    "rstd", "act", "xn", "transposed", "evac_act", "evac_dve"))
                xn = [region[:, 8192 + i * D:8192 + (i + 1) * D] for i in range(2)]
                junk = region[:, 8192 + 2 * D:8192 + 3 * D]
                with nc.Block() as block:
                    if prefetch is not None:
                        block.sync(prefetch)

                    @block.scalar
                    def _(act):
                        ch = Chain(act, s_ach)
                        for t in range(TT):
                            ch.link(act_e.activation(junk, x[:, t, :], ACT.Square, accum_out=ss[:, t:t + 1]))
                        act_e.activation(ss, ss, ACT.Sqrt, scale=1.0 / D, bias=eps).then_inc(s_rs, 1)
                        for t in range(TT):
                            act.wait_ge(s_tr, t + 1)
                            for k in range(KC // 2):
                                last = act_e.activation(hT[:, k, t * P:(t + 1) * P], ps[t % 2][:, k, :], ACT.Identity,
                                                        scale=modvec(L, sc)[:, k:k + 1], bias=modvec(L, sh)[:, k:k + 1])
                            last.then_inc(s_ea, 1)

                    @block.vector
                    def _(dve):
                        dve.wait_ge(s_rs, 1)
                        vec.reciprocal(rstd, ss).then_inc(s_rs, 1)
                        dve.wait_ge(s_rs, 2)

                        def normalise(t):
                            if t >= 2:
                                dve.wait_ge(s_tr, t - 1)
                            vec.tensor_scalar(xn[t % 2], x[:, t, :], rstd[:, t:t + 1], None, ALU.mult).then_inc(s_xn, 1)

                        normalise(0)
                        for t in range(TT):
                            if t + 1 < TT:
                                normalise(t + 1)
                            dve.wait_ge(s_tr, t + 1)
                            for k in range(KC // 2, KC):
                                last = vec.tensor_scalar(hT[:, k, t * P:(t + 1) * P], ps[t % 2][:, k, :],
                                                         modvec(L, sc)[:, k:k + 1], modvec(L, sh)[:, k:k + 1],
                                                         ALU.mult, ALU.add)
                            last.then_inc(s_ed, 1)

                    @block.tensor
                    def _(pe):
                        for t in range(TT):
                            pe.wait_ge(s_xn, t + 1)
                            if t >= 2:
                                pe.wait_ge(s_ea, t - 1)
                                pe.wait_ge(s_ed, t - 1)
                            for k in range(KC):
                                last = pe_e.transpose(ps[t % 2][:, k, :], xn[t % 2][:, k * P:(k + 1) * P], ident)
                            last.then_inc(s_tr, 1)

        def attention(tag, L, diff):
            A = arena
            wa = [A[:, 6144 + i * 1024:6144 + (i + 1) * 1024] for i in range(WA)]
            qz = [A[:, 10240 + i * 1024:10240 + (i + 1) * 1024].rearrange("p (h n) -> p h n", h=2) for i in range(2)]
            kT = [A[:, 12288 + i * 512:12288 + (i + 1) * 512] for i in range(2)]
            vn = [A[:, 13312 + i * 512:13312 + (i + 1) * 512].rearrange("p (t n) -> p t n", t=TT) for i in range(2)]
            vT = A[:, 14336:14848]
            aT = [A[:, 14848 + i * 2048:14848 + (i + 1) * 2048].rearrange("p (k q) -> p k q", k=TT) for i in range(2)]
            tA = [A[:, 18944 + i * 1024:18944 + (i + 1) * 1024].rearrange("p (h n) -> p h n", h=2) for i in range(2)]
            tB = [A[:, 20992 + i * 1024:20992 + (i + 1) * 1024].rearrange("p (h n) -> p h n", h=2) for i in range(2)]
            raw = A[:, 23040:23552]
            shf = A[:, 23552:24064]
            cosT, sinT, osb, osq = (A[:, 16896 + i * 512:16896 + (i + 1) * 512] for i in range(4))
            oT = region[:, 0:4096].rearrange("p (k n) -> p k n", k=KC)
            wo = region[:, 4096:12288].rearrange("p (k n) -> p k n", k=KC)
            NH = 1 if diff else 2
            with ExitStack() as ph:
                Z = [bank(f"{tag}_Z{i}", [P, 2, S], ph) for i in range(2)]
                PB = [bank(f"{tag}_P{i}", [P, S], ph) for i in range(2)]
                TR = bank(tag + "_TR", [P, S], ph)
                O = bank(tag + "_O", [P, S], ph)
                names = ("proj q_evac k_evac v_evac q_ready k_ready z_done nm_done p_done a_done t_done tr_evac vt_done "
                         "v_ready pv_done o_evac sp_done d_done used row ss_done rs_done rstd angles tables o_done dve act zero fill wo h_high h_low w0_high w0_low w_high w_low").split()
                s_ = {n: sem(f"{tag}_{n}") for n in names}
                s_win = s_w_in[L]
                s_wa = [sem(f"{tag}_wa{i}") for i in range(WA)]
                if not diff:
                    s_["q_ready"], s_["k_ready"] = s_["q_evac"], s_["k_evac"]
                z_free = s_["p_done"] if diff else s_["d_done"]
                ada = {0: [G_A], 1: [SH_M], STEPS - 1: [SC_M, G_M]} if diff else {}

                def steps(body, eng_obj, chains=(), per=()):
                    body(0, 0, 0)
                    body(1, 1, 0)
                    turns = (STEPS - 3) // 2
                    with eng_obj.Fori(0, turns) as i:
                        for c, n in zip(chains, per):
                            c.enter(i, n)
                        body(i * 2 + 2, 0, i + 1)
                        body(i * 2 + 3, 1, i + 1)
                    for c in chains:
                        c.leave(turns)
                    body(STEPS - 1, 0, turns + 1)
                    body(STEPS, 1, turns + 1)

                def rope_angles(dve, ch):
                    two_pi = (6.28125, 0.0019353071795864769)
                    magic = 12582912.0
                    ch.link(vec.tensor_copy(raw, region[:, 512:1024].bitcast(I32)))
                    ch.link(vec.tensor_scalar(raw, raw, cst[:, C_INVF:C_INVF + 1], None, ALU.mult))
                    ch.link(vec.tensor_scalar(shf, raw, 0.15915494309189535, magic, ALU.mult, ALU.add))
                    ch.link(vec.tensor_scalar(shf, shf, -magic, None, ALU.add))
                    for part in two_pi:
                        ch.link(vec.scalar_tensor_tensor(raw, shf, -part, raw, ALU.mult, ALU.add))
                    ch.link(vec.tensor_scalar(cosT, raw, 1.5707963267948966, None, ALU.add))
                    ch.link(vec.tensor_scalar(shf, cosT, 3.141592653589793, -6.283185307179586, ALU.is_gt, ALU.mult))
                    ch.link(vec.tensor_tensor(cosT, cosT, shf, ALU.add))
                    for dst, src in ((cosT, cosT), (sinT, raw)):
                        last = vec.tensor_scalar(dst, src, 3.1415925, -3.1415925, ALU.min, ALU.max)
                    last.then_inc(s_["angles"], 1)

                def doing(s):
                    if not isinstance(s, int):
                        return True, True, True
                    return s < KC, 1 <= s <= KC, s >= 2

                with nc.Block() as block:
                    @block.sync
                    def _(sp):
                        def body(s, b, use):
                            if not doing(s)[0]:
                                return
                            if not isinstance(s, int) or s >= 2:
                                sp.wait_ge(s_["proj"], (s - 1) * 3)
                                load_w_in(sp, L, s, b)
                            if diff:
                                if isinstance(s, int) and s == 0:
                                    sp.wait_ge(s_["zero"], 3)
                                for n in range(YROWS // P // KC):
                                    rows = bass.ds(s * (YROWS // KC) + n * P, P)
                                    sp.dma_start(ybuf[rows, :], gbc[:, :]).then_inc(s_["fill"], 16)

                        steps(body, sp)
                        if diff:
                            sp.wait_ge(s_["fill"], 16 * YROWS // P)
                        sp.wait_ge(s_["proj"], 3 * KC)
                        sp.dma_start(wo, w_out[L].rearrange("(k p) n -> p k n", p=P)).then_inc(s_["wo"], 16)
                        sp.wait_ge(s_["wo"], 16)

                    @block.gpsimd
                    def _(pool):
                        def split_w_in(s, b, use):
                            pool.wait_ge(s_win[b], use * 48 + 48)
                            for g in range(3):
                                w, high, low = (m[:, :, g, :] for m in (win[b], w_hi, w_lo[b]))
                                pool.wait_ge(s_["proj"], (s - 1) * 3 + g + 1)
                                pool_e.tensor_tensor(high, w, ones.unsqueeze(1).to_broadcast([P, KC, P]),
                                                     ALU.mult).then_inc(s_["w_high"], 1)
                                pool.wait_ge(s_["w_high"], (s - 1) * 3 + g + 1)
                                pool_e.tensor_tensor(low, w, high.bitcast(F32), ALU.subtract).then_inc(s_["w_low"], 1)

                        for i in range(2):
                            pool_e.memset(qz[i][:, :, :], 0.0).then_inc(s_["zero"], 1)
                        if diff:
                            pool_e.memset(gbc[:, :], 0.0).then_inc(s_["zero"], 1)
                            pool.sem_inc(s_["o_done"], 1)

                        def tile(vector, m0, k, row, col):
                            m = m0 + k
                            if not isinstance(m, int) or m >= WA:
                                pool.wait_ge(s_["used"], m - (WA - 1))
                            src = w_ada.rearrange("l r n -> (l r) n")[bass.ds(row, P), bass.ds(col, D)]
                            pool.dma_start(wa[k % WA], src).then_inc(s_wa[k % WA], 16)

                        def body(s, b, use):
                            static = isinstance(s, int)
                            if doing(s)[0] and not (static and s == 0):
                                split_w_in(s, b, use)
                            vs = (ada.get(s, []) if static else [None]) if diff else []
                            for n, v in enumerate(vs):
                                for k in range(KC):
                                    if static:
                                        tile(v, (s + n) * KC, k, k * P, v * D)
                                    else:
                                        tile(v, s * KC, k, D + k * P, (s - 2) * D)

                        steps(body, pool)

                    @block.tensor
                    def _(pe):
                        def project(s, b, use, g):
                            if g == 0:
                                if not isinstance(s, int) or s >= 1:
                                    pe.wait_ge(s_["v_evac"], s)
                            elif g == 1:
                                if not isinstance(s, int) or s >= 1:
                                    pe.wait_ge(s_["k_evac"], s)
                                    if diff:
                                        pe.wait_ge(s_["row"], s)
                            else:
                                pe.wait_ge(s_["q_evac"], s + 1)
                            if isinstance(s, int) and s == 0:
                                pe.wait_ge(s_["w0_low"], g + 1)
                            else:
                                pe.wait_ge(s_["w_low"], (s - 1) * 3 + g + 1)
                            for k in range(KC):
                                if isinstance(s, int) and s == 0 and g == 0:
                                    pe.wait_ge(s_["h_low"], k + 1)
                                whi, wlo, hhi, hlo = w_hi[:, k, g, :], w_lo[b][:, k, g, :], h_hi[:, k, :], h_lo[:, k, :]
                                pe_e.matmul(PB[g % 2][:, :], wlo, hhi, start=(k == 0), stop=False)
                                pe_e.matmul(PB[g % 2][:, :], whi, hlo, start=False, stop=False)
                                last = pe_e.matmul(PB[g % 2][:, :], whi, hhi, start=False, stop=(k == KC - 1))
                            last.then_inc(s_["proj"], 1)

                        def ada_half(s, b, half, extra=0):
                            if half == 0:
                                if isinstance(s, int) and s == STEPS - 1:
                                    pe.wait_ge(s_["row"], s + extra)
                                else:
                                    pe.wait_ge(s_["k_evac"], s + 1)
                            for k in range(4 * half, 4 * half + 4):
                                m = (s + extra) * KC + k
                                pe.wait_ge(s_wa[k % WA], ((s + extra) * 2 + half + 1) * 16)
                                for j in range(4):
                                    last = pe_e.matmul(PB[1][32 * j:32 * j + 32, 0:QV], cact[:, k, :],
                                                       wa[k % WA][:, j * QV:(j + 1) * QV],
                                                       start=(k == 0), stop=(k == KC - 1))
                                last.then_inc(s_["used"], 1)

                        def scores(s, cb, qb):
                            n = (s - 1) * 4 + qb
                            if qb == 0:
                                pe.wait_ge(s_["q_ready"], s)
                                pe.wait_ge(s_["k_ready"], s)
                            if not isinstance(n, int) or n >= 2:
                                pe.wait_ge(z_free, n - 1)
                            N = (qb + 1) * P
                            for h in range(2):
                                pe_e.matmul(Z[qb % 2][:, h, 0:N], qz[cb][:, h, qb * P:N], kT[cb][:, 0:N],
                                            start=True, stop=False)
                                last = pe_e.matmul(Z[qb % 2][:, h, qb * P:N], identb, maskc if diff else masks,
                                                   start=False, stop=True)
                            last.then_inc(s_["z_done"], 1)

                        def transposes(s, qb):
                            n = (s - 1) * 4 + qb
                            pe.wait_ge(s_["a_done"], n + 1)
                            if not isinstance(n, int) or n >= 1:
                                pe.wait_ge(s_["tr_evac"], n * NH)
                            if qb == 0:
                                pe.wait_ge(s_["v_ready"], s)
                                if NH == 2 and (not isinstance(s, int) or s >= 2):
                                    pe.wait_ge(s_["o_evac"], s - 1)
                            for h in range(NH):
                                src = tB[qb % 2] if diff else tA[qb % 2]
                                for kc in range(qb + 1):
                                    last = pe_e.transpose((TR, O)[h][:, kc * P:(kc + 1) * P],
                                                          src[:, h, kc * P:(kc + 1) * P], ident)
                                last.then_inc(s_["t_done"], 1)

                        def values(s, cb):
                            pe.wait_ge(s_["v_ready"], s - 1)
                            pe.wait_ge(s_["tr_evac"], (s - 1) * (4 * NH))
                            if diff:
                                pe.wait_ge(s_["o_done"], s - 1)
                            for kc in range(TT):
                                for h in range(NH):
                                    rows = slice(0, P) if diff else slice(h * H64, (h + 1) * H64)
                                    last = pe_e.matmul(O[rows, kc * P:S], vn[cb][:, kc, rows], aT[h][:, kc, kc * P:S],
                                                       start=(kc == 0), stop=(kc == TT - 1))
                            last.then_inc(s_["pv_done"], 1)

                        def square_sum(s):
                            pe.wait_ge(s_["o_evac"], s - 1)
                            pe_e.matmul(O[:, :], ones, osq, start=True, stop=True).then_inc(s_["ss_done"], 1)

                        def v_transpose(s):
                            pe.wait_ge(s_["v_evac"], s)
                            if not isinstance(s, int) or s >= 2:
                                pe.wait_ge(s_["tr_evac"], (s - 1) * (4 * NH))
                            for t in range(TT):
                                last = pe_e.transpose(TR[:, t * P:(t + 1) * P], vT[:, t * P:(t + 1) * P], ident)
                            last.then_inc(s_["vt_done"], 1)

                        def body(s, b, use):
                            proj, attend, weigh = doing(s)
                            cb = 1 - b
                            if attend:
                                scores(s, cb, 0)
                                scores(s, cb, 1)
                            if weigh:
                                values(s, b)
                            if attend:
                                v_transpose(s)
                            if proj:
                                project(s, b, use, 0)
                            if weigh and diff:
                                square_sum(s)
                            if attend:
                                transposes(s, 0)
                                scores(s, cb, 2)
                                transposes(s, 1)
                                scores(s, cb, 3)
                            if proj:
                                project(s, b, use, 1)
                            elif diff and attend:
                                ada_half(s, b, 0, 0)
                                ada_half(s, b, 1, 0)
                            if not diff and proj:
                                project(s, b, use, 2)
                            if attend:
                                transposes(s, 2)
                            if diff and proj:
                                ada_half(s, b, 0)
                                project(s, b, use, 2)
                                ada_half(s, b, 1)
                            elif diff and attend:
                                ada_half(s, b, 0, 1)
                                ada_half(s, b, 1, 1)
                            if attend:
                                transposes(s, 3)

                        pe.wait_ge(s_["zero"], 2)
                        steps(body, pe)

                    @block.scalar
                    def _(act):
                        ch = Chain(act, s_["act"])

                        def exps(s, qb):
                            n, N, b = (s - 1) * 4 + qb, (qb + 1) * P, qb % 2
                            act.wait_ge(s_["nm_done"], n + 1)
                            if not isinstance(n, int) or n >= 2:
                                act.wait_ge(s_["a_done"], n - 1)
                            for h in range(2):
                                last = act_e.activation(tA[b][:, h, 0:N], Z[b][:, h, 0:N], ACT.Exp,
                                                        bias=nmx[:, b, h:h + 1], accum_out=lsum[:, b, h:h + 1])
                            last.then_inc(s_["p_done"], 1)

                        def softplus_terms(s, pair):
                            blocks = [((s - 1) * 4 + qb, (qb + 1) * P, qb % 2) for qb in pair]
                            for n, N, b in blocks:
                                act.wait_ge(s_["z_done"], n + 1)
                                if not isinstance(n, int) or n >= 2:
                                    act.wait_ge(s_["t_done"], (n - 1) * 2)
                                ch.link(act_e.activation(tA[b][:, :, 0:N], Z[b][:, :, 0:N], ACT.Abs))
                                last = act_e.activation(tA[b][:, :, 0:N], tA[b][:, :, 0:N], ACT.Exp, scale=-1.0)
                                ch.link(last)
                            for n, N, b in blocks:
                                act_e.activation(tA[b][:, :, 0:N], tA[b][:, :, 0:N], ACT.Ln,
                                                 bias=1.0).then_inc(s_["sp_done"], 1)

                        def weights(s, qb):
                            n, N, b = (s - 1) * 4 + qb, (qb + 1) * P, qb % 2
                            act.wait_ge(s_["d_done"], n + 1)
                            act_e.activation(tA[b][:, :, 0:N], tB[b][:, :, 0:N], ACT.Exp).then_inc(s_["a_done"], 1)

                        def q_out(s, b):
                            act.wait_ge(s_["proj"], s * 3 + 1)
                            if diff:
                                if not isinstance(s, int) or s >= 1:
                                    act.wait_ge(s_["k_ready"], s)
                                act_e.activation(raw, PB[0][:, :], ACT.Copy, scale=0.125).then_inc(s_["q_evac"], 1)
                                return
                            if not isinstance(s, int) or s >= 2:
                                act.wait_ge(s_["z_done"], (s - 1) * 4)
                            for h in range(2):
                                rows = slice(h * H64, (h + 1) * H64)
                                last = act_e.activation(qz[b][rows, h, :], PB[0][rows, :], ACT.Copy, scale=0.125)
                            last.then_inc(s_["q_evac"], 1)

                        def k_out(s, b):
                            act.wait_ge(s_["proj"], s * 3 + 2)
                            if diff:
                                act.wait_ge(s_["q_ready"], s + 1)
                                act_e.activation(raw, PB[1][:, :], ACT.Copy).then_inc(s_["k_evac"], 1)
                                return
                            if not isinstance(s, int) or s >= 2:
                                act.wait_ge(s_["z_done"], (s - 1) * 4)
                            act_e.activation(kT[b], PB[1][:, :], ACT.Copy).then_inc(s_["k_evac"], 1)

                        def v_out(s, b):
                            act.wait_ge(s_["proj"], s * 3 + 3)
                            if not isinstance(s, int) or s >= 1:
                                act.wait_ge(s_["vt_done"], s)
                            act_e.activation(vT, PB[0][:, :], ACT.Copy).then_inc(s_["v_evac"], 1)

                        def v_natural(s, b):
                            act.wait_ge(s_["vt_done"], s)
                            if not isinstance(s, int) or s >= 2:
                                act.wait_ge(s_["pv_done"], s - 1)
                            act_e.activation(vn[b][:, :, :], TR[:, :].rearrange("p (t n) -> p t n", t=TT),
                                             ACT.Copy).then_inc(s_["v_ready"], 1)

                        def a_transposed(s, qb):
                            n = (s - 1) * 4 + qb
                            act.wait_ge(s_["t_done"], n + 1)
                            if qb == 0 and (not isinstance(s, int) or s >= 2):
                                act.wait_ge(s_["pv_done"], s - 1)
                            act_e.activation(aT[0][:, 0:qb + 1, qb * P:(qb + 1) * P],
                                             TR[:, 0:(qb + 1) * P].rearrange("p (k q) -> p k q", q=P),
                                             ACT.Copy).then_inc(s_["tr_evac"], 1)

                        def o_out(s):
                            act.wait_ge(s_["pv_done"], s - 1)
                            if diff:
                                act.wait_ge(s_["o_done"], s - 1)
                                act_e.activation(osb, O[:, :], ACT.Copy)
                                act_e.activation(osq, O[:, :], ACT.Square).then_inc(s_["o_evac"], 1)
                                return
                            act_e.activation(oT[:, bass.ds(s - 2, 1), :].rearrange("p c n -> p (c n)"), O[:, :],
                                             ACT.Copy).then_inc(s_["o_evac"], 1)

                        def o_rstd(s):
                            act.wait_ge(s_["ss_done"], s - 1)
                            act_e.activation(tR, O[:, :], ACT.Ln, scale=1.0 / P, bias=eps).then_inc(s_["rs_done"], 1)
                            act.wait_ge(s_["rs_done"], s - 1)
                            act_e.activation(tR, tR, ACT.Exp, scale=-0.5).then_inc(s_["rstd"], 1)

                        tR = A[:, 24064:24576]

                        def body(s, b, use):
                            proj, attend, weigh = doing(s)
                            if attend and diff:
                                exps(s, 0)
                                exps(s, 1)
                            elif attend:
                                softplus_terms(s, (0, 1))
                            if weigh:
                                o_out(s)
                            if attend:
                                v_natural(s, 1 - b)
                                if not diff:
                                    weights(s, 0)
                                    weights(s, 1)
                            if proj:
                                q_out(s, b)
                            if attend and diff:
                                a_transposed(s, 0)
                            if weigh and diff:
                                o_rstd(s)
                            if attend and diff:
                                exps(s, 2)
                                a_transposed(s, 1)
                                exps(s, 3)
                            if attend and not diff:
                                softplus_terms(s, (2, 3))
                                weights(s, 2)
                            if proj:
                                k_out(s, b)
                            if attend:
                                if diff:
                                    a_transposed(s, 2)
                                else:
                                    weights(s, 3)
                            if proj:
                                v_out(s, b)
                            if attend and diff:
                                a_transposed(s, 3)

                        act.wait_ge(s_win[0], 48)
                        for g in range(3):
                            act_e.activation(w_hi[:, :, g, :], win[0][:, :, g, :],
                                             ACT.Copy).then_inc(s_["w0_high"], 1)
                            for k in range(KC) if g == 0 else ():
                                act_e.activation(h_hi[:, k, :], hT[:, k, :], ACT.Copy).then_inc(s_["h_high"], 1)
                        if diff:
                            act.wait_ge(s_["zero"], 2)
                            act.wait_ge(s_["angles"], 1)
                            act_e.activation(sinT, sinT, ACT.Sin)
                            act_e.activation(cosT, cosT, ACT.Sin).then_inc(s_["tables"], 1)
                        act.wait_ge(s_["zero"], 2)
                        steps(body, act, () if diff else (ch,), () if diff else (16,))

                    @block.vector
                    def _(dve):
                        ch = Chain(dve, s_["dve"])

                        def maxes(s, qb):
                            n, N, b = (s - 1) * 4 + qb, (qb + 1) * P, qb % 2
                            dve.wait_ge(s_["z_done"], n + 1)
                            if not isinstance(n, int) or n >= 2:
                                dve.wait_ge(s_["p_done"], n - 1)
                            vec.reduce_max(nmx[:, b, :], Z[b][:, :, 0:N], AX.X, negate=True).then_inc(s_["nm_done"], 1)

                        def combine(s, qb):
                            n, N, b = (s - 1) * 4 + qb, (qb + 1) * P, qb % 2
                            dve.wait_ge(s_["p_done"], n + 1)
                            ch.link(vec.reciprocal(lrec[:, b, :], lsum[:, b, :]))
                            ch.link(vec.tensor_tensor(lrec[:, b, 1:2], lrec[:, b, 1:2], neglam, ALU.mult))
                            if not isinstance(n, int) or n >= 2:
                                dve.wait_ge(s_["t_done"], n - 1)
                            ch.link(vec.tensor_scalar(tB[b][:, 1, 0:N], tA[b][:, 1, 0:N], lrec[:, b, 1:2], None, ALU.mult))
                            vec.scalar_tensor_tensor(tB[b][:, 0, 0:N], tA[b][:, 0, 0:N], lrec[:, b, 0:1],
                                                     tB[b][:, 1, 0:N], ALU.mult, ALU.add).then_inc(s_["a_done"], 1)

                        def rotate(s, b, g):
                            dve.wait_ge(s_["k_evac"] if g else s_["q_evac"], s + 1)
                            mask = [8 + i for i in range(8)] + list(range(8)) + list(range(16, 32))
                            rc = tB[0][:, 1, :]
                            if not isinstance(s, int) or s >= 1:
                                dve.wait_ge(s_["a_done"], (s - 1) * 4 + 2 + 2 * g)
                            if g:
                                dve.wait_ge(s_["q_ready"], s + 1)
                            vec.tensor_tensor(rc, raw, cosT, ALU.mult)
                            ch.link(vec.stream_shuffle(shf, raw, mask))
                            ch.link(vec.tensor_tensor(shf, shf, sinT, ALU.mult))
                            if not isinstance(s, int) or s >= 2:
                                dve.wait_ge(s_["z_done"], (s - 1) * 4)
                            if g:
                                vec.tensor_tensor(kT[b], rc, shf, ALU.add).then_inc(s_["k_ready"], 1)
                                return
                            for h in range(2):
                                rows = slice(h * H64, (h + 1) * H64)
                                last = vec.tensor_tensor(qz[b][rows, h, :], rc[rows, :], shf[rows, :], ALU.add)
                            last.then_inc(s_["q_ready"], 1)

                        def vector_row(s, extra=0):
                            static = isinstance(s, int)
                            m = s + extra
                            dve.wait_ge(s_["used"], (m + 1) * KC)
                            slot = (G_A, SH_M, None, None, None, None, None, None, SC_M, G_M)[m] if static else s - 2 + NV
                            row = modrow[:, bass.ds(slot, 1), :].rearrange("p v n -> p (v n)")
                            vec.tensor_tensor(row, PB[1][:, 0:QV], row, ALU.add).then_inc(s_["row"], 1)

                        def o_norm(s):
                            dve.wait_ge(s_["rstd"], s - 1)
                            dst = oT[:, bass.ds(s - 2, 1), :].rearrange("p c n -> p (c n)")
                            vec.scalar_tensor_tensor(dst, osb, subg, A[:, 24064:24576], ALU.mult,
                                                     ALU.mult).then_inc(s_["o_done"], 1)

                        def suffix(s, qb):
                            n, N, b = (s - 1) * 4 + qb, (qb + 1) * P, qb % 2
                            dve.wait_ge(s_["sp_done"], n + 1)
                            ch.link(vec.scalar_tensor_tensor(tA[b][:, :, 0:N], Z[b][:, :, 0:N], 0.0, tA[b][:, :, 0:N],
                                                             ALU.max, ALU.add))
                            if not isinstance(n, int) or n >= 2:
                                dve.wait_ge(s_["a_done"], n - 1)
                            for h in range(2):
                                src = tA[b][:, h, 0:N][:, ::-1]
                                last = vec.tensor_tensor_scan(tB[b][:, h, 0:N][:, ::-1], src, src, 0.0, ALU.add, ALU.bypass)
                            ch.link(last)
                            vec.tensor_tensor(tB[b][:, :, 0:N], Z[b][:, :, 0:N], tB[b][:, :, 0:N],
                                              ALU.subtract).then_inc(s_["d_done"], 1)

                        def a_transposed(s, qb):
                            n = (s - 1) * 4 + qb
                            if qb == 0 and (not isinstance(s, int) or s >= 2):
                                dve.wait_ge(s_["pv_done"], s - 1)
                            for h in range(2):
                                dve.wait_ge(s_["t_done"], n * 2 + h + 1)
                                vec.tensor_copy(aT[h][:, 0:qb + 1, qb * P:(qb + 1) * P],
                                                (TR, O)[h][:, 0:(qb + 1) * P].rearrange("p (k q) -> p k q", q=P)
                                                ).then_inc(s_["tr_evac"], 1)

                        def body(s, b, use):
                            proj, attend, weigh = doing(s)
                            if diff:
                                if attend:
                                    maxes(s, 0)
                                    maxes(s, 1)
                                    combine(s, 0)
                                    combine(s, 1)
                                if proj:
                                    rotate(s, b, 0)
                                if attend:
                                    maxes(s, 2)
                                if weigh:
                                    o_norm(s)
                                if attend:
                                    combine(s, 2)
                                    maxes(s, 3)
                                    combine(s, 3)
                                if proj:
                                    rotate(s, b, 1)
                                    vector_row(s)
                                elif attend:
                                    vector_row(s)
                                    vector_row(s, 1)
                            elif attend:
                                suffix(s, 0)
                                suffix(s, 1)
                                a_transposed(s, 0)
                                a_transposed(s, 1)
                                suffix(s, 2)
                                suffix(s, 3)
                                a_transposed(s, 2)
                                a_transposed(s, 3)

                        for g in range(3):
                            dve.wait_ge(s_["w0_high"], g + 1)
                            w = win[0][:, :, g, :]
                            vec.tensor_tensor(w_lo[0][:, :, g, :], w, w_hi[:, :, g, :].bitcast(F32), ALU.subtract).then_inc(s_["w0_low"], 1)
                            for k in range(KC) if g == 0 else ():
                                dve.wait_ge(s_["h_high"], k + 1)
                                vec.tensor_tensor(h_lo[:, k, :], hT[:, k, :], h_hi[:, k, :].bitcast(F32),
                                                  ALU.subtract).then_inc(s_["h_low"], 1)
                        if diff:
                            rope_angles(dve, ch)
                            dve.wait_ge(s_["zero"], 2)
                            dve.wait_ge(s_["tables"], 1)
                            ch.link(vec.tensor_scalar(sinT, sinT, cst[:, C_SGN:C_SGN + 1], None, ALU.mult))
                            ch.link(vec.tensor_scalar(cosT, cosT, cst[:, C_ROT:C_ROT + 1], cst[:, C_PASS:C_PASS + 1],
                                                      ALU.mult, ALU.add))
                        steps(body, dve, (ch,), (32,) if diff else (16,))

        def gate_up_slot(g):
            mem = region if g == 2 else arena[:, g * 12288:(g + 1) * 12288]
            return mem[:, 0:8192].rearrange("p (g k f) -> p g k f", g=2, k=KC)

        def down_slot(b):
            return arena[:, b * 12288 + 8192:(b + 1) * 12288].rearrange("p (c d) -> p c d", c=FC)

        def load_gate_up(sp, L, e, g, s_landed):
            for n, w in enumerate((w_gate, w_up)):
                src = w[L][bass.ds(e, 1), :, :].rearrange("e (k p) f -> p (e k) f", p=P)
                sp.dma_start(gate_up_slot(g)[:, n, :, :], src).then_inc(s_landed, 16)

        def load_down(sp, L, e, b, s_landed):
            src = w_down[L][bass.ds(e, 1), :, :].rearrange("e (k p) f -> p (e k) f", p=P)
            sp.dma_start(down_slot(b)[:, :, :], src).then_inc(s_landed, 16)

        def out_projection(tag, L, s_gu, s_dn):
            oT = region[:, 0:4096].rearrange("p (k n) -> p k n", k=KC)
            wo = region[:, 4096:12288].rearrange("p (k n) -> p k n", k=KC)
            xn = modrow[:, L * NV:L * NV + 4, :].rearrange("p v n -> p (v n)")
            part_ss = small[:, 28:36]
            with ExitStack() as ph:
                ps = [bank(f"{tag}_ps{i}", [P, S], ph) for i in range(4)]
                psT = [bank(f"{tag}_psT{i}", [P, KC, P], ph) for i in range(2)]
                ps_gate = psT[0][:, :, :].rearrange("p k n -> p (k n)").rearrange("p (j n) -> p j n", j=4)
                ps_cols = psT[1][:, 0:4, :].rearrange("p (v i) n -> p v i n", v=2)
                s_mm, s_g, s_x, s_bc, s_gbc, s_ct, s_cols, s_ss, s_rs, s_xn, s_tr, s_ea, s_ed, s_ch, s_rec = (
                    sem(f"{tag}_{n}") for n in ("mm", "gated", "x", "gate_mm", "gate", "cols_T", "cols", "sumsq", "rstd",
                                                "xn", "transposed", "evac_act", "evac_dve", "dve", "reciprocal"))
                halves = [(t, h) for t in range(TT) for h in range(2)]
                with nc.Block() as block:
                    @block.sync
                    def _(sp):
                        for b in range(2):
                            load_gate_up(sp, L, b, b, s_gu[b])
                            load_down(sp, L, b, b, s_dn[b])
                        sp.wait_ge(s_mm, len(halves))
                        load_gate_up(sp, L, 2, 2, s_gu[2])

                    @block.tensor
                    def _(pe):
                        broadcast_on_pe(ps_gate, L, G_A).then_inc(s_bc, 1)
                        columns_on_pe(ps_cols, L, (SH_M, SC_M)).then_inc(s_ct, 1)

                        def transposes(t):
                            pe.wait_ge(s_xn, t + 1)
                            if t == 0:
                                pe.wait_ge(s_gbc, 1)
                            if t == 1:
                                pe.wait_ge(s_cols, 1)
                            if t >= 2:
                                pe.wait_ge(s_ea, t - 1)
                                pe.wait_ge(s_ed, t - 1)
                            for k in range(KC):
                                last = pe_e.transpose(psT[t % 2][:, k, :], xn[:, k * P:(k + 1) * P], ident)
                            last.then_inc(s_tr, 1)

                        for n, (t, h) in enumerate(halves):
                            if n >= 4:
                                pe.wait_ge(s_x, n - 3)
                            for k in range(KC):
                                last = pe_e.matmul(ps[n % 4][:, :], oT[:, k, t * P:(t + 1) * P],
                                                   wo[:, k, h * S:(h + 1) * S], start=(k == 0), stop=(k == KC - 1))
                            last.then_inc(s_mm, 1)
                            if h == 1 and t >= 1:
                                transposes(t - 1)
                        transposes(TT - 1)

                    @block.scalar
                    def _(act):
                        ch = Chain(act, s_ss)

                        def stats(t):
                            for h in range(2):
                                act.wait_ge(s_x, 2 * t + h + 1)
                                ch.link(act_e.activation(xrow[:, :], x[:, t, h * S:(h + 1) * S], ACT.Square,
                                                         accum_out=part_ss[:, 2 * t + h:2 * t + h + 1]))
                            ch.link(act_e.activation(ss[:, t:t + 1], part_ss[:, 2 * t:2 * t + 1], ACT.Identity,
                                                     bias=part_ss[:, 2 * t + 1:2 * t + 2]))
                            act_e.activation(ss[:, t:t + 1], ss[:, t:t + 1], ACT.Sqrt, scale=1.0 / D, bias=eps).then_inc(s_rs, 1)

                        def scaled_out(t):
                            act.wait_ge(s_tr, t + 1)
                            act.wait_ge(s_cols, 1)
                            for k in range(KC // 2):
                                last = act_e.activation(hT[:, k, t * P:(t + 1) * P], psT[t % 2][:, k, :], ACT.Identity,
                                                        scale=modvec(L, SC_M)[:, k:k + 1], bias=modvec(L, SH_M)[:, k:k + 1])
                            last.then_inc(s_ea, 1)

                        for t in range(TT):
                            stats(t)
                            if t >= 1:
                                scaled_out(t - 1)
                        scaled_out(TT - 1)

                    @block.vector
                    def _(dve):
                        dve.wait_ge(s_bc, 1)
                        vec.tensor_copy(gbc[:, :].rearrange("p (j n) -> p j n", j=4), ps_gate).then_inc(s_gbc, 1)
                        dve.wait_ge(s_ct, 1)
                        columns_out(Chain(dve, s_ch), ps_cols, L, (SH_M, SC_M))
                        dve.sem_inc(s_cols, 1)
                        dve.wait_ge(s_gbc, 1)

                        def scaled_out(t):
                            dve.wait_ge(s_tr, t + 1)
                            for k in range(KC // 2, KC):
                                last = vec.tensor_scalar(hT[:, k, t * P:(t + 1) * P], psT[t % 2][:, k, :],
                                                         modvec(L, SC_M)[:, k:k + 1], modvec(L, SH_M)[:, k:k + 1],
                                                         ALU.mult, ALU.add)
                            last.then_inc(s_ed, 1)

                        for n, (t, h) in enumerate(halves):
                            dve.wait_ge(s_mm, n + 1)
                            vec.tensor_tensor(ps[n % 4][:, :], ps[n % 4][:, :], gbc[:, h * S:(h + 1) * S],
                                              ALU.mult).then_inc(s_g, 1)
                            dve.wait_ge(s_g, n + 1)
                            xs = x[:, t, h * S:(h + 1) * S]
                            vec.tensor_tensor(xs, xs, ps[n % 4][:, :], ALU.add).then_inc(s_x, 1)
                            if h == 1:
                                if t >= 1:
                                    scaled_out(t - 1)
                                dve.wait_ge(s_rs, t + 1)
                                vec.reciprocal(rstd[:, t:t + 1], ss[:, t:t + 1]).then_inc(s_rec, 1)
                                dve.wait_ge(s_rec, t + 1)
                                vec.tensor_scalar(xn, x[:, t, :], rstd[:, t:t + 1], None, ALU.mult).then_inc(s_xn, 1)
                        scaled_out(TT - 1)

        late = region[:, 10752:12288]
        LW = {w: late[:, i * 128:(i + 1) * 128] for i, w in enumerate(("scores", "first", "second", "rank", "tmp", "row", "add"))}
        LT = {w: v.rearrange("p (t e) -> p t e", t=TT) for w, v in LW.items()}
        late_v4 = [late[:, 896 + i * 4:900 + i * 4] for i in range(5)]
        fl, pre, cf = (late[:, 928 + i * 96:1024 + i * 96] for i in range(3))
        cnt = late[:, 1216:1248]
        ovf = late[0:1, 1248:1264].rearrange("p (a b) -> p a b", a=2)

        def gate_weights(ch):
            for n, choice in enumerate(("first", "second")):
                ch.link(vec.tensor_tensor(LT["tmp"], LT[choice], LT["scores"], ALU.mult))
                ch.link(vec.tensor_reduce(late_v4[n], LT["tmp"], AX.X, ALU.add))
            ch.link(vec.tensor_tensor(late_v4[2], late_v4[0], late_v4[1], ALU.add))
            ch.link(vec.reciprocal(late_v4[2], late_v4[2]))
            for n in range(2):
                ch.link(vec.tensor_tensor(gates[:, n, :], late_v4[n], late_v4[2], ALU.mult))
            for b in range(NB):
                ch.link(vec.tensor_scalar(fl[:, b * E:(b + 1) * E], cnt, float(P * (b + 1)), None, ALU.is_gt))
            ch.link(vec.tensor_tensor_scan(pre, fl, fl, 0.0, ALU.add, ALU.bypass))

        def buffer_rows(ch):
            for b in range(NB):
                ch.link(vec.tensor_scalar(cf[:, b * E:(b + 1) * E], pre[:, b * E:(b + 1) * E], float(P),
                                          float((E - 1) * P - (b + 1) * P), ALU.mult, ALU.add))
            for b in reversed(range(NB)):
                below = cf[:, (b - 1) * E:b * E] if b else cst[:, C_E:C_E + E]
                ch.link(vec.tensor_tensor(cf[:, b * E:(b + 1) * E], cf[:, b * E:(b + 1) * E], below, ALU.subtract))
            ch.link(vec.tensor_tensor(LT["row"], LT["rank"], cst[:, C_E:C_E + E].unsqueeze(1).to_broadcast([P, TT, E]),
                                      ALU.add))
            for b in range(NB):
                ch.link(vec.tensor_scalar(LT["add"], LT["rank"], float(P * (b + 1)), None, ALU.is_ge))
                ch.link(vec.tensor_tensor(LT["add"], LT["add"], cf[:, b * E:(b + 1) * E].unsqueeze(1)
                                          .to_broadcast([P, TT, E]), ALU.mult))
                ch.link(vec.tensor_tensor(LT["row"], LT["row"], LT["add"], ALU.add))
            for n, choice in enumerate(("first", "second")):
                ch.link(vec.tensor_tensor(LT["tmp"], LT[choice], LT["row"], ALU.mult))
                ch.link(vec.tensor_reduce(late_v4[3 + n], LT["tmp"], AX.X, ALU.add))
                ch.link(vec.tensor_copy(slots[:, n, :], late_v4[3 + n]))

        def later_blocks(ch, L):
            n = NB * E
            ov = [m[0:1, 0:NOV * n].rearrange("p (j n) -> p j n", j=NOV)
                  for m in (modrow[:, L * NV:L * NV + G_M, :].rearrange("p v n -> p (v n)"), late)]

            def row(a):
                return a.unsqueeze(1).to_broadcast([1, NOV, n])
            ch.link(vec.tensor_tensor(ov[0], row(pre[0:1, :]), cst[0:1, C_OVJ:C_OVJ + NOV].unsqueeze(2)
                                      .to_broadcast([1, NOV, n]), ALU.is_equal))
            ch.link(vec.tensor_tensor(ov[0], ov[0], row(fl[0:1, :]), ALU.mult))
            for i, col in enumerate((C_OVE, C_OVB)):
                ch.link(vec.tensor_tensor(ov[1], ov[0], row(cst[0:1, col:col + n]), ALU.mult))
                ch.link(vec.tensor_reduce(ovf[:, i, 0:NOV], ov[1], AX.X, ALU.add))
                ch.link(vec.tensor_copy(ovf[:, i, NOV:NOV + 1], pre[0:1, n - 1:n]))
            ch.link(vec.tensor_copy(overs[:, :, :], ovf))

        def router(tag):
            R = region[:, 8192:10752]
            W = [LW["scores"], R[:, 0:128], LW["first"], LW["second"], LW["tmp"], R[:, 128:256], LW["rank"]]

            def tile(i):
                return W[i].rearrange("p (t e) -> p t e", t=TT)

            part = R[:, 256:768]
            maskb = R[:, 768:832].bitcast(BF16).rearrange("p (t e) -> p t e", t=TT)
            m8 = R[:, 832:960].rearrange("p (g n) -> p g n", n=EG)
            v16 = [R[:, 960 + i * 16:976 + i * 16] for i in range(4)]
            v4 = [R[:, 1024 + i * 4:1028 + i * 4] for i in range(5)]
            with ExitStack() as ph:
                psP, psL, psR, psC = (bank(f"{tag}_ps{i}", [P, S], ph) for i in range(4))
                s_lp, s_part, s_lg, s_exp, s_mx, s_mask, s_pos, s_ch = (sem(f"{tag}_{n}") for n in (
                    "partial", "part_out", "logits", "exp", "max", "mask", "pos", "dve"))
                with nc.Block() as block:
                    @block.tensor
                    def _(pe):
                        for r in range(2):
                            for j in range(4):
                                k = 2 * j + r
                                last = pe_e.matmul(psP[32 * j:32 * j + 32, :], wrt[:, k, :], hT[:, k, :],
                                                   start=(r == 0), stop=(r == 1))
                        last.then_inc(s_lp, 1)
                        pe.wait_ge(s_part, 1)
                        for t in range(TT):
                            last = pe_e.matmul(psL[:, t * E:(t + 1) * E], part[:, t * P:(t + 1) * P],
                                               cst[:, C_FOLD:C_FOLD + E], start=True, stop=True)
                        last.then_inc(s_lg, 1)
                        pe.wait_ge(s_mask, 1)
                        for t in range(TT):
                            for u in range(t + 1):
                                pe_e.matmul(psR[:, t * E:(t + 1) * E], trib if u == t else onesb, maskb[:, u, :],
                                            start=(u == 0), stop=(u == t))
                        for u in range(TT):
                            last = pe_e.matmul(psC[:, 0:E], onesb, maskb[:, u, :], start=(u == 0), stop=(u == TT - 1))
                        last.then_inc(s_pos, 1)

                    @block.scalar
                    def _(act):
                        act.wait_ge(s_lp, 1)
                        act_e.activation(part, psP[:, :], ACT.Copy).then_inc(s_part, 1)
                        act.wait_ge(s_mx, 1)
                        act_e.activation(W[0], W[0], ACT.Exp).then_inc(s_exp, 1)

                    @block.vector
                    def _(dve):
                        ch = Chain(dve, s_ch)

                        def per_tile(v):
                            return v.unsqueeze(2).to_broadcast([P, TT, E])

                        dve.wait_ge(s_lg, 1)
                        ch.link(vec.tensor_copy(tile(1), psL[:, 0:TT * E].rearrange("p (t e) -> p t e", t=TT)))
                        ch.link(vec.reduce_max(v4[0], tile(1), AX.X))
                        vec.tensor_tensor(tile(0), tile(1), per_tile(v4[0]), ALU.subtract).then_inc(s_mx, 1)
                        dve.wait_ge(s_exp, 1)
                        ch.link(vec.tensor_reduce(v4[1], tile(0), AX.X, ALU.add))
                        ch.link(vec.reciprocal(v4[1], v4[1]))
                        ch.link(vec.tensor_tensor(tile(0), tile(0), per_tile(v4[1]), ALU.mult))
                        ch.link(vec.tensor_tensor(tile(1), tile(0), brt[:, :].unsqueeze(1).to_broadcast([P, TT, E]), ALU.add))
                        sel = W[1].rearrange("p (g n) -> p g n", n=EG)
                        for g in range(TT * NG):
                            last = vec.max(m8[:, g, :], sel[:, g, :])
                        ch.link(last)
                        ch.link(vec.tensor_tensor(v16[0], m8[:, :, 0:1].rearrange("p g o -> p (g o)"),
                                                  m8[:, :, 1:2].rearrange("p g o -> p (g o)"), ALU.add))

                        def first_largest(dst, src, rev, n, a, v):
                            def b(c):
                                return c.unsqueeze(2).to_broadcast([P, TT, n])
                            ch.link(vec.reduce_max(v, src, AX.X))
                            ch.link(vec.tensor_tensor(a, src, b(v), ALU.is_equal))
                            ch.link(vec.tensor_tensor(a, a, rev.unsqueeze(1).to_broadcast([P, TT, n]), ALU.mult))
                            ch.link(vec.reduce_max(v, a, AX.X))
                            ch.link(vec.tensor_tensor(dst, a, b(v), ALU.is_equal))

                        g4 = [v.rearrange("p (t g) -> p t g", t=TT) for v in v16]
                        first_largest(g4[1], g4[0], cst[:, C_GRV:C_GRV + NG], NG, g4[2], v4[2])
                        ch.link(vec.tensor_tensor(W[1].rearrange("p (g n) -> p g n", n=EG), sel,
                                                  v16[1].unsqueeze(2).to_broadcast([P, TT * NG, EG]), ALU.mult))
                        ch.link(vec.tensor_scalar(v16[3], v16[1], BIG, -BIG, ALU.mult, ALU.add))
                        ch.link(vec.tensor_tensor(W[1].rearrange("p (g n) -> p g n", n=EG), sel,
                                                  v16[3].unsqueeze(2).to_broadcast([P, TT * NG, EG]), ALU.add))
                        rev = cst[:, C_REV:C_REV + E]
                        first_largest(tile(2), tile(1), rev, E, tile(4), v4[3])
                        ch.link(vec.scalar_tensor_tensor(W[1], W[2], -3 * BIG, W[1], ALU.mult, ALU.add))
                        first_largest(tile(3), tile(1), rev, E, tile(4), v4[4])
                        vec.tensor_tensor(maskb[:, :, :], tile(2), tile(3), ALU.add).then_inc(s_mask, 1)
                        ch.link(vec.tensor_tensor(W[5], W[2], W[3], ALU.add))
                        ch.link(vec.tensor_scalar(W[5], W[5], -10000.0, 10000.0, ALU.mult, ALU.add))
                        dve.wait_ge(s_pos, 1)
                        ch.link(vec.tensor_copy(W[6], psR[:, 0:TT * E]))
                        ch.link(vec.tensor_tensor(posm[:, :, :], tile(6), tile(5), ALU.add))
                        ch.link(vec.tensor_copy(counts[:, :], psC[0:1, 0:E]))
                        ch.link(vec.tensor_copy(cnt, psC[:, 0:E]))

        def experts(tag, L, s_gu, s_dn):
            R, T = region[:, 8192:10752], hT[:, :, :].rearrange("p a b -> p (a b)")
            xg = [T[:, i * 1024:(i + 1) * 1024].rearrange("p (k n) -> p k n", k=KC) for i in range(2)]
            ysb = [T[:, 2048 + i * 1024:3072 + i * 1024] for i in range(2)]
            Ssel = [R[:, i * 512:(i + 1) * 512].rearrange("p (t n) -> p t n", t=TT) for i in range(2)]
            hs, hid, hidT = (R[:, 1024 + i * 512:1536 + i * 512] for i in range(3))
            gs, sh = modvec(L, SC_M), modvec(L, SH_M)
            shifted = small[:, 24:28]
            with ExitStack() as ph:
                GX = bank(tag + "_GX", [P, KC, P], ph)
                G, U, TR = (bank(f"{tag}_{n}", [P, S], ph) for n in ("G", "U", "TR"))
                Y = bank(tag + "_Y", [P, 2, S], ph)
                XR = bank(tag + "_XR", [P, S], ph)
                s_ = {n: sem(f"{tag}_{n}") for n in ("sel rows xr gx xg gu hs hid tr hidT dn y overs late "
                                                       "osel ogx oxg ogu ohs ohid otr ohidT odn oy ow odone ostored onext dve").split()}
                s_y = [sem(f"{tag}_yw{i}") for i in range(2)]

                def select(b, ranks):
                    for t in range(TT):
                        last = vec.tensor_scalar(Ssel[b][:, t, :], cst[:, C_IOTA:C_IOTA + P], ranks(t), rstd[:, t:t + 1],
                                                 ALU.is_equal, ALU.mult)
                    return last

                def gather(b):
                    for k in range(KC):
                        for t in range(TT):
                            last = pe_e.matmul(GX[:, k, :], x[:, t, k * P:(k + 1) * P], Ssel[b][:, t, :],
                                               start=(t == 0), stop=(t == TT - 1))
                    return last

                def gather_rows(b, n):
                    w = D * n // P
                    for t in range(TT):
                        for j in range(P // n):
                            last = pe_e.matmul(XR[j * n:(j + 1) * n, 0:w], Ssel[b][:, t, 0:n], x[:, t, j * w:(j + 1) * w],
                                               start=(t == 0), stop=(t == TT - 1))
                    return last

                def row_transposes(n):
                    for c in range(n * KC // P):
                        last = pe_e.transpose(GX[:, c, :], xrow[:, c * P:(c + 1) * P], ident)
                    return last

                def modulate(b, n):
                    per = n * KC // P
                    for k in range(KC):
                        src = GX[:, k % per, k // per * n:(k // per + 1) * n]
                        last = vec.tensor_scalar(xg[b][:, k, 0:n], src, gs[:, k:k + 1], sh[:, k:k + 1],
                                                 ALU.mult, ALU.add)
                    return last

                def gate_up_small(g, xb):
                    gu = gate_up_slot(g)
                    for k in range(KC):
                        for h in range(2):
                            last = pe_e.matmul(G[h * H64:(h + 1) * H64, :].rearrange("p (g f) -> p g f", g=2),
                                               xg[xb][:, k, 0:H64], gu[:, :, k, h * (F // 2):(h + 1) * (F // 2)],
                                               start=(k == 0), stop=(k == KC - 1))
                    return last

                def gate_up_tiny(g, xb):
                    gu = gate_up_slot(g)
                    for k in range(KC):
                        for j in range(4):
                            last = pe_e.matmul(G[j * H32:(j + 1) * H32, 0:F // 2].rearrange("p (g f) -> p g f", g=2),
                                               xg[xb][:, k, 0:H32], gu[:, :, k, j * P:(j + 1) * P],
                                               start=(k == 0), stop=(k == KC - 1))
                    return last

                def gate_up_full(g, xb):
                    gu = gate_up_slot(g)
                    for w, ps in enumerate((G, U)):
                        for k in range(KC):
                            last = pe_e.matmul(ps[:, :], xg[xb][:, k, :], gu[:, w, k, :], start=(k == 0), stop=(k == KC - 1))
                    return last

                def hidden_transposes(n):
                    for c in range(n):
                        last = pe_e.transpose(TR[:, c * P:(c + 1) * P], hid[:, c * P:(c + 1) * P], ident)
                    return last

                def down_small(b):
                    dn = down_slot(b)
                    for f in range(FC):
                        lhsT = hidT[:, (f % 2) * P + (f // 2) * H64:(f % 2) * P + (f // 2) * H64 + H64]
                        for h in range(2):
                            last = pe_e.matmul(Y[h * H64:(h + 1) * H64, 0, :], lhsT, dn[:, f, h * S:(h + 1) * S],
                                               start=(f == 0), stop=(f == FC - 1))
                    return last

                def down_tiny(b):
                    dn = down_slot(b)
                    for f in range(FC):
                        for j in range(4):
                            last = pe_e.matmul(Y[j * H32:(j + 1) * H32, 0, 0:QV], hidT[:, f * H32:(f + 1) * H32],
                                               dn[:, f, j * QV:(j + 1) * QV], start=(f == 0), stop=(f == FC - 1))
                    return last

                def down_full(b):
                    dn = down_slot(b)
                    for h in range(2):
                        for f in range(FC):
                            last = pe_e.matmul(Y[:, h, :], hidT[:, f * P:(f + 1) * P], dn[:, f, h * S:(h + 1) * S],
                                               start=(f == 0), stop=(f == FC - 1))
                    return last

                def experts_loop(eng, body):
                    for e in range(2):
                        body(e, e, 0, e, 0)
                    turns = (E - 3) // 6
                    with eng.Fori(0, turns) as i:
                        for r in range(2, 8):
                            body(i * 6 + r, r % 2, i * 3 + r // 2, r % 3, i * 2 + r // 3)
                    for e in range(2 + 6 * turns, E):
                        body(e, e % 2, e // 2, e % 3, e // 3)

                def since(e, n=1):
                    return not isinstance(e, int) or e >= n

                def one_of(eng, c, waits, full, small, tiny):
                    def form(run):
                        for s, v in waits:
                            eng.wait_ge(s, v)
                        run()

                    with eng.If(c > H32):
                        with eng.If(c > H64):
                            form(full)
                        with eng.Else():
                            form(small)
                    with eng.Else():
                        form(tiny)

                def count_of(eng, e):
                    return eng.value_load(counts[0:1, bass.ds(e, 1)], min_val=0, max_val=S)

                def tail(eng, body):
                    eng.wait_ge(s_["overs"], 1)
                    n = eng.value_load(overs[0:1, 0, NOV:NOV + 1], min_val=0, max_val=NOV)
                    with eng.If(n > 0):
                        with eng.Fori(0, NOV) as j:
                            with eng.If(j < n):
                                e = eng.value_load(overs[0:1, 0, bass.ds(j, 1)], min_val=0, max_val=E - 1)
                                k = eng.value_load(overs[0:1, 1, bass.ds(j, 1)], min_val=0, max_val=NB)
                                body(j, e, k)
                            with eng.Else():
                                pass
                    with eng.Else():
                        pass

                with nc.Block() as block:
                    @block.sync
                    def _(sp):
                        def store(e, b, groups):
                            n, per = P // groups, 4 // groups
                            for q in range(4):
                                src = ysb[b][q // per * n:(q // per + 1) * n, q % per * QV:(q % per + 1) * QV]
                                sp.dma_start(ybuf[bass.ds(e * P, n), q * QV:(q + 1) * QV], src).then_inc(s_y[b], 16)

                        def body(e, b, use, g, guse):
                            if not isinstance(e, int) or e + 3 < E:
                                sp.wait_ge(s_["gu"], e + 1)
                                load_gate_up(sp, L, e + 3, g, s_gu[g])
                            if not isinstance(e, int) or e + 2 < E:
                                sp.wait_ge(s_["dn"], e + 1)
                                load_down(sp, L, e + 2, b, s_dn[b])
                            one_of(sp, count_of(sp, e), [(s_["y"], e + 1)],
                                   lambda: store(e, b, 1), lambda: store(e, b, 2), lambda: store(e, b, 4))

                        experts_loop(sp, body)
                        for b in range(2):
                            sp.wait_ge(s_y[b], 32 * E)

                        def extra(j, e, k):
                            load_gate_up(sp, L, e, 0, s_["ow"])
                            load_down(sp, L, e, 0, s_["ow"])
                            sp.wait_ge(s_["oy"], j + 1)
                            sp.dma_start(ybuf[bass.ds(j * P + E * P, P), :], ysb[0]).then_inc(s_["odone"], 16)
                            sp.wait_ge(s_["odone"], j * 16 + 16)
                            sp.sem_inc(s_["ostored"], 1)

                        tail(sp, extra)

                    @block.tensor
                    def _(pe):
                        def gathering(e, c, b):
                            one_of(pe, c, [(s_["sel"], e + 1)] + [(s_["xg"], e)] * since(e),
                                   lambda: gather(b).then_inc(s_["rows"], 1),
                                   lambda: gather_rows(b, H64).then_inc(s_["rows"], 1),
                                   lambda: gather_rows(b, H32).then_inc(s_["rows"], 1))

                        def turning(e, c):
                            one_of(pe, c, [(s_["xr"], e + 1)],
                                   lambda: pe.sem_inc(s_["gx"], 1),
                                   lambda: row_transposes(H64).then_inc(s_["gx"], 1),
                                   lambda: row_transposes(H32).then_inc(s_["gx"], 1))

                        def body(e, b, use, g, guse):
                            last = isinstance(e, int) and e == E - 1
                            c = count_of(pe, e)
                            one_of(pe, c, [(s_gu[g], guse * 32 + 32), (s_["xg"], e + 1)] + [(s_["hid"], e)] * since(e),
                                   lambda: gate_up_full(g, b).then_inc(s_["gu"], 1),
                                   lambda: gate_up_small(g, b).then_inc(s_["gu"], 1),
                                   lambda: gate_up_tiny(g, b).then_inc(s_["gu"], 1))
                            if not last:
                                cn = count_of(pe, e + 1)
                                gathering(e + 1, cn, 1 - b)
                            one_of(pe, c, [(s_["hid"], e + 1)] + [(s_["hidT"], e)] * since(e),
                                   lambda: hidden_transposes(FC).then_inc(s_["tr"], 1),
                                   lambda: hidden_transposes(2).then_inc(s_["tr"], 1),
                                   lambda: hidden_transposes(1).then_inc(s_["tr"], 1))
                            if not last:
                                turning(e + 1, cn)
                            one_of(pe, c, [(s_dn[b], use * 16 + 16), (s_["hidT"], e + 1)] + [(s_["y"], e)] * since(e),
                                   lambda: down_full(b).then_inc(s_["dn"], 1),
                                   lambda: down_small(b).then_inc(s_["dn"], 1),
                                   lambda: down_tiny(b).then_inc(s_["dn"], 1))

                        c0 = count_of(pe, 0)
                        gathering(0, c0, 0)
                        turning(0, c0)
                        experts_loop(pe, body)

                        def extra(j, e, k):
                            pe.wait_ge(s_["osel"], j + 1)
                            gather(0).then_inc(s_["ogx"], 1)
                            pe.wait_ge(s_["ow"], j * 48 + 48)
                            pe.wait_ge(s_["oxg"], j + 1)
                            gate_up_full(0, 0).then_inc(s_["ogu"], 1)
                            pe.wait_ge(s_["ohid"], j + 1)
                            hidden_transposes(FC).then_inc(s_["otr"], 1)
                            pe.wait_ge(s_["ohidT"], j + 1)
                            down_full(0).then_inc(s_["odn"], 1)

                        tail(pe, extra)

                    @block.scalar
                    def _(act):
                        def rows_out(e, c):
                            one_of(act, c, [(s_["rows"], e + 1)] + [(s_["gx"], e)] * since(e),
                                   lambda: act.sem_inc(s_["xr"], 1),
                                   lambda: act_e.activation(xrow[:, :], XR[:, :], ACT.Copy).then_inc(s_["xr"], 1),
                                   lambda: act_e.activation(xrow[:, 0:QV], XR[:, 0:QV], ACT.Copy).then_inc(s_["xr"], 1))

                        def body(e, b, use, g, guse):
                            c = count_of(act, e)
                            one_of(act, c, [(s_["gu"], e + 1)] + [(s_["hid"], e)] * since(e),
                                   lambda: act_e.activation(hs[:, :], G[:, :], ACT.Silu).then_inc(s_["hs"], 1),
                                   lambda: act_e.activation(hs[:, 0:F // 2], G[:, 0:F // 2], ACT.Silu).then_inc(s_["hs"], 1),
                                   lambda: act_e.activation(hs[:, 0:P], G[:, 0:P], ACT.Silu).then_inc(s_["hs"], 1))
                            if not (isinstance(e, int) and e == E - 1):
                                rows_out(e + 1, count_of(act, e + 1))
                            one_of(act, c, [(s_["tr"], e + 1)] + [(s_["dn"], e)] * since(e),
                                   lambda: act_e.activation(hidT[:, :], TR[:, :], ACT.Copy).then_inc(s_["hidT"], 1),
                                   lambda: act_e.activation(hidT[:, 0:2 * P], TR[:, 0:2 * P], ACT.Copy).then_inc(s_["hidT"], 1),
                                   lambda: act_e.activation(hidT[:, 0:P], TR[:, 0:P], ACT.Copy).then_inc(s_["hidT"], 1))
                            both = Y[:, :, :].rearrange("p a b -> p (a b)")
                            one_of(act, c, [(s_["dn"], e + 1)] + [(s_y[b], use * 64)] * since(e, 2),
                                   lambda: act_e.activation(ysb[b], both, ACT.Copy).then_inc(s_["y"], 1),
                                   lambda: act_e.activation(ysb[b][:, 0:S], Y[:, 0, :], ACT.Copy).then_inc(s_["y"], 1),
                                   lambda: act_e.activation(ysb[b][:, 0:QV], Y[:, 0, 0:QV], ACT.Copy).then_inc(s_["y"], 1))

                        rows_out(0, count_of(act, 0))
                        experts_loop(act, body)

                        def extra(j, e, k):
                            act.wait_ge(s_["ogu"], j + 1)
                            act_e.activation(hs[:, :], G[:, :], ACT.Silu).then_inc(s_["ohs"], 1)
                            act.wait_ge(s_["otr"], j + 1)
                            act_e.activation(hidT[:, :], TR[:, :], ACT.Copy).then_inc(s_["ohidT"], 1)
                            act.wait_ge(s_["odn"], j + 1)
                            for b in range(2):
                                act.wait_ge(s_y[b], 32 * E)
                            act_e.activation(ysb[0], Y[:, :, :].rearrange("p a b -> p (a b)"), ACT.Copy).then_inc(s_["oy"], 1)

                        tail(act, extra)

                    @block.vector
                    def _(dve):
                        ch = Chain(dve, s_["late"])

                        def selecting(e, b):
                            if since(e, 2):
                                dve.wait_ge(s_["gx"], e - 1)
                            select(b, lambda t: posm[:, t, bass.ds(e, 1)]).then_inc(s_["sel"], 1)

                        def modulating(e, b):
                            waits = [(s_["gx"], e + 1)] + [(s_["gu"], e - 1)] * since(e, 2)
                            one_of(dve, count_of(dve, e), waits,
                                   lambda: modulate(b, P).then_inc(s_["xg"], 1),
                                   lambda: modulate(b, H64).then_inc(s_["xg"], 1),
                                   lambda: modulate(b, H32).then_inc(s_["xg"], 1))

                        def body(e, b, use, g, guse):
                            last = isinstance(e, int) and e == E - 1
                            c = count_of(dve, e)
                            if not last:
                                selecting(e + 1, 1 - b)
                            one_of(dve, c, [(s_["hs"], e + 1)] + [(s_["tr"], e)] * since(e),
                                   lambda: vec.tensor_tensor(hid[:, :], U[:, :], hs[:, :], ALU.mult).then_inc(s_["hid"], 1),
                                   lambda: vec.tensor_tensor(hid[:, 0:F // 2], G[:, F // 2:F], hs[:, 0:F // 2],
                                                             ALU.mult).then_inc(s_["hid"], 1),
                                   lambda: vec.tensor_tensor(hid[:, 0:P], G[:, P:2 * P], hs[:, 0:P],
                                                             ALU.mult).then_inc(s_["hid"], 1))
                            if not last:
                                modulating(e + 1, 1 - b)
                            if isinstance(e, int) and e == 0:
                                gate_weights(ch)
                            if isinstance(e, int) and e == 1:
                                buffer_rows(ch)
                            if isinstance(e, int) and e == E - 6:
                                later_blocks(ch, L)
                                dve.sem_inc(s_["overs"], 1)

                        selecting(0, 0)
                        modulating(0, 0)
                        experts_loop(dve, body)

                        def extra(j, e, k):
                            dve.wait_ge(s_["gx"], E)
                            off = cst[:, bass.ds(k + C_128B, 1)]
                            vec.tensor_tensor(shifted, posm[:, :, bass.ds(e, 1)].rearrange("p t o -> p (t o)"),
                                              off.to_broadcast([P, TT]), ALU.subtract).then_inc(s_["dve"], 1)
                            dve.wait_ge(s_["dve"], j * 1 + 1)
                            select(0, lambda t: shifted[:, t:t + 1]).then_inc(s_["osel"], 1)
                            dve.wait_ge(s_["ogx"], j + 1)
                            modulate(0, P).then_inc(s_["oxg"], 1)
                            dve.wait_ge(s_["ohs"], j + 1)
                            vec.tensor_tensor(hid[:, :], U[:, :], hs[:, :], ALU.mult).then_inc(s_["ohid"], 1)
                            dve.wait_ge(s_["odn"], j + 1)
                            dve.sem_inc(s_["onext"], 1)

                        dve.wait_ge(s_["dn"], E)
                        tail(dve, extra)

        def combine(tag, L):
            final = L == DEPTH - 1
            A = arena
            yt = [A[:, 6144 + i * D:6144 + (i + 1) * D] for i in range(8)]
            tmp = [A[:, 14336 + i * D:14336 + (i + 1) * D] for i in range(2)]
            xn = [A[:, 16384 + i * D:16384 + (i + 1) * D] for i in range(2)]
            junk, gf = A[:, 18432:19456], A[:, 19456:20480]
            with ExitStack() as ph:
                ps_gate = bank(tag + "_psG", [P, 4, QV], ph)
                ps_cols = bank(tag + "_psC", [P, 2, 2, P], ph)
                psT = [bank(f"{tag}_psT{i}", [P, KC, P], ph) for i in range(2)]
                s_yg = [sem(f"{tag}_y{i}") for i in range(8)]
                s_a, s_b, s_c, s_x, s_bc, s_gbc, s_ct, s_cols, s_ss, s_rs, s_xn, s_tr, s_ea, s_ed, s_ch, s_gf, s_out, s_rec = (
                    sem(f"{tag}_{n}") for n in ("first", "sum", "gated", "x", "gate_mm", "gate", "cols_T", "cols", "sumsq",
                                                "rstd", "xn", "transposed", "evac_act", "evac_dve", "dve", "final_g", "stored",
                                                "reciprocal"))
                with nc.Block() as block:
                    @block.sync
                    def _(sp):
                        if not final:
                            sp.wait_ge(s_yg[2 * TT - 1], 16)
                            load_first_w_in(sp, L + 1)
                            return
                        sp.dma_start(gf, final_g.partition_broadcast(P)).then_inc(s_gf, 16)
                        for t in range(TT):
                            sp.wait_ge(s_xn, t + 1)
                            sp.dma_start(out[0].rearrange("(t p) d -> t p d", p=P)[t], x[:, t, :]).then_inc(s_out, 16)
                        sp.wait_ge(s_out, 16 * TT)

                    @block.gpsimd
                    def _(pool):
                        for t in range(TT):
                            for n in range(2):
                                pool_e.indirect_dma_start(
                                    out=yt[2 * t + n], out_offset=None, in_=ybuf[:, :],
                                    in_offset=bass.IndirectOffsetOnAxis(ap=slots[:, n, t:t + 1], axis=0),
                                ).then_inc(s_yg[2 * t + n], 16)
                        for t in range(TT):
                            pool.wait_ge(s_c, t + 1)
                            pool_e.tensor_tensor(x[:, t, :], x[:, t, :], tmp[t % 2], ALU.add).then_inc(s_x, 1)

                    @block.tensor
                    def _(pe):
                        broadcast_on_pe(ps_gate, L, G_M).then_inc(s_bc, 1)
                        if final:
                            return
                        columns_on_pe(ps_cols, L + 1, (SH_A, SC_A)).then_inc(s_ct, 1)
                        for t in range(TT):
                            pe.wait_ge(s_xn, t + 1)
                            if t >= 2:
                                pe.wait_ge(s_ea, t - 1)
                                pe.wait_ge(s_ed, t - 1)
                            for k in range(KC):
                                last = pe_e.transpose(psT[t % 2][:, k, :], xn[t % 2][:, k * P:(k + 1) * P], ident)
                            last.then_inc(s_tr, 1)

                    @block.scalar
                    def _(act):
                        ch = Chain(act, s_ss)

                        def first(t):
                            act.wait_ge(s_yg[2 * t], 16)
                            if t >= 2:
                                act.wait_ge(s_x, t - 1)
                            act_e.activation(tmp[t % 2], yt[2 * t], ACT.Copy, scale=gates[:, 0, t:t + 1]).then_inc(s_a, 1)

                        def stats(t):
                            act.wait_ge(s_x, t + 1)
                            ch.link(act_e.activation(junk, x[:, t, :], ACT.Square, accum_out=ss[:, t:t + 1]))
                            act_e.activation(ss[:, t:t + 1], ss[:, t:t + 1], ACT.Sqrt, scale=1.0 / D, bias=eps).then_inc(s_rs, 1)

                        def scaled_out(t):
                            act.wait_ge(s_tr, t + 1)
                            act.wait_ge(s_cols, 1)
                            for k in range(KC // 2):
                                last = act_e.activation(hT[:, k, t * P:(t + 1) * P], psT[t % 2][:, k, :], ACT.Identity,
                                                        scale=modvec(L + 1, SC_A)[:, k:k + 1],
                                                        bias=modvec(L + 1, SH_A)[:, k:k + 1])
                            last.then_inc(s_ea, 1)

                        for t in range(TT + 2):
                            if t < TT:
                                first(t)
                            if 1 <= t <= TT:
                                stats(t - 1)
                            if t >= 2 and not final:
                                scaled_out(t - 2)

                    @block.vector
                    def _(dve):
                        dve.wait_ge(s_bc, 1)
                        vec.tensor_copy(gbc[:, :].rearrange("p (j n) -> p j n", j=4), ps_gate[:, :, :]).then_inc(s_gbc, 1)
                        if not final:
                            dve.wait_ge(s_ct, 1)
                            columns_out(Chain(dve, s_ch), ps_cols, L + 1, (SH_A, SC_A))
                            dve.sem_inc(s_cols, 1)
                        dve.wait_ge(s_gbc, 1)

                        def weighted(t):
                            dve.wait_ge(s_yg[2 * t + 1], 16)
                            dve.wait_ge(s_a, t + 1)
                            vec.scalar_tensor_tensor(tmp[t % 2], yt[2 * t + 1], gates[:, 1, t:t + 1], tmp[t % 2],
                                                     ALU.mult, ALU.add).then_inc(s_b, 1)
                            dve.wait_ge(s_b, t + 1)
                            vec.tensor_tensor(tmp[t % 2], tmp[t % 2], gbc[:, :], ALU.mult).then_inc(s_c, 1)

                        def normalised(t):
                            dve.wait_ge(s_rs, t + 1)
                            vec.reciprocal(rstd[:, t:t + 1], ss[:, t:t + 1]).then_inc(s_rec, 1)
                            dve.wait_ge(s_rec, t + 1)
                            if final:
                                if t == 0:
                                    dve.wait_ge(s_gf, 16)
                                vec.scalar_tensor_tensor(x[:, t, :], x[:, t, :], rstd[:, t:t + 1], gf, ALU.mult,
                                                         ALU.mult).then_inc(s_xn, 1)
                                return
                            if t >= 2:
                                dve.wait_ge(s_tr, t - 1)
                            vec.tensor_scalar(xn[t % 2], x[:, t, :], rstd[:, t:t + 1], None, ALU.mult).then_inc(s_xn, 1)

                        def scaled_out(t):
                            dve.wait_ge(s_tr, t + 1)
                            for k in range(KC // 2, KC):
                                last = vec.tensor_scalar(hT[:, k, t * P:(t + 1) * P], psT[t % 2][:, k, :],
                                                         modvec(L + 1, SC_A)[:, k:k + 1], modvec(L + 1, SH_A)[:, k:k + 1],
                                                         ALU.mult, ALU.add)
                            last.then_inc(s_ed, 1)

                        for t in range(TT + 2):
                            if t < TT:
                                weighted(t)
                            if 1 <= t <= TT:
                                normalised(t - 1)
                            if t >= 2 and not final:
                                scaled_out(t - 2)

        vectors_to_columns("v0", 0, [SH_A, SC_A])
        for L in range(DEPTH):
            n = f"l{L}"
            if L == 0:
                norm_transpose(n + "n1", L, SC_A, SH_A, lambda sp: load_first_w_in(sp, 0))
            attention(n + "at", L, L % 2 == 0)
            s_gu = [sem(f"{n}_wgu{i}") for i in range(3)]
            s_dn = [sem(f"{n}_wdn{i}") for i in range(2)]
            out_projection(n + "op", L, s_gu, s_dn)
            router(n + "ro")
            experts(n + "ex", L, s_gu, s_dn)
            combine(n + "co", L)
            clear_semaphores()


def constants():
    import numpy as np

    c = np.zeros((P, C_N), np.float32)
    r, n = np.arange(P)[:, None], np.arange(P)[None, :]
    c[:, C_ID:C_ID + P] = r == n
    c[:, C_ONE:C_ONE + P] = 1
    for j in range(4):
        c[32 * j, C_SEL + j * P:C_SEL + (j + 1) * P] = 1
    c[:, C_IOTA:C_IOTA + P] = n
    c[:, C_FOLD:C_FOLD + E] = r % E == np.arange(E)[None, :]
    c[:, C_MC:C_MC + P] = np.where(n > r, -BIG, 0)
    c[:, C_MS:C_MS + P] = np.where(n >= r, -BIG, 0)
    c[:, C_TRI:C_TRI + P] = r < n
    c[:, C_E:C_E + E] = P * np.arange(E)
    c[:, C_REV:C_REV + E] = E - np.arange(E)
    c[:, C_GRV:C_GRV + NG] = NG - np.arange(NG)
    half = 8
    f = np.arange(P) % H64
    c[:, C_EPS] = EPS
    c[:, C_INVF] = np.power(np.float32(500000.0), -(f % half).astype(np.float32) * np.float32(2.0 / (2 * half)))
    c[:, C_SGN] = np.where(f < half, -1, np.where(f < 2 * half, 1, 0))
    c[:, C_ROT] = f < 2 * half
    c[:, C_PASS] = f >= 2 * half
    for b in range(NB):
        c[:, C_OVE + b * E:C_OVE + (b + 1) * E] = np.arange(E)
        c[:, C_OVB + b * E:C_OVB + (b + 1) * E] = b + 1
        c[:, C_128B + b + 1] = P * (b + 1)
    c[:, C_OVJ:C_OVJ + NOV] = np.arange(NOV) + 1
    return c


_INS = ["x", "c", "positions", "w_ada", "b_ada", "norm_g", "w_in", "w_out", "diff_lambda", "diff_subln_g",
        "w_router", "b_router", "w_gate", "w_up", "w_down", "final_norm_g"]


def kernel(**inputs):
    import numpy as np
    import concourse.bacc as bacc
    from concourse.bass_utils import run_bass_kernel_spmd

    nc = bacc.Bacc("TRN2", target_bir_lowering=False, num_devices=1)
    arrays, args = {}, []
    for name in _INS:
        a = np.ascontiguousarray(inputs[name])
        arrays[f"in_{name}"] = a
        args.append(nc.dram_tensor(f"in_{name}", a.shape, mybir.dt.from_np(a.dtype), kind="ExternalInput").ap())
    arrays["in_consts"] = constants()
    args.append(nc.dram_tensor("in_consts", (P, C_N), F32, kind="ExternalInput").ap())
    args.append(nc.dram_tensor("out_0", (1, S, D), F32, kind="ExternalOutput").ap())
    build_trunk(nc, *args)
    r = run_bass_kernel_spmd(nc, [arrays], core_ids=[0])
    return r.results[0]["out_0"]
```
